# Optimizing a Trainium2 kernel written in Bass

```python
import jax
import jax.numpy as jnp
from jax import lax
import numpy as np

D_MODEL = 1024
BATCH = 1
SEQ = 256
DEPTH = 2

GRID_W = 64
CTX_LEN = 256
D_MIX = D_MODEL
HG_HEAD_DIM = 128
HG_WIDTH = D_MIX // 2
HG_HEADS = HG_WIDTH // HG_HEAD_DIM
HG_CHUNK = 64
MLA_WIDTH = D_MIX - HG_WIDTH
MLA_V = 64
MLA_HEADS = MLA_WIDTH // MLA_V
MLA_NOPE = 64
MLA_ROPE = 32
Q_LORA = 256
KV_LORA = 128
ROPE_BASE = 10000.0
Q_BLOCK = 128
N_EXPERTS = 64
TOP_K = 8
EXPERT_HIDDEN = 256
SHARED_HIDDEN = 256
ROUTED_SCALE = 2.5
DISPATCH_BLOCK = 128
N_MOD = 6
LN_EPS = 1e-6
RMS_EPS = 1e-6
DEEPNORM_ALPHA = (2 * DEPTH) ** 0.25
DEEPNORM_BETA = (8 * DEPTH) ** -0.25
N_IN = 5 * HG_WIDTH + Q_LORA + KV_LORA + MLA_ROPE

kernel_name = "hybrid_hgrn2_mla_moe_dit_block"

def _normalize(x):
    xf = x.astype(jnp.float32)
    mu = jnp.mean(xf, axis=-1, keepdims=True)
    var = jnp.mean(jnp.square(xf - mu), axis=-1, keepdims=True)
    return (xf - mu) * lax.rsqrt(var + LN_EPS)

def layer_norm(x, w, b):
    return (_normalize(x) * w.astype(jnp.float32) + b.astype(jnp.float32)).astype(x.dtype)

def modulate(x, shift, scale):
    y = _normalize(x) * (1.0 + scale.astype(jnp.float32)) + shift.astype(jnp.float32)
    return y.astype(x.dtype)

def rms_norm(x, w):
    xf = x.astype(jnp.float32)
    y = xf * lax.rsqrt(jnp.mean(jnp.square(xf), axis=-1, keepdims=True) + RMS_EPS)
    return (y * w.astype(jnp.float32)).astype(x.dtype)

def axial_rope(n_tok):
    pos = jnp.arange(n_tok, dtype=jnp.int32)
    row = (pos // GRID_W).astype(jnp.float32)
    col = (pos % GRID_W).astype(jnp.float32)
    n_freq = MLA_ROPE // 4
    inv = ROPE_BASE ** (-jnp.arange(n_freq, dtype=jnp.float32) / n_freq)
    ang = jnp.concatenate([row[:, None] * inv, col[:, None] * inv], axis=-1)
    return jnp.cos(ang), jnp.sin(ang)

def apply_rope(x, cos, sin):
    x1, x2 = jnp.split(x.astype(jnp.float32), 2, axis=-1)
    return jnp.concatenate([x1 * cos - x2 * sin, x2 * cos + x1 * sin], axis=-1).astype(x.dtype)

def seg_flip(a, n_ctx):
    return jnp.concatenate([jnp.flip(a[:, :n_ctx], axis=1), jnp.flip(a[:, n_ctx:], axis=1)], axis=1)

def gla_chunk_scan(q, k, v, log_f):
    bsz, n_tok, n_heads, dk = q.shape
    dv = v.shape[-1]
    n_chunks = n_tok // HG_CHUNK

    def chunks(a):
        return a.astype(jnp.float32).reshape(bsz, n_chunks, HG_CHUNK, n_heads, a.shape[-1]).transpose(1, 0, 3, 2, 4)

    lower = jnp.tril(jnp.ones((HG_CHUNK, HG_CHUNK), dtype=bool))[:, :, None]

    def step(state, inp):
        qc, kc, vc, gc = inp
        b = jnp.cumsum(gc, axis=-2)
        b_last = b[..., -1:, :]
        rel = jnp.where(lower, b[..., :, None, :] - b[..., None, :, :], -jnp.inf)
        scores = jnp.sum(qc[..., :, None, :] * kc[..., None, :, :] * jnp.exp(rel), axis=-1)
        o = scores @ vc + jnp.einsum('bhcd,bhdv->bhcv', qc * jnp.exp(b), state)
        state = state * jnp.swapaxes(jnp.exp(b_last), -1, -2) + jnp.einsum('bhcd,bhcv->bhdv', kc * jnp.exp(b_last - b), vc)
        return state, o

    s0 = jnp.zeros((bsz, n_heads, dk, dv), jnp.float32)
    _, o = lax.scan(step, s0, (chunks(q), chunks(k), chunks(v), chunks(log_f)))
    return o.transpose(1, 0, 3, 2, 4).reshape(bsz, n_tok, n_heads, dv)

def hgrn2_mixer(f_fw, f_bw, i_in, q_in, g_in, lb, norm_w, n_ctx):
    bsz, n_tok, _ = i_in.shape

    def heads(a):
        return a.reshape(bsz, n_tok, HG_HEADS, HG_HEAD_DIM)

    q = heads(jax.nn.silu(q_in) * HG_HEAD_DIM ** -0.5)
    v = heads(i_in)

    def forget(z, lb_dir):
        f = lb_dir + (1.0 - lb_dir) * jax.nn.sigmoid(z.astype(jnp.float32))
        return heads(1.0 - f), heads(jnp.log(f))

    k_fw, lf_fw = forget(f_fw, lb[:HG_WIDTH])
    k_bw, lf_bw = forget(f_bw, lb[HG_WIDTH:])
    o_fw = gla_chunk_scan(q, k_fw, v, lf_fw)
    o_bw = seg_flip(gla_chunk_scan(seg_flip(q, n_ctx), seg_flip(k_bw, n_ctx), seg_flip(v, n_ctx), seg_flip(lf_bw, n_ctx)), n_ctx)
    o = rms_norm(o_fw + o_bw, norm_w).reshape(bsz, n_tok, HG_WIDTH)
    return (o * jax.nn.silu(g_in.astype(jnp.float32))).astype(i_in.dtype)

def mla_mixer(cq, ckv, kpe, q_norm_w, w_uq, kv_norm_w, w_ukv, n_ctx, with_ctx):
    bsz, n_tok, _ = cq.shape
    n_lat = n_tok - n_ctx
    q = (rms_norm(cq, q_norm_w) @ w_uq).reshape(bsz, n_tok, MLA_HEADS, MLA_NOPE + MLA_ROPE)
    kv = (rms_norm(ckv, kv_norm_w) @ w_ukv).reshape(bsz, n_tok, MLA_HEADS, MLA_NOPE + MLA_V)
    q_nope, q_pe = q[..., :MLA_NOPE], q[..., MLA_NOPE:]
    k_nope, v = kv[..., :MLA_NOPE], kv[..., MLA_NOPE:]
    cos, sin = axial_rope(n_lat)
    qn_x, qp_x = q_nope[:, n_ctx:], q_pe[:, n_ctx:]
    qr_x = apply_rope(qp_x, cos[:, None, :], sin[:, None, :])
    kn_x, v_x = k_nope[:, n_ctx:], v[:, n_ctx:]
    kr_x = apply_rope(kpe[:, n_ctx:], cos, sin)
    kn_c, v_c, kp_c = k_nope[:, :n_ctx], v[:, :n_ctx], kpe[:, :n_ctx]
    scale = (MLA_NOPE + MLA_ROPE) ** -0.5
    n_blk = n_lat // Q_BLOCK

    def to_blocks(a):
        return jnp.moveaxis(a.reshape(bsz, n_blk, Q_BLOCK, *a.shape[2:]), 1, 0)

    def attend_block(blk):
        qn, qr, qp = blk
        s_lat = jnp.einsum('bqhd,bkhd->bhqk', qn, kn_x) + jnp.einsum('bqhd,bkd->bhqk', qr, kr_x)
        s_ctx = jnp.einsum('bqhd,bkhd->bhqk', qn, kn_c) + jnp.einsum('bqhd,bkd->bhqk', qp, kp_c)
        p = jax.nn.softmax(jnp.concatenate([s_lat, s_ctx], axis=-1).astype(jnp.float32) * scale, axis=-1).astype(v.dtype)
        return jnp.einsum('bhqk,bkhv->bqhv', p[..., :n_lat], v_x) + jnp.einsum('bhqk,bkhv->bqhv', p[..., n_lat:], v_c)

    o_x = lax.map(attend_block, (to_blocks(qn_x), to_blocks(qr_x), to_blocks(qp_x)))
    o_x = jnp.moveaxis(o_x, 0, 1).reshape(bsz, n_lat, MLA_WIDTH)
    if not with_ctx:
        return o_x, None
    s_c = jnp.einsum('bqhd,bkhd->bhqk', q_nope[:, :n_ctx], kn_c) + jnp.einsum('bqhd,bkd->bhqk', q_pe[:, :n_ctx], kp_c)
    p_c = jax.nn.softmax(s_c.astype(jnp.float32) * scale, axis=-1).astype(v.dtype)
    o_c = jnp.einsum('bhqk,bkhv->bqhv', p_c, v_c).reshape(bsz, n_ctx, MLA_WIDTH)
    return o_x, o_c

def token_mixer(hx, hc, w_in, lb, hg_norm_w, q_norm_w, w_uq, kv_norm_w, w_ukv, w_out, with_ctx):
    n_ctx = hc.shape[1]
    h = jnp.concatenate([hc, hx], axis=1)
    proj = h @ w_in
    sizes = (HG_WIDTH,) * 5 + (Q_LORA, KV_LORA, MLA_ROPE)
    f_fw, f_bw, i_in, q_in, g_in, cq, ckv, kpe = jnp.split(proj, np.cumsum(sizes)[:-1].tolist(), axis=-1)
    o_hg = hgrn2_mixer(f_fw, f_bw, i_in, q_in, g_in, lb, hg_norm_w, n_ctx)
    o_mla_x, o_mla_c = mla_mixer(cq, ckv, kpe, q_norm_w, w_uq, kv_norm_w, w_ukv, n_ctx, with_ctx)
    out_x = jnp.concatenate([o_hg[:, n_ctx:], o_mla_x], axis=-1) @ w_out
    if not with_ctx:
        return out_x, None
    out_c = jnp.concatenate([o_hg[:, :n_ctx], o_mla_c], axis=-1) @ w_out
    return out_x, out_c

def moe_ffn(h, router_w, router_bias, w1, w3, w2, sw1, sw3, sw2):
    n_tok, d = h.shape
    scores = jax.nn.sigmoid(jnp.dot(h, router_w).astype(jnp.float32))
    _, top_idx = lax.top_k(scores + router_bias.astype(jnp.float32), TOP_K)
    top_s = jnp.take_along_axis(scores, top_idx, axis=-1)
    top_w = ROUTED_SCALE * top_s / jnp.sum(top_s, axis=-1, keepdims=True)
    n_assign = n_tok * TOP_K
    e_flat = top_idx.reshape(n_assign)
    tok_flat = jnp.repeat(jnp.arange(n_tok, dtype=jnp.int32), TOP_K)
    order = jnp.argsort(e_flat)
    e_sorted = e_flat[order]
    counts = jnp.zeros((N_EXPERTS,), jnp.int32).at[e_flat].add(1)
    padded = (counts + DISPATCH_BLOCK - 1) // DISPATCH_BLOCK * DISPATCH_BLOCK
    pad_end = jnp.cumsum(padded)
    pad_start = pad_end - padded
    start = jnp.cumsum(counts) - counts
    dest = pad_start[e_sorted] + jnp.arange(n_assign, dtype=jnp.int32) - start[e_sorted]
    n_blocks = -(-(n_assign + N_EXPERTS * (DISPATCH_BLOCK - 1)) // DISPATCH_BLOCK)
    n_slots = n_blocks * DISPATCH_BLOCK
    slot_tok = jnp.zeros((n_slots,), jnp.int32).at[dest].set(tok_flat[order])
    slot_w = jnp.zeros((n_slots,), jnp.float32).at[dest].set(top_w.reshape(n_assign)[order])
    block_expert = jnp.minimum(jnp.searchsorted(pad_end, jnp.arange(n_blocks, dtype=jnp.int32) * DISPATCH_BLOCK, side='right'), N_EXPERTS - 1)

    def expert_block(acc, blk):
        idx, wts, e = blk
        xb = h[idx]
        hid = jax.nn.silu(xb @ w1[e]) * (xb @ w3[e])
        out = (hid @ w2[e]).astype(jnp.float32) * wts[:, None]
        return acc.at[idx].add(out), None

    routed, _ = lax.scan(expert_block, jnp.zeros((n_tok, d), jnp.float32),
                         (slot_tok.reshape(n_blocks, DISPATCH_BLOCK), slot_w.reshape(n_blocks, DISPATCH_BLOCK), block_expert))
    shared = (jax.nn.silu(h @ sw1) * (h @ sw3)) @ sw2
    return (routed + shared.astype(jnp.float32)).astype(h.dtype)

def setup_inputs(seed: int = 0) -> dict:
    key = jax.random.key(seed)
    ks = jax.random.split(key, 26)
    D = D_MODEL

    def nrm(k, shape, scale):
        return jax.random.normal(k, shape, jnp.float32) * scale

    return {
        "x": nrm(ks[0], (BATCH, SEQ, D), 1.0),
        "c": nrm(ks[1], (BATCH, D), 1.0),
        "ctx": nrm(ks[2], (BATCH, CTX_LEN, D), 1.0),
        "c_ctx": nrm(ks[3], (D,), 1.0),
        "w_mod": nrm(ks[4], (DEPTH, D, N_MOD * D), D ** -0.5),
        "b_mod": nrm(ks[5], (DEPTH, N_MOD * D), 0.02),
        "w_in": nrm(ks[6], (DEPTH, D, N_IN), D ** -0.5),
        "hg_lb": nrm(ks[7], (DEPTH, 2 * HG_WIDTH), 1.0),
        "hg_norm_w": 1.0 + nrm(ks[8], (DEPTH, HG_HEAD_DIM), 0.02),
        "q_norm_w": 1.0 + nrm(ks[9], (DEPTH, Q_LORA), 0.02),
        "w_uq": nrm(ks[10], (DEPTH, Q_LORA, MLA_HEADS * (MLA_NOPE + MLA_ROPE)), Q_LORA ** -0.5),
        "kv_norm_w": 1.0 + nrm(ks[11], (DEPTH, KV_LORA), 0.02),
        "w_ukv": nrm(ks[12], (DEPTH, KV_LORA, MLA_HEADS * (MLA_NOPE + MLA_V)), KV_LORA ** -0.5),
        "w_out": nrm(ks[13], (DEPTH, D_MIX, D), D_MIX ** -0.5 * DEEPNORM_BETA),
        "ln1_w": 1.0 + nrm(ks[14], (DEPTH, D), 0.02),
        "ln1_b": nrm(ks[15], (DEPTH, D), 0.02),
        "router_w": nrm(ks[16], (DEPTH, D, N_EXPERTS), D ** -0.5),
        "router_bias": nrm(ks[17], (DEPTH, N_EXPERTS), 0.01),
        "moe_w1": nrm(ks[18], (DEPTH, N_EXPERTS, D, EXPERT_HIDDEN), D ** -0.5),
        "moe_w3": nrm(ks[19], (DEPTH, N_EXPERTS, D, EXPERT_HIDDEN), D ** -0.5),
        "moe_w2": nrm(ks[20], (DEPTH, N_EXPERTS, EXPERT_HIDDEN, D), EXPERT_HIDDEN ** -0.5 * DEEPNORM_BETA),
        "shared_w1": nrm(ks[21], (DEPTH, D, SHARED_HIDDEN), D ** -0.5),
        "shared_w3": nrm(ks[22], (DEPTH, D, SHARED_HIDDEN), D ** -0.5),
        "shared_w2": nrm(ks[23], (DEPTH, SHARED_HIDDEN, D), SHARED_HIDDEN ** -0.5 * DEEPNORM_BETA),
        "ln2_w": 1.0 + nrm(ks[24], (DEPTH, D), 0.02),
        "ln2_b": nrm(ks[25], (DEPTH, D), 0.02),
    }

def reference(x, c, ctx, c_ctx, w_mod, b_mod, w_in, hg_lb, hg_norm_w, q_norm_w, w_uq, kv_norm_w, w_ukv,
              w_out, ln1_w, ln1_b, router_w, router_bias, moe_w1, moe_w3, moe_w2, shared_w1, shared_w3,
              shared_w2, ln2_w, ln2_b):
    bsz, n_lat, d = x.shape
    n_ctx = ctx.shape[1]
    lb_all = jnp.cumsum(jax.nn.softmax(hg_lb.astype(jnp.float32), axis=0), axis=0)
    lb_all = lb_all - lb_all[:1]
    cx = ctx
    for l in range(DEPTH):
        with_ctx = l < DEPTH - 1
        mod_x = jnp.dot(jax.nn.silu(c), w_mod[l]) + b_mod[l]
        mod_c = jnp.dot(jax.nn.silu(c_ctx), w_mod[l]) + b_mod[l]
        sh_a, sc_a, g_a, sh_f, sc_f, g_f = jnp.split(mod_x[:, None, :], N_MOD, axis=-1)
        csh_a, csc_a, cg_a, csh_f, csc_f, cg_f = jnp.split(mod_c, N_MOD, axis=-1)
        hx = modulate(x, sh_a, sc_a)
        hc = modulate(cx, csh_a, csc_a)
        mx, mc = token_mixer(hx, hc, w_in[l], lb_all[l], hg_norm_w[l], q_norm_w[l], w_uq[l], kv_norm_w[l],
                             w_ukv[l], w_out[l], with_ctx)
        x = layer_norm(DEEPNORM_ALPHA * x + g_a * mx, ln1_w[l], ln1_b[l])
        hx = modulate(x, sh_f, sc_f)
        if with_ctx:
            cx = layer_norm(DEEPNORM_ALPHA * cx + cg_a * mc, ln1_w[l], ln1_b[l])
            hc = modulate(cx, csh_f, csc_f)
            tokens = jnp.concatenate([hc.reshape(bsz * n_ctx, d), hx.reshape(bsz * n_lat, d)], axis=0)
        else:
            tokens = hx.reshape(bsz * n_lat, d)
        ff = moe_ffn(tokens, router_w[l], router_bias[l], moe_w1[l], moe_w3[l], moe_w2[l],
                     shared_w1[l], shared_w3[l], shared_w2[l])
        if with_ctx:
            fc = ff[:bsz * n_ctx].reshape(bsz, n_ctx, d)
            fx = ff[bsz * n_ctx:].reshape(bsz, n_lat, d)
            cx = layer_norm(DEEPNORM_ALPHA * cx + cg_f * fc, ln2_w[l], ln2_b[l])
        else:
            fx = ff.reshape(bsz, n_lat, d)
        x = layer_norm(DEEPNORM_ALPHA * x + g_f * fx, ln2_w[l], ln2_b[l])
    return x


_drawn_inputs = setup_inputs


def setup_inputs(seed=0):
    import zlib

    import numpy as np

    out = dict(_drawn_inputs(seed))
    spreads = {}
    factors = {'hg_lb': 3.217, 'hg_norm_w': 3.085, 'q_norm_w': 8.0, 'kv_norm_w': 4.84}
    for name, (base, spread) in spreads.items():
        noise = np.random.default_rng([zlib.crc32(name.encode()), seed]).standard_normal(out[name].shape)
        drawn = base * np.exp(spread * noise) if base else spread * noise
        out[name] = jnp.asarray(drawn.astype(out[name].dtype))
    for name, factor in factors.items():
        out[name] = (out[name] * factor).astype(out[name].dtype)
    return out
```

```python
from contextlib import ExitStack

import numpy as np

import concourse.bass as bass
from concourse import mybir

ALU = mybir.AluOpType
ACT = mybir.ActivationFunctionType
AX = mybir.AxisListType
F32 = mybir.dt.float32
BF16 = mybir.dt.bfloat16
I32 = mybir.dt.int32
U8 = mybir.dt.uint8

P = 128
D = 1024
KC = D // P
DEPTH = 2
TILES = 4
HEADS = 4
HD = 128
HGW = HEADS * HD
MLA_HEADS = 8
MV = 64
NOPE = 64
ROPE = 32
QK = NOPE + ROPE
QL = 256
KVL = 128
NE = 64
TOPK = 8
EH = 256
ROUTED_SCALE = 2.5
EPS = 1e-6
ALPHA = (2 * DEPTH) ** 0.25
GRID_W = 64
ROPE_BASE = 10000.0
UC = 256
RING = 4
NLEV = 8
CHUNKS_FW = [0, 1, 2, 3]
CHUNKS_BW = [1, 0, 3, 2]
NSLOT = 104
NB = 3
TURNS = (-(-NE // NB), 32)
BIG = 4096.0
MODU = 6 * D // UC

UNITS = ([(k, p) for p in range(2) for k in ("ffw", "fbw", "q", "i", "g")]
         + [("cq", 0), ("ckv", 0), ("uq", 0), ("ukv", 0)]
         + [("out", u) for u in range(4)] + [("sw1", 0), ("sw3", 0), ("sw2", 0)])


def unit_no(l, name, k=0):
    return DEPTH * MODU + l * len(UNITS) + UNITS.index((name, k))


def rstd_calls(l):
    tiles = range(TILES) if l < DEPTH - 1 else range(2, 4)
    return ([("a", 0)] + [("hg", 0), ("hg", 1), ("cq", 0), ("ckv", 0)]
            + [(k, t) for t in tiles for k in ("post1", "post2")] + [("fin", t) for t in tiles])


RSTD = [(l, *c) for l in range(DEPTH) for c in rstd_calls(l)]


def rstd_no(l, name, k=0):
    return RSTD.index((l, name, k)) + 1


def constants():
    s = np.arange(P)
    x = s[:, None] ^ s[None, :]
    masks = np.stack([x == 0] + [(x >= 1 << n) & (x < 2 << n) for n in range(6, -1, -1)], 1)
    pos = np.arange(256)
    n_freq = ROPE // 4
    inv = ROPE_BASE ** (-np.arange(n_freq, dtype=np.float32) / n_freq)
    ang = np.concatenate([(pos // GRID_W)[:, None] * inv, (pos % GRID_W)[:, None] * inv], -1).T.astype(np.float32)
    cs = np.stack([np.concatenate([np.cos(ang)] * 2), np.concatenate([np.sin(ang)] * 2)], 1)
    swap = np.zeros((ROPE, ROPE), np.float32)
    for i in range(ROPE // 2):
        swap[i + ROPE // 2, i] = -1.0
        swap[i, i + ROPE // 2] = 1.0
    ident = np.eye(P, dtype=np.float32)
    iota = np.broadcast_to(s.astype(np.float32), (P, P)).copy()
    scan = np.ones((P, 1024), np.float32)
    scan[:, ::P] = 0.0
    vals = np.zeros((P, TILES, 1, 12), np.float32)
    for t in range(TILES):
        vals[:, t, 0, 0] = s
        vals[:, t, 0, 1] = P * t
        vals[:, t, 0, 2] = -BIG
        vals[:, t, 0, 4] = TOPK * s
        vals[:, t, 0, 5] = TOPK * P * t
        vals[:, t, 0, 6] = -BIG * TOPK
    tab = np.zeros((P, NSLOT), np.float32)
    tab[:, :NE] = np.arange(NE)
    slot = np.broadcast_to(np.arange(NSLOT - NE, dtype=np.float32), (P, NSLOT - NE)).copy()
    big = np.broadcast_to(np.array([BIG, BIG * TOPK], np.float32), (P, 2)).copy()
    return dict(k_masks=masks.astype(np.float32).reshape(P, NLEV * P), k_cs=cs.astype(np.float32),
                k_swap=swap, k_ident=ident, k_iota=iota, k_scan=scan, k_vals=vals[:, :, 0],
                k_tri=(s[:, None] < s[None, :]).astype(np.float32), k_tab=tab, k_slot=slot, k_big=big)


def build(nc, A, out):
    with ExitStack() as ctx:
        ctx.enter_context(nc.allow_non_contiguous_dma(reason="small parameter columns"))

        def sb(name, shape, dt=F32):
            return ctx.enter_context(nc.sbuf_tensor(name, shape, dt))

        sems = {}

        def sem(name):
            if name not in sems:
                sems[name] = ctx.enter_context(nc.semaphore(name))
            return sems[name]

        mod_dram = nc.dram_tensor("mod_dram", (2, DEPTH * 6 * D), F32, kind="Internal").ap()
        h_dram = [nc.dram_tensor(f"h_dram{l}", (TILES * P, D), F32, kind="Internal").ap() for l in range(DEPTH)]
        y_dram = [nc.dram_tensor(f"y_dram{l}", (TILES * P * TOPK, D), F32, kind="Internal").ap() for l in range(DEPTH)]

        X = sb("X", [P, TILES, D])
        hT = sb("hT", [P, KC, TILES * P])
        ring = sb("ring", [P, RING, KC * UC])
        EW0 = sb("EW0", [P, 3 * KC * EH])
        UF = 26112
        U = sb("U", [P, UF])
        masks = sb("masks", [P, NLEV * P], U8)
        cs = sb("cs", [P, 2, 256])
        swap = sb("swap", [P, ROPE])
        ident = sb("ident", [P, P])
        iota = sb("iota", [P, P])
        trif = sb("trif", [P, P])
        tri = sb("tri", [P, P], BF16)
        ones = sb("ones", [P, P], BF16)
        slotno = sb("slotno", [P, NSLOT - NE])
        bigc = sb("bigc", [P, 2])
        half = sb("half", [P, 8])
        rin = sb("rin", [P, 8])
        rout = sb("rout", [P, 8])
        ccol = sb("ccol", [P, 2, KC])
        csil = sb("csil", [P, KC, 2])
        modcol = sb("modcol", [P, 2, 2, KC])
        lbc = sb("lbc", [P, DEPTH, 8])
        lbt = sb("lbt", [P, 3, 8])
        lb = sb("lb", [P, DEPTH, 8])
        oml = sb("oml", [P, DEPTH, 8])
        hgw = sb("hgw", [P, DEPTH, HD])
        qnw = sb("qnw", [P, DEPTH, 2])
        kvw = sb("kvw", [P, DEPTH])
        rbias = sb("rbias", [P, DEPTH, NE])
        rw = sb("rw", [P, DEPTH, KC, NE])
        stats = sb("stats", [P, TILES, 2, 6])
        mv = sb("mv", [P, TILES, 2])
        el = sb("el", [P, 2, 8])
        amax = sb("amax", [P, 2, 2])
        nmax = sb("nmax", [P, 2, 2])
        asum = sb("asum", [P, 2, 2])
        ainv = sb("ainv", [P, 2, 2])
        selb = sb("selb", [P, TILES, NE], BF16)
        posm = sb("posm", [P, TILES, NE])
        top8 = sb("top8", [P, TILES, 8])
        gsum = sb("gsum", [P, TILES, 2])
        csig = sb("csig", [P, 2, KC])
        ssq = sb("ssq", [P, 8])
        kv = sb("kv", [P, TILES, 12])
        exb = sb("exb", [P, NSLOT - NE])
        cnt = sb("cnt", [P, NE])
        over = sb("over", [P, NE])
        icum = sb("icum", [P, NE])
        onesf = sb("onesf", [P, NE])
        tabf = sb("tabf", [P, NSLOT])
        tabi = sb("tabi", [P, NSLOT + 4], I32)
        noff = sb("noff", [P, NSLOT])
        nturn = sb("nturn", [P, 2])
        idxf = sb("idxf", [P, NB, 3])
        idxi = sb("idxi", [P, NB, 2], I32)
        sidx = sb("sidx", [P, NB, 1], I32)

        def u(a, *shape):
            n = int(np.prod(shape))
            v = U[:, a:a + n]
            if len(shape) == 2:
                v = v.rearrange("p (a b) -> p a b", b=shape[1])
            if len(shape) == 3:
                v = v.rearrange("p (a b c) -> p a b c", b=shape[1], c=shape[2])
            return v

        modrow = U[0:2, 0:DEPTH * 6 * D]
        bmod = U[0:2, DEPTH * 6 * D:2 * DEPTH * 6 * D]
        maskf = U[:, 2 * DEPTH * 6 * D:2 * DEPTH * 6 * D + NLEV * P]
        mixT = u(0, KC, 512)
        a0 = 4096
        XH = u(a0 + 5120, 2, 1024)
        KR = u(a0 + 21504, 512)[NOPE:QK]
        KPR = u(a0 + 20992, 512)[NOPE:QK]
        kk = [u(a0, 1024), u(a0 + 1024, 1024)]
        bb = [u(a0 + 2048, 1024), u(a0 + 3072, 1024)]
        qq = u(a0 + 4096, 1024)
        EA = [u(a0 + 5120 + 2048 * n, 1024) for n in range(3)]
        EB = [u(a0 + 6144 + 2048 * n, 1024) for n in range(3)]
        QE = [u(a0 + 11264, 1024), u(a0 + 12288, 1024)]
        KDT = [u(a0 + 13312, 1024), u(a0 + 14336, 1024)]
        ST = u(a0 + 15360, 2, 512)
        SS = u(a0 + 16384, 12, 128)
        V = u(a0 + 17920, TILES, 256)
        G = u(a0 + 18944, TILES, 256)
        OT = u(a0 + 19968, TILES, 256)
        scanm = u(a0 + 20992, 1024)
        cqn = u(a0, TILES, QL)
        ckvn = u(a0 + 1024, TILES, KVL)
        cqT = u(a0 + 1536, 2, 512)
        ckvT = u(a0 + 2560, 512)
        qraw = u(a0 + 3072, MLA_HEADS, 512)
        qrot = u(a0 + 7168, MLA_HEADS, 256)
        qsw = u(a0 + 9216, MLA_HEADS * 256)
        kT = u(a0 + 11264, MLA_HEADS, 512)
        VM = u(a0 + 15360, TILES, 512)
        PR = u(a0 + 17408, 2, 2, 512)
        PTT = [u(a0 + 19456, 4, 256), u(a0 + 9216, 4, 256)]
        BV = u(a0, 8, 1024)
        H = u(a0 + 8192, 2, 1024)
        XG = u(a0 + 9216, NB, 1024)
        XT = u(a0 + 12288, 1024)
        GT = u(a0 + 12288, 2, UC)
        vals = U[:, a0 + 14336:a0 + 15872].bitcast(BF16).rearrange("p (t e k) -> p t e k", t=TILES, k=12)
        Y = [u(a0 + 4096, 1024), u(a0 + 5120, 1024), u(a0 + 13312, 1024)]
        HID = u(a0 + 6656, 2, 256)
        HIDT = u(a0 + 7168, 2, 256)
        HX = u(a0 + 6656, 256)
        HXT = u(a0 + 6912, 256)
        PH = U[:, a0 + 7168:a0 + 7936].bitcast(BF16).rearrange("p (b t j) -> p b t j", b=NB, j=P)
        SG = u(a0 + 8192, 256)
        FF = u(0, TILES, D)
        RB = [u(a0 + 8192, 4, 1024), u(UF - 6144, 4, 1024)]
        EW = [EW0[:, :], U[:, UF - 6144:UF], ring[:, 0:3, :].rearrange("p a b -> p (a b)")]
        W13 = [w[:, 0:4096].rearrange("p (m c n) -> p m c n", m=2, c=KC) for w in EW]
        W2 = [w[:, 4096:6144].rearrange("p (c n) -> p c n", c=2) for w in EW]
        cmpb = u(a0 + 4096, NSLOT - NE, NE)
        CW = u(a0 + 8448, TILES, NE)
        sco, bia, rep, sel, kth = (u(a0 + 12288 + 256 * n, TILES, NE) for n in range(5))

        bank = [ctx.enter_context(nc.psum_tensor(f"bank{n}", [P, 512], F32)) for n in range(8)]

        def bk(n, *shape):
            v = bank[n][:, :]
            if len(shape) == 2:
                return v[:, 0:shape[0] * shape[1]].rearrange("p (a b) -> p a b", b=shape[1])
            return v

        def seg_head(a, j):
            return a.rearrange("p (s j t) -> p s j t", s=2, j=2)[:, :, j, :]

        def tiles_of(l):
            return list(range(TILES)) if l < DEPTH - 1 else [2, 3]

        def segs_of(l):
            return [0, 1] if l < DEPTH - 1 else [1]

        def unit(n):
            return ring[:, n % RING, :]

        def unit_landed(eng, n):
            eng.wait_ge(sem(f"ring_landed{n % RING}"), 16 * (n // RING + 1))

        def nparts(l, name):
            nt, ns = len(tiles_of(l)), len(segs_of(l))
            return dict(ffw=2, fbw=2, q=2, i=2, g=ns, cq=ns, ckv=2, uq=MLA_HEADS, ukv=MLA_HEADS + TILES,
                        out=nt, sw1=1, sw3=nt, sw2=nt)[name]

        def part_base(l, name, k):
            done = 0
            for ll in range(DEPTH):
                for nm, kk_ in UNITS:
                    if (ll, nm, kk_) == (l, name, k):
                        return done
                    done += nparts(ll, nm) - 1

        def part_done(ins, l, name, k, n):
            ins.then_inc(sem("unit_done" if n == nparts(l, name) - 1 else "part_done"), 1)

        def wait_part(eng, l, name, k, n):
            if n == nparts(l, name) - 1:
                eng.wait_ge(sem("unit_done"), unit_no(l, name, k) + 1)
            elif name == "out":
                eng.wait_ge(sem("part_done"), part_base(l, name, 0) + 4 * n + k + 1)
            else:
                eng.wait_ge(sem("part_done"), part_base(l, name, k) + n + 1)

        items = [[(h, x) for h in range(MLA_HEADS) for x in ((1, 0) if l < DEPTH - 1 else (1,))] for l in range(DEPTH)]
        item0 = [0, len(items[0])]

        small = [(maskf, A["k_masks"]), (cs[NOPE:QK, :, :], A["k_cs"]), (swap[NOPE:QK, :], A["k_swap"]),
                 (iota[:, :], A["k_iota"]), (trif[:, :], A["k_tri"]), (slotno[:, :], A["k_slot"]), (bigc[:, :], A["k_big"]),
                 (tabf[:, :], A["k_tab"]), (kv[:, :, :], A["k_vals"])]
        for l_ in range(DEPTH):
            small += [(lbc[:, l_, :], A["hg_lb"][l_].rearrange("(n p) -> p n", p=P)),
                      (hgw[:, l_, :], A["hg_norm_w"][l_].partition_broadcast(P)),
                      (qnw[:, l_, :], A["q_norm_w"][l_].rearrange("(n p) -> p n", p=P)),
                      (kvw[:, l_:l_ + 1], A["kv_norm_w"][l_].rearrange("(p n) -> p n", n=1)),
                      (rbias[:, l_, :], A["router_bias"][l_].partition_broadcast(P)),
                      (rw[:, l_, :, :], A["router_w"][l_].rearrange("(p c) n -> p c n", c=KC))]

        def expert_src(w, e):
            return w[e].rearrange("(p c) n -> p (c n)", p=P)

        block = ctx.enter_context(nc.Block())

        @block.sync
        def _(sp):
            sp.dma_start(ident[:, :], A["k_ident"]).then_inc(sem("ident_landed"), 16)
            sp.dma_start(ccol[:, 0, :], A["c"][0].rearrange("(p c) -> p c", p=P)).then_inc(sem("c_landed"), 16)
            sp.dma_start(ccol[:, 1, :], A["c_ctx"].rearrange("(p c) -> p c", p=P)).then_inc(sem("c_landed"), 16)

            def load_unit(n, dst, src):
                if n >= RING:
                    sp.wait_ge(sem("unit_done"), n - RING + 1)
                sp.dma_start(dst, src).then_inc(sem(f"ring_landed{n % RING}"), 16)

            def cols(n, w, a, m, pat="(p c) n -> p c n"):
                load_unit(n, unit(n)[:, 0:KC * m].rearrange("p (c n) -> p c n", n=m),
                          w[:, a:a + m].rearrange(pat, p=P, c=KC))

            for l in range(DEPTH):
                for v in range(MODU):
                    cols(l * MODU + v, A["w_mod"][l], v * UC, UC)
                    if l == 0 and v == 3:
                        for t in range(TILES):
                            src = A["ctx"][0] if t < 2 else A["x"][0]
                            sp.dma_start(X[:, t, :], src[(t % 2) * P:(t % 2 + 1) * P, :]).then_inc(sem("x_landed"), 16)
                        for dst, src in small:
                            sp.dma_start(dst, src).then_inc(sem("small_landed"), 16)
            for l in range(DEPTH):
                w_in = A["w_in"][l]
                start = dict(ffw=0, fbw=HGW, i=2 * HGW, q=3 * HGW, g=4 * HGW)
                for name, k in UNITS:
                    n = unit_no(l, name, k)
                    if name in start:
                        cols(n, w_in, start[name] + k * UC, UC)
                    elif name == "cq":
                        cols(n, w_in, 5 * HGW, QL)
                    elif name == "ckv":
                        cols(n, w_in, 5 * HGW + QL, KVL + ROPE)
                    elif name == "uq":
                        load_unit(n, unit(n)[:, 0:2 * MLA_HEADS * QK].rearrange("p (c n) -> p c n", c=2),
                                  A["w_uq"][l].rearrange("(c p) n -> p c n", p=P))
                    elif name == "ukv":
                        load_unit(n, unit(n)[:, 0:MLA_HEADS * P], A["w_ukv"][l])
                    elif name == "out":
                        cols(n, A["w_out"][l], k * UC, UC, "(c p) n -> p c n")
                    elif name in ("sw1", "sw3"):
                        cols(n, A["shared_w1" if name == "sw1" else "shared_w3"][l], 0, UC)
                    else:
                        load_unit(n, unit(n).rearrange("p (c n) -> p c n", c=2),
                                  A["shared_w2"][l].rearrange("(p c) n -> p c n", c=2))
                w1, w3, w2 = A["moe_w1"][l], A["moe_w3"][l], A["moe_w2"][l]

                def load_expert(b, e):
                    sp.dma_start(EW[b][:, 0:2048], expert_src(w1, e)).then_inc(sem(f"w13_landed{b}_{l}"), 16)
                    sp.dma_start(EW[b][:, 2048:4096], expert_src(w3, e)).then_inc(sem(f"w13_landed{b}_{l}"), 16)

                def load_down(b, e):
                    sp.dma_start(EW[b][:, 4096:6144], expert_src(w2, e)).then_inc(sem(f"w2_landed{b}_{l}"), 16)

                load_expert(0, 0)
                load_down(0, 0)
                sp.wait_ge(sem("attn_out"), item0[l] + len(items[l]))
                load_expert(1, 1)
                load_down(1, 1)
                sp.wait_ge(sem("unit_done"), unit_no(l, *UNITS[-1]) + 1)
                load_expert(2, 2)
                load_down(2, 2)
                for e in range(NB, 2 * NB):
                    sp.wait_ge(sem(f"up_done{l}"), e - NB + 1)
                    load_expert(e % NB, e)
                    sp.wait_ge(sem(f"down_done{l}"), e - NB + 1)
                    load_down(e % NB, e)
                sp.wait_ge(sem("table_ready"), l + 1)
                final = sp.value_load(tabi[0:1, NSLOT:NSLOT + 1], min_val=TURNS[0] - 1, max_val=TURNS[1] - 1)
                with sp.Fori(2, final + 1) as turn_no:
                    for b in range(NB):
                        e = sp.value_load(tabi[0:1, bass.ds(NB * turn_no + b, 1)], min_val=0, max_val=NE - 1)
                        sp.wait_ge(sem(f"up_done{l}"), NB * turn_no + (b - NB + 1))
                        sp.dma_start(EW[b][:, 0:2048], w1[bass.ds(e, 1)].rearrange("e (p c) n -> p (e c n)", p=P)).then_inc(sem(f"w13_landed{b}_{l}"), 16)
                        sp.dma_start(EW[b][:, 2048:4096], w3[bass.ds(e, 1)].rearrange("e (p c) n -> p (e c n)", p=P)).then_inc(sem(f"w13_landed{b}_{l}"), 16)
                        sp.wait_ge(sem(f"down_done{l}"), NB * turn_no + (b - NB + 1))
                        sp.dma_start(EW[b][:, 4096:6144], w2[bass.ds(e, 1)].rearrange("e (p c) n -> p (e c n)", p=P)).then_inc(sem(f"w2_landed{b}_{l}"), 16)
                sp.wait_ge(sem(f"down_done{l}"), NB * final + NB)

            for x in range(2):
                sp.wait_ge(sem("x_final"), TILES * (DEPTH - 1) + x + 1)
                sp.dma_start(out[0, x * P:(x + 1) * P, :], X[:, 2 + x, :]).then_inc(sem("out_stored"), 16)
            sp.wait_ge(sem("out_stored"), 32)

        @block.gpsimd
        def _(gp):
            gp.memset(half[:, :], -0.5).then_inc(sem("pool_set"), 1)
            gp.memset(rin[:, :], 1.0).then_inc(sem("pool_set"), 1)
            gp.memset(ones[:, :], 1.0).then_inc(sem("pool_set"), 1)
            gp.memset(onesf[:, :], 1.0).then_inc(sem("pool_set"), 1)
            gp.wait_ge(sem("pool_set"), 2)
            gp.dma_start(bmod.rearrange("p (l n) -> p l n", l=DEPTH),
                         A["b_mod"].rearrange("l n -> (l n)").partition_broadcast(2).rearrange("p (l n) -> p l n", l=DEPTH)
                         ).then_inc(sem("bmod_landed"), 16)
            gp.wait_ge(sem("mod_added"), DEPTH * MODU)
            gp.dma_start(mod_dram, modrow).then_inc(sem("mod_stored"), 16)
            gp.wait_ge(sem("mod_stored"), 16)

            def rstd(l, name, k=0):
                n = rstd_no(l, name, k)
                gp.wait_ge(sem("var_ready"), n)
                gp.tensor_tensor(rout[:, :], rin[:, :], half[:, :], ALU.pow).then_inc(sem("rstd_ready"), 1)

            def mod_row(l, part, s):
                return mod_dram[s:s + 1, (l * 6 + part) * D:(l * 6 + part + 1) * D]

            for l in range(DEPTH):
                tiles = tiles_of(l)
                streams = [0, 1] if l < DEPTH - 1 else [0]
                if l:
                    gp.wait_ge(sem("h_ready"), TILES * l)
                gp.dma_start(scanm, A["k_scan"]).then_inc(sem("scan_landed"), 16) if l == 0 else None
                for s in range(2):
                    for part in range(2):
                        gp.dma_start(modcol[:, s, part, :],
                                     mod_row(l, part, s).rearrange("a (p c) -> (a p) c", c=KC)
                                     ).then_inc(sem("modcol_landed"), 16)
                if l:
                    gp.wait_ge(sem("x_final"), TILES * l)
                    gp.dma_start(scanm, A["k_scan"]).then_inc(sem("scan_landed"), 16)
                rstd(l, "a")
                rstd(l, "hg", 0)
                rstd(l, "hg", 1)
                rstd(l, "cq")
                rstd(l, "ckv")
                gp.wait_ge(sem("attn_out"), item0[l] + len(items[l]))
                for row, src in [(2, A["ln1_w"][l:l + 1]), (3, A["ln1_b"][l:l + 1])]:
                    gp.dma_start(BV[:, row, :], src.rearrange("a n -> (a n)").partition_broadcast(P)).then_inc(sem("rows1_landed"), 16)
                for s in streams:
                    for row, part in [(0 + s, 2), (4 + s, 3), (6 + s, 4)]:
                        gp.dma_start(BV[:, row, :], mod_row(l, part, s).rearrange("a n -> (a n)").partition_broadcast(P)).then_inc(sem("rows1_landed"), 16)
                for n, t in enumerate(tiles):
                    rstd(l, "post1", t)
                    rstd(l, "post2", t)
                    gp.wait_ge(sem("h_ready"), TILES * l + n + 1)
                    gp.dma_start(h_dram[l][n * P:(n + 1) * P, :], H[:, n % 2, :]).then_inc(sem(f"h_stored{n % 2}"), 16)
                gp.wait_ge(sem("h_stored0"), 32 * l + 16 * (len(tiles) // 2))
                gp.wait_ge(sem("h_stored1"), 32 * l + 16 * (len(tiles) // 2))
                for row, src in [(2, A["ln2_w"][l:l + 1]), (3, A["ln2_b"][l:l + 1])]:
                    gp.dma_start(BV[:, row, :], src.rearrange("a n -> (a n)").partition_broadcast(P)).then_inc(sem("rows2_landed"), 16)
                for s in streams:
                    gp.dma_start(BV[:, s, :], mod_row(l, 5, s).rearrange("a n -> (a n)").partition_broadcast(P)).then_inc(sem("rows2_landed"), 16)
                rows = P * len(tiles)

                def take_waits():
                    gp.sem_inc(sem("pool_turn"), 1)

                def gather(i, b):
                    gp.wait_ge(sem(f"idx_ready{l}"), i + 1)
                    if not isinstance(i, int) or i >= NB:
                        gp.wait_ge(sem(f"xg_turned{l}"), i - (NB - 1))
                    take_waits()
                    gp.indirect_dma_start(out=XG[:, b, :], out_offset=None, in_=h_dram[l][0:rows, :],
                                          in_offset=bass.IndirectOffsetOnAxis(ap=idxi[:, b, 0:1], axis=0),
                                          bounds_check=rows - 1, oob_is_err=False,
                                          compute_op=ALU.bypass).then_inc(sem(f"xg_landed{b}_{l}"), 16)

                def scatter(i, b):
                    gp.wait_ge(sem(f"y_ready{l}"), 2 * i + 2)
                    take_waits()
                    gp.indirect_dma_start(out=y_dram[l][0:rows * TOPK, :],
                                          out_offset=bass.IndirectOffsetOnAxis(ap=sidx[:, b, 0:1], axis=0),
                                          in_=Y[b], in_offset=None,
                                          bounds_check=rows * TOPK - 1, oob_is_err=False,
                                          compute_op=ALU.bypass).then_inc(sem(f"y_stored{b}_{l}"), 16)

                gp.wait_ge(sem("h_turned"), TILES * l + len(tiles))
                gp.memset(XG[:, :, :], 0.0).then_inc(sem("pool_set"), 1)
                gp.wait_ge(sem("pool_set"), l + 5)
                gp.wait_ge(sem("table_ready"), l + 1)
                final = gp.value_load(tabi[0:1, NSLOT:NSLOT + 1], min_val=TURNS[0] - 1, max_val=TURNS[1] - 1)
                for i in range(NB):
                    gather(i, i)
                for i in range(2 * NB):
                    gather(i + NB, i % NB)
                    if i:
                        scatter(i - 1, (i - 1) % NB)
                with gp.Fori(2, final + 1) as turn_no:
                    for b in range(NB):
                        i = NB * turn_no + b
                        gather(i + NB, b)
                        scatter(i - 1, (b - 1) % NB)
                scatter(NB * final + (NB - 1), NB - 1)
                for b in range(NB):
                    gp.wait_ge(sem(f"y_stored{b}_{l}"), 16 * (final + 1))
                for b in range(NB):
                    gp.wait_ge(sem(f"xg_landed{b}_{l}"), 16 * (final + 2))
                gp.wait_ge(sem(f"xg_turned{l}"), NB * final + (NB + 1))
                take_waits()
                for n, t in enumerate(tiles):
                    for k in range(2):
                        if n:
                            gp.wait_ge(sem("rb_summed"), 2 * TILES * l + 2 * (n - 1) + k + 1)
                            if k:
                                gp.wait_ge(sem("rb_read"), 2 * TILES * l + 2 * n - 1)
                        gp.dma_start(RB[k].rearrange("p k d -> p (k d)"),
                                     y_dram[l][n * P * TOPK:(n + 1) * P * TOPK, :].rearrange("(p k) d -> p k d", k=TOPK)[:, 4 * k:4 * k + 4, :].rearrange("p k d -> p (k d)")
                                     ).then_inc(sem(f"rb_landed{k}"), 16)
                    if n:
                        rstd(l, "fin", tiles[n - 1])
                rstd(l, "fin", tiles[-1])

        @block.tensor
        def _(pe):
            def mm(o, lhsT, rhs, start=True, stop=True):
                return nc.tensor.matmul(o, lhsT, rhs, start=start, stop=stop)

            pe.wait_ge(sem("dve_start"), 1)
            for n in range(DEPTH * MODU):
                unit_landed(pe, n)
                if n >= 4:
                    pe.wait_ge(sem("mod_added"), n - 3)
                for c in range(KC):
                    last = mm(bank[n % 4][0:2, 0:UC], csil[:, c, :], unit(n)[:, c * UC:(c + 1) * UC], c == 0, c == KC - 1)
                last.then_inc(sem("unit_done"), 1)
            pe.wait_ge(sem("mod_added"), DEPTH * MODU)
            pe.wait_ge(sem("small_landed"), 16 * len(small))
            pe.wait_ge(sem("ident_landed"), 16)

            def turn(src, b0):
                for c in range(KC):
                    last = nc.tensor.transpose(bank[b0 + c // 4][:, (c % 4) * P:(c % 4 + 1) * P], src[:, c::KC], ident[:, :])
                return last

            for l in range(DEPTH):
                tiles, segs = tiles_of(l), segs_of(l)
                nt = len(tiles)
                x0 = tiles[0] * P

                for t in range(TILES):
                    pe.wait_ge(sem("xh_ready"), TILES * l + t + 1)
                    if t >= 2:
                        pe.wait_ge(sem("ht_low"), TILES * l + t - 1)
                        pe.wait_ge(sem("ht_high"), TILES * l + t - 1)
                    turn(XH[:, t % 2, :], 2 * (t % 2)).then_inc(sem("xh_turned"), 1)
                pe.wait_ge(sem("ht_low"), TILES * l + TILES)
                pe.wait_ge(sem("ht_high"), TILES * l + TILES)

                def feature_major(name, k, b0, t0):
                    n = unit_no(l, name, k)
                    unit_landed(pe, n)
                    for j in range(2):
                        for c in range(KC):
                            last = mm(bank[b0 + j][:, t0:512], unit(n)[:, c * UC + j * P:c * UC + (j + 1) * P],
                                      hT[:, c, t0:512], c == 0, c == KC - 1)
                        part_done(last, l, name, k, j)

                def token_major(name, k, b0, ts, part=0, w=UC, m=UC, each=2):
                    n = unit_no(l, name, k)
                    unit_landed(pe, n)
                    for x, t in enumerate(ts):
                        for c in range(KC):
                            last = mm(bank[b0 + t // each][:, (t % each) * m:(t % each + 1) * m],
                                      hT[:, c, t * P:(t + 1) * P], unit(n)[:, c * w:c * w + m], c == 0, c == KC - 1)
                        if t % each == each - 1:
                            part_done(last, l, name, k, part)
                            part += 1

                for p in range(2):
                    cp = 2 * l + p
                    if cp % 2:
                        pe.wait_ge(sem("ot_ready"), cp)
                        pe.wait_ge(sem("mix_ready"), cp)
                    feature_major("ffw", p, 0, 0)
                    feature_major("fbw", p, 2, 0)
                    if cp:
                        pe.wait_ge(sem("lvl_used"), NLEV * cp)
                        pe.wait_ge(sem("attn_out"), item0[l])
                    feature_major("q", p, 4, x0)
                    token_major("i", p, 6, range(TILES))
                    pe.wait_ge(sem("f_sig"), 4 * cp + 2)
                    token_major("g", p, 0, tiles)
                    pe.wait_ge(sem("v_ready"), 2 * cp + 2)
                    for d in range(2):
                        b0 = 6 if d == 0 else 0
                        pe.wait_ge(sem("kd_ready"), 2 * cp + d + 1)
                        if d:
                            pe.wait_ge(sem("g_used"), cp + 1)
                        for blk in range(8):
                            last = nc.tensor.transpose(bank[b0 + blk // 4][:, (blk % 4) * P:(blk % 4 + 1) * P],
                                                       EA[0][:, blk * P:(blk + 1) * P] if d == 0 else EB[0][:, blk * P:(blk + 1) * P],
                                                       ident[:, :])
                        last.then_inc(sem("kd_turned"), 1)
                    pe.wait_ge(sem("kdt_ready"), 4 * cp + 4)
                    for k in range(3):
                        if k == 2:
                            pe.wait_ge(sem("state_ready"), 3 * cp + 1)
                        for d, order in enumerate((CHUNKS_FW, CHUNKS_BW)):
                            for j in range(2):
                                ch = order[k]
                                blk = (ch // 2) * 4 + j * 2 + ch % 2
                                last = mm(bank[6 + k % 2][:, (2 * d + j) * P:(2 * d + j + 1) * P],
                                          KDT[d][:, blk * P:(blk + 1) * P], V[:, ch, j * P:(j + 1) * P])
                        last.then_inc(sem("state_sum"), 1)
                    pe.wait_ge(sem("f_sig"), 4 * cp + 4)
                    pe.wait_ge(sem("q_ready"), cp + 1)
                    for n in range(NLEV):
                        pe.wait_ge(sem("lvl_ready"), NLEV * cp + n + 1)
                        if n >= 2:
                            pe.wait_ge(sem("lvl_used"), NLEV * cp + n - 1)
                        for s in segs:
                            for j in range(2):
                                for c in range(2):
                                    blk = s * 4 + j * 2 + c
                                    last = mm(bank[2 + 2 * (n % 2) + s][:, (j * 2 + c) * P:(j * 2 + c + 1) * P],
                                              EB[n % 3][:, blk * P:(blk + 1) * P],
                                              (EA[n % 3] if n else qq)[:, blk * P:(blk + 1) * P])
                        last.then_inc(sem("lvl_done"), 1)
                    pe.wait_ge(sem("lvl_used"), NLEV * (cp + 1))
                    pe.wait_ge(sem("state_ready"), 3 * cp + 3)
                    pe.wait_ge(sem("qe_ready"), cp + 1)
                    for s in segs:
                        for c in range(2):
                            for j in range(2):
                                ch = 2 * s + c
                                blk = s * 4 + j * 2 + c
                                o = bank[s][:, (c * 2 + j) * P:(c * 2 + j + 1) * P]
                                parts = [(ST[:, s, (j * 2 + c) * P:(j * 2 + c + 1) * P], V[:, ch, j * P:(j + 1) * P])]
                                for d, order in enumerate((CHUNKS_FW, CHUNKS_BW)):
                                    at = order.index(ch)
                                    if at:
                                        parts.append((QE[d][:, blk * P:(blk + 1) * P], SS[:, (d * 2 + j) * 3 + at - 1, :]))
                                for a, (x, y) in enumerate(parts):
                                    last = mm(o, x, y, a == 0, a == len(parts) - 1)
                    last.then_inc(sem("o_done"), 1)
                    pe.wait_ge(sem("ot_ready"), cp + 1)
                    for j in range(2):
                        for t in tiles:
                            last = nc.tensor.transpose(bank[2 + j][:, t * P:(t + 1) * P], OT[:, t, j * P:(j + 1) * P], ident[:, :])
                    last.then_inc(sem("ot_turned"), 1)

                pe.wait_ge(sem("ot_ready"), 2 * l + 2)
                token_major("cq", 0, 0, tiles)
                n = unit_no(l, "ckv")
                unit_landed(pe, n)
                w = KVL + ROPE
                for t in range(TILES):
                    for c in range(KC):
                        last = mm(bank[4][:, t * KVL:(t + 1) * KVL], hT[:, c, t * P:(t + 1) * P],
                                  unit(n)[:, c * w:c * w + KVL], c == 0, c == KC - 1)
                part_done(last, l, "ckv", 0, 0)
                for c in range(KC):
                    last = mm(bank[5][NOPE:QK, :], unit(n)[:, c * w + KVL:(c + 1) * w], hT[:, c, :], c == 0, c == KC - 1)
                part_done(last, l, "ckv", 0, 1)
                pe.wait_ge(sem("mix_ready"), 2 * l + 2)
                pe.wait_ge(sem("cqn_ready"), l + 1)
                for c in range(2):
                    for t in tiles:
                        last = nc.tensor.transpose(bank[2 + c][:, t * P:(t + 1) * P], cqn[:, t, c * P:(c + 1) * P], ident[:, :])
                last.then_inc(sem("cq_turned"), 1)
                pe.wait_ge(sem("ckvn_ready"), l + 1)
                for t in range(TILES):
                    last = nc.tensor.transpose(bank[6][:, t * P:(t + 1) * P], ckvn[:, t, :], ident[:, :])
                last.then_inc(sem("ckv_turned"), 1)
                pe.wait_ge(sem("cqt_ready"), 2 * l + 2)
                pe.wait_ge(sem("ckvt_ready"), l + 1)
                n = unit_no(l, "uq")
                unit_landed(pe, n)
                for h in range(MLA_HEADS):
                    if h >= 2:
                        pe.wait_ge(sem("qraw_ready"), MLA_HEADS * l + h - 1)
                    for c in range(2):
                        last = mm(bank[h % 2][0:QK, x0:512], unit(n)[:, c * MLA_HEADS * QK + h * QK:c * MLA_HEADS * QK + (h + 1) * QK],
                                  cqT[:, c, x0:512], c == 0, c == 1)
                    part_done(last, l, "uq", 0, h)
                n = unit_no(l, "ukv")
                unit_landed(pe, n)
                pe.wait_ge(sem("kpr_ready"), l + 1)
                for h in range(MLA_HEADS):
                    if h >= 2:
                        pe.wait_ge(sem("kt_ready"), MLA_HEADS * l + h - 1)
                    last = mm(bank[4 + h % 2][0:NOPE, :], unit(n)[:, h * P:h * P + NOPE], ckvT)
                    part_done(last, l, "ukv", 0, h)
                wv = unit(n)[:, 0:MLA_HEADS * P].rearrange("p (h x) -> p h x", x=P)[:, :, NOPE:P]
                for t in range(TILES):
                    if t >= 2:
                        pe.wait_ge(sem("vm_ready"), TILES * l + t - 1)
                    last = mm(bank[6 + t % 2][:, :], ckvT[:, t * P:(t + 1) * P], wv)
                    part_done(last, l, "ukv", 0, MLA_HEADS + t)
                pe.wait_ge(sem("qraw_ready"), MLA_HEADS * (l + 1))
                for n in range(5):
                    if n >= 2:
                        pe.wait_ge(sem("swap_used"), 5 * l + n - 1)
                    if n < 4:
                        src, o = qraw[NOPE:QK, 2 * n:2 * n + 2, 256:512], bank[2 + n % 2][NOPE:QK, :].rearrange("p (h t) -> p h t", h=2)
                    else:
                        src, o = KPR[:, 256:512], bank[2][NOPE:QK, 0:256]
                    mm(o, swap[NOPE:QK, :], src).then_inc(sem("swap_done"), 1)
                its = items[l]

                def scores(m):
                    h, x = its[m]
                    g = item0[l] + m
                    if m >= 2:
                        pe.wait_ge(sem("probs_ready"), g - 1)
                    for qt in range(2):
                        o = bank[2 * (m % 2) + qt]
                        if x:
                            mm(o[:, 0:256], qrot[0:QK, h, qt * P:(qt + 1) * P], kT[0:QK, h, 256:512])
                            last = mm(o[:, 256:512], qraw[0:QK, h, 256 + qt * P:256 + (qt + 1) * P], kT[0:QK, h, 0:256])
                        else:
                            last = mm(o[:, 0:256], qraw[0:QK, h, qt * P:(qt + 1) * P], kT[0:QK, h, 0:256])
                    last.then_inc(sem("scores_done"), 1)

                pe.wait_ge(sem("swap_used"), 5 * (l + 1))
                pe.wait_ge(sem("keys_ready"), l + 1)
                pe.wait_ge(sem("kt_ready"), MLA_HEADS * (l + 1))
                pe.wait_ge(sem("vm_ready"), TILES * (l + 1))
                scores(0)
                for m, (h, x) in enumerate(its):
                    g = item0[l] + m
                    if m + 1 < len(its):
                        scores(m + 1)
                    nk = 4 if x else 2
                    pe.wait_ge(sem("probs_ready"), g + 1)
                    if m:
                        pe.wait_ge(sem("pt_ready"), g)
                    for kt in range(nk):
                        for qt in range(2):
                            last = nc.tensor.transpose(bank[4 + kt // 2][:, (kt % 2) * 256 + qt * P:(kt % 2) * 256 + (qt + 1) * P],
                                                       PR[:, m % 2, qt, kt * P:(kt + 1) * P], ident[:, :])
                    last.then_inc(sem("probs_turned"), 1)
                    pe.wait_ge(sem("pt_ready"), g + 1)
                    if m >= 2:
                        pe.wait_ge(sem("attn_out"), g - 1)
                    o = bank[6 + m % 2][(h % 2) * MV:(h % 2 + 1) * MV, 0:256]
                    for kt in range(nk):
                        tile = (kt + 2) % 4 if x else kt
                        last = mm(o, VM[:, tile, h * MV:(h + 1) * MV], PTT[m % 2][:, kt, :], kt == 0, kt == nk - 1)
                    last.then_inc(sem("pv_done"), 1)

                pe.wait_ge(sem("attn_out"), item0[l] + len(its))
                def project(x):
                    t = tiles[x]
                    for k in range(4):
                        n = unit_no(l, "out", k)
                        unit_landed(pe, n)
                        q = x * 4 + k
                        if q >= 4:
                            pe.wait_ge(sem("mix_added"), 4 * TILES * l + q - 3)
                        for c in range(KC):
                            last = mm(bank[4 + k][:, 0:UC], mixT[:, c, t * P:(t + 1) * P], unit(n)[:, c * UC:(c + 1) * UC], c == 0, c == KC - 1)
                        part_done(last, l, "out", k, x)

                def turn_h(x):
                    pe.wait_ge(sem("h_ready"), TILES * l + x + 1)
                    if x >= 2:
                        pe.wait_ge(sem("ht2_low"), TILES * l + x - 1)
                        pe.wait_ge(sem("ht2_high"), TILES * l + x - 1)
                    turn(H[:, x % 2, :], 2 * (x % 2)).then_inc(sem("h_turned"), 1)

                for x in range(nt):
                    project(x)
                    if x >= 2:
                        turn_h(x - 2)
                pe.wait_ge(sem("mix_added"), 4 * TILES * l + 4 * nt)
                turn_h(nt - 2)
                turn_h(nt - 1)
                pe.wait_ge(sem("ht2_low"), TILES * l + nt)
                pe.wait_ge(sem("ht2_high"), TILES * l + nt)
                for x, t in enumerate(tiles):
                    for c in range(KC):
                        last = mm(bank[7][:, x * NE:(x + 1) * NE], hT[:, c, t * P:(t + 1) * P], rw[:, l, c, :], c == 0, c == KC - 1)
                last.then_inc(sem("logits_done"), 1)

                def shared_up(x):
                    t = tiles[x]
                    for m, name in enumerate(("sw1", "sw3")):
                        n = unit_no(l, name)
                        unit_landed(pe, n)
                        for c in range(KC):
                            last = mm(bank[2 + x % 2][:, m * EH:(m + 1) * EH], hT[:, c, t * P:(t + 1) * P], unit(n)[:, c * UC:(c + 1) * UC], c == 0, c == KC - 1)
                        if name == "sw3":
                            part_done(last, l, name, 0, x)
                        elif x == nt - 1:
                            part_done(last, l, name, 0, 0)

                def hidden_turn(x):
                    for c in range(2):
                        last = nc.tensor.transpose(bank[4][:, c * P:(c + 1) * P], HID[:, x % 2, c::2], ident[:, :])
                    return last

                def shared_down(x):
                    pe.wait_ge(sem("shid_ready"), TILES * l + x + 1)
                    if x:
                        pe.wait_ge(sem("shidt_ready"), TILES * l + x)
                        pe.wait_ge(sem("sff_ready"), 2 * TILES * l + 2 * x)
                    hidden_turn(x).then_inc(sem("shid_turned"), 1)
                    pe.wait_ge(sem("shidt_ready"), TILES * l + x + 1)
                    n = unit_no(l, "sw2")
                    unit_landed(pe, n)
                    for y in range(2):
                        for c in range(2):
                            last = mm(bank[5 + y][:, :], HIDT[:, x % 2, c * P:(c + 1) * P], unit(n)[:, c * D + y * 512:c * D + (y + 1) * 512], c == 0, c == 1)
                    part_done(last, l, "sw2", 0, x)

                shared_up(0)
                shared_up(1)
                pe.wait_ge(sem("sel_ready"), l + 1)
                pe.wait_ge(sem("dve_start"), 3)
                pe.wait_ge(sem("pool_set"), 4)
                for x in range(nt):
                    for y in range(x + 1):
                        mm(bank[0][:, x * NE:(x + 1) * NE], (tri if y == x else ones)[:, :], selb[:, y, :], y == 0, y == x)
                for y in range(nt):
                    last = mm(bank[1][:, 0:NE], ones[:, :], selb[:, y, :], y == 0, y == nt - 1)
                last.then_inc(sem("places_done"), 1)
                shared_down(0)
                for x in range(2, nt):
                    pe.wait_ge(sem("shid_ready"), TILES * l + x - 1)
                    shared_up(x)
                    shared_down(x - 1)
                shared_down(nt - 1)

                pe.wait_ge(sem("small_landed"), 16 * len(small))

                def slots(i, b):
                    pe.wait_ge(sem(f"hot_ready{l}"), i + 1)
                    e = pe.value_load(tabi[0:1, bass.ds(i, 1)] if not isinstance(i, int) else tabi[0:1, i:i + 1], min_val=0, max_val=NE - 1)
                    for x in range(nt):
                        last = mm(bank[7][:, 0:12], PH[:, b, x, :], vals[:, x, bass.ds(e, 1), :].rearrange("p e k -> p (e k)"), x == 0, x == nt - 1)
                    last.then_inc(sem(f"slots_done{l}"), 1)

                def up(b):
                    for c in range(KC):
                        last = mm(bank[2][:, :].rearrange("p (m n) -> p m n", m=2), XT[:, c * P:(c + 1) * P], W13[b][:, :, c, :], c == 0, c == KC - 1)
                    last.then_inc(sem(f"up_done{l}"), 1)

                def down(b):
                    for y in range(2):
                        for c in range(2):
                            last = mm(bank[5 + y][:, :], HXT[:, c * P:(c + 1) * P], W2[b][:, c, y * 512:(y + 1) * 512], c == 0, c == 1)
                    last.then_inc(sem(f"down_done{l}"), 1)

                def expert_turn():
                    for c in range(2):
                        last = nc.tensor.transpose(bank[4][:, c * P:(c + 1) * P], HX[:, c::2], ident[:, :])
                    last.then_inc(sem(f"hid_turned{l}"), 1)

                def step(turn_no, b):
                    i = NB * turn_no + b
                    static = isinstance(i, int)
                    pe.wait_ge(sem(f"xt_low{l}"), i + 1)
                    pe.wait_ge(sem(f"xt_high{l}"), i + 1)
                    if not static or i:
                        pe.wait_ge(sem(f"hid_ready{l}"), i)
                    pe.wait_ge(sem(f"w13_landed{b}_{l}"), 32 * (turn_no + 1))
                    up(b)
                    if not static or i:
                        expert_turn()
                    pe.wait_ge(sem(f"xg_landed{(b + 1) % NB}_{l}"), 16 * (turn_no + 1 + (b + 1) // NB))
                    turn(XG[:, (b + 1) % NB, :], 0).then_inc(sem(f"xg_turned{l}"), 1)
                    pe.wait_ge(sem(f"idx_ready{l}"), i + NB)
                    slots(i + NB, b)
                    if not static or i:
                        pe.wait_ge(sem(f"hidt_ready{l}"), i)
                        if not static or i > 1:
                            pe.wait_ge(sem(f"y_ready{l}"), 2 * i - 2)
                        pe.wait_ge(sem(f"w2_landed{(b - 1) % NB}_{l}"), 16 * (turn_no + (1 if b else 0)))
                        down((b - 1) % NB)

                pe.wait_ge(sem("table_ready"), l + 1)
                pe.wait_ge(sem("sff_ready"), 2 * TILES * l + 2 * nt)
                final = pe.value_load(tabi[0:1, NSLOT:NSLOT + 1], min_val=TURNS[0] - 1, max_val=TURNS[1] - 1)
                for i in range(NB):
                    if i:
                        pe.wait_ge(sem(f"idx_ready{l}"), i)
                    slots(i, i)
                pe.wait_ge(sem(f"xg_landed0_{l}"), 16)
                turn(XG[:, 0, :], 0).then_inc(sem(f"xg_turned{l}"), 1)
                for i in range(2 * NB):
                    step(i // NB, i % NB)
                with pe.Fori(2, final + 1) as turn_no:
                    for b in range(NB):
                        step(turn_no, b)
                pe.wait_ge(sem(f"hid_ready{l}"), NB * final + NB)
                expert_turn()
                pe.wait_ge(sem(f"hidt_ready{l}"), NB * final + NB)
                pe.wait_ge(sem(f"y_ready{l}"), 2 * NB * final + 2 * (NB - 1))
                pe.wait_ge(sem(f"w2_landed{NB - 1}_{l}"), 16 * (final + 1))
                down(NB - 1)
                pe.wait_ge(sem(f"xt_low{l}"), NB * final + (NB + 1))
                pe.wait_ge(sem(f"xt_high{l}"), NB * final + (NB + 1))

                for x in range(nt):
                    if x >= 2:
                        pe.wait_ge(sem("rb_read"), 2 * TILES * l + 2 * x - 2)
                    if x == 0:
                        pe.wait_ge(sem(f"y_ready{l}"), 2 * NB * final + 2 * NB)
                    for k in range(2):
                        pe.wait_ge(sem(f"rb_landed{k}"), 64 * l + 16 * (x + 1))
                        for j in range(4 - 2 * k):
                            for y in range(2):
                                last = mm(bank[4 + 2 * (x % 2) + y][:, :], ident[:, :], RB[k][:, j, y * 512:(y + 1) * 512], k + j == 0, k == 1 and j == 1)
                        last.then_inc(sem("rb_summed"), 1)

        @block.scalar
        def _(act):
            def do(o, i, f, **kw):
                return nc.scalar.activation(o, i, f, **kw)

            act.wait_ge(sem("c_landed"), 32)
            do(csig[:, :, :], ccol[:, :, :], ACT.Sigmoid).then_inc(sem("act_start"), 1)
            act.wait_ge(sem("dve_start"), 2)
            do(lbt[:, 0:2, :], lbt[:, 0:2, :], ACT.Exp).then_inc(sem("act_start"), 1)
            act.wait_ge(sem("small_landed"), 16 * len(small))

            for l in range(DEPTH):
                tiles, segs = tiles_of(l), segs_of(l)
                nt, s0 = len(tiles), segs[0]
                x0 = tiles[0] * P
                act.wait_ge(sem("modcol_ready"), l + 1)
                for t in range(TILES):
                    act.wait_ge(sem("xh_turned"), TILES * l + t + 1)
                    for c in range(4):
                        m = modcol[:, 1 - t // 2, :, c:c + 1]
                        last = do(hT[:, c, t * P:(t + 1) * P], bank[2 * (t % 2)][:, c * P:(c + 1) * P], ACT.Identity, scale=m[:, 1, :], bias=m[:, 0, :])
                    last.then_inc(sem("ht_low"), 1)
                for p in range(2):
                    cp = 2 * l + p
                    if p:
                        act.wait_ge(sem("lvl_used"), NLEV * cp)
                    for d in range(2):
                        for j in range(2):
                            wait_part(act, l, ("ffw", "fbw")[d], p, j)
                            do(seg_head(kk[d], j), bk(2 * d + j, 2, 256), ACT.Sigmoid).then_inc(sem("f_sig"), 1)
                    for j in range(2):
                        wait_part(act, l, "q", p, j)
                        do(seg_head(qq, j)[:, s0:2, :], bk(4 + j, 2, 256)[:, s0:2, :], ACT.Sigmoid).then_inc(sem("q_sig"), 1)
                    for b in range(2):
                        wait_part(act, l, "i", p, b)
                        do(V[:, 2 * b:2 * b + 2, :], bk(6 + b, 2, 256), ACT.Copy).then_inc(sem("v_ready"), 1)
                    for n, s in enumerate(segs):
                        wait_part(act, l, "g", p, n)
                        do(G[:, 2 * s:2 * s + 2, :], bk(s, 2, 256), ACT.Sigmoid).then_inc(sem("g_sig"), 1)
                    for d in range(2):
                        act.wait_ge(sem("f_ready"), 2 * cp + d + 1)
                        do(bb[d], kk[d], ACT.Ln).then_inc(sem("lf_ready"), 1)
                    for d in range(2):
                        act.wait_ge(sem("b_ready"), 2 * cp + d + 1)
                        do(QE[d], bb[d], ACT.Exp).then_inc(sem("eb_ready"), 1)
                    for d in range(2):
                        act.wait_ge(sem("kdx_ready"), 2 * cp + d + 1)
                        e = (EA, EB)[d][0]
                        do(e, e, ACT.Exp).then_inc(sem("kde_ready"), 1)
                    for d in range(2):
                        act.wait_ge(sem("kd_turned"), 2 * cp + d + 1)
                        for y in range(2):
                            do(KDT[d][:, y * 512:(y + 1) * 512], bank[(6, 0)[d] + y][:, :], ACT.Copy).then_inc(sem("kdt_ready"), 1)
                    r = slice(512 * s0, 1024)
                    for n in range(1, NLEV):
                        act.wait_ge(sem("ex_ready"), (NLEV - 1) * cp + n)
                        do(EA[n % 3][:, r], EA[n % 3][:, r], ACT.Exp)
                        do(EB[n % 3][:, r], EB[n % 3][:, r], ACT.Exp).then_inc(sem("exp_done"), 1)
                    act.wait_ge(sem("o_done"), cp + 1)
                    for s in segs:
                        for n in range(4):
                            last = do(EA[1][:, (s * 4 + n) * P:(s * 4 + n + 1) * P], bank[s][:, n * P:(n + 1) * P], ACT.Square, accum_out=ssq[:, s * 4 + n:s * 4 + n + 1])
                    last.then_inc(sem("ssq_ready"), 1)
                    act.wait_ge(sem("ot_turned"), cp + 1)
                    for j in range(2):
                        last = do(mixT[:, 2 * p + j, x0:512], bank[2 + j][:, x0:512], ACT.Copy)
                    last.then_inc(sem("mix_ready"), 1)
                for n, s in enumerate(segs):
                    wait_part(act, l, "cq", 0, n)
                    for t in (2 * s, 2 * s + 1):
                        last = do(EA[1][:, t * QL:(t + 1) * QL], bank[s][:, (t % 2) * QL:(t % 2 + 1) * QL], ACT.Square, accum_out=ssq[:, t:t + 1])
                last.then_inc(sem("ssq_ready"), 1)
                wait_part(act, l, "ckv", 0, 0)
                act.wait_ge(sem("var_ready"), rstd_no(l, "cq"))
                for t in range(TILES):
                    last = do(EB[1][:, t * P:(t + 1) * P], bank[4][:, t * P:(t + 1) * P], ACT.Square, accum_out=ssq[:, t:t + 1])
                last.then_inc(sem("ssq_ready"), 1)
                wait_part(act, l, "ckv", 0, 1)
                do(KPR, bank[5][NOPE:QK, :], ACT.Copy).then_inc(sem("kpr_ready"), 1)
                act.wait_ge(sem("cq_turned"), l + 1)
                for c in range(2):
                    do(cqT[:, c, x0:512], bank[2 + c][:, x0:512], ACT.Copy, scale=qnw[:, l, c:c + 1]).then_inc(sem("cqt_ready"), 1)
                act.wait_ge(sem("ckv_turned"), l + 1)
                do(ckvT, bank[6][:, :], ACT.Copy, scale=kvw[:, l:l + 1]).then_inc(sem("ckvt_ready"), 1)
                for h in range(MLA_HEADS):
                    wait_part(act, l, "uq", 0, h)
                    do(qraw[0:QK, h, x0:512], bank[h % 2][0:QK, x0:512], ACT.Copy).then_inc(sem("qraw_ready"), 1)
                for h in range(MLA_HEADS):
                    wait_part(act, l, "ukv", 0, h)
                    do(kT[0:NOPE, h, :], bank[4 + h % 2][0:NOPE, :], ACT.Copy).then_inc(sem("kt_ready"), 1)
                for t in range(TILES):
                    wait_part(act, l, "ukv", 0, MLA_HEADS + t)
                    do(VM[:, t, :], bank[6 + t % 2][:, :], ACT.Copy).then_inc(sem("vm_ready"), 1)
                its = items[l]

                def probs(m):
                    g = item0[l] + m
                    act.wait_ge(sem("nmax_ready"), g + 1)
                    if m >= 2:
                        act.wait_ge(sem("probs_turned"), g - 1)
                    nk = 512 if its[m][1] else 256
                    for qt in range(2):
                        last = do(PR[:, m % 2, qt, 0:nk], bank[2 * (m % 2) + qt][:, 0:nk], ACT.Exp,
                                  bias=nmax[:, m % 2, qt:qt + 1], scale=QK ** -0.5, accum_out=asum[:, m % 2, qt:qt + 1])
                    last.then_inc(sem("pexp_ready"), 1)

                probs(0)
                for m in range(len(its)):
                    g = item0[l] + m
                    if m + 1 < len(its):
                        probs(m + 1)
                    act.wait_ge(sem("probs_turned"), g + 1)
                    if m >= 2:
                        act.wait_ge(sem("pv_done"), g - 1)
                    for y in range(2 if its[m][1] else 1):
                        last = do(PTT[m % 2][:, 2 * y:2 * y + 2, :], bk(4 + y, 2, 256), ACT.Copy)
                    last.then_inc(sem("pt_ready"), 1)

                for x, t in enumerate(tiles):
                    act.wait_ge(sem("h_turned"), TILES * l + x + 1)
                    do(hT[:, 0:4, t * P:(t + 1) * P], bk(2 * (x % 2), 4, P), ACT.Copy).then_inc(sem("ht2_low"), 1)
                act.wait_ge(sem("logits_done"), l + 1)
                do(sco[:, 0:nt, :], bk(7, TILES, NE)[:, 0:nt, :], ACT.Sigmoid).then_inc(sem("sco_ready"), 1)

                def shared_sig(x):
                    wait_part(act, l, "sw3", 0, x)
                    if x:
                        act.wait_ge(sem("shid_ready"), TILES * l + x)
                    do(SG, bank[2 + x % 2][:, 0:EH], ACT.Sigmoid).then_inc(sem("ssig_ready"), 1)

                act.wait_ge(sem("h_stored0"), 32 * l + 16 * (nt // 2))
                shared_sig(0)
                shared_sig(1)
                for x in range(nt):
                    act.wait_ge(sem("shid_turned"), TILES * l + x + 1)
                    do(HIDT[:, x % 2, :], bank[4][:, 0:EH], ACT.Copy).then_inc(sem("shidt_ready"), 1)
                    wait_part(act, l, "sw2", 0, x)
                    do(FF[:, x, 0:512], bank[5][:, :], ACT.Copy).then_inc(sem("sff_ready"), 1)
                    if x + 2 < nt:
                        shared_sig(x + 2)

                def xt_low(i):
                    act.wait_ge(sem(f"xg_turned{l}"), i + 1)
                    if not isinstance(i, int) or i:
                        act.wait_ge(sem(f"up_done{l}"), i)
                    do(XT[:, 0:512], bank[0][:, :], ACT.Copy).then_inc(sem(f"xt_low{l}"), 1)

                def hidden_out(i):
                    act.wait_ge(sem(f"hid_turned{l}"), i + 1)
                    if not isinstance(i, int) or i:
                        act.wait_ge(sem(f"down_done{l}"), i)
                    do(HXT, bank[4][:, 0:EH], ACT.Copy).then_inc(sem(f"hidt_ready{l}"), 1)

                def step(turn_no, b):
                    i = NB * turn_no + b
                    static = isinstance(i, int)
                    act.wait_ge(sem(f"up_done{l}"), i + 1)
                    if not static or i:
                        act.wait_ge(sem(f"hid_ready{l}"), i)
                    do(SG, bank[2][:, 0:EH], ACT.Sigmoid).then_inc(sem(f"sig_ready{l}"), 1)
                    if not static or i:
                        hidden_out(i - 1)
                    xt_low(i + 1)
                    if not static or i:
                        y_low(i - 1, turn_no - (0 if b else 1), (b - 1) % NB)

                def y_low(i, before, b):
                    act.wait_ge(sem(f"down_done{l}"), i + 1)
                    if not isinstance(i, int) or i >= NB:
                        act.wait_ge(sem(f"y_stored{b}_{l}"), 16 * before)
                    do(Y[b][:, 0:512], bank[5][:, :], ACT.Copy).then_inc(sem(f"y_ready{l}"), 1)

                xt_low(0)
                for i in range(2 * NB):
                    step(i // NB, i % NB)
                act.wait_ge(sem("table_ready"), l + 1)
                final = act.value_load(tabi[0:1, NSLOT:NSLOT + 1], min_val=TURNS[0] - 1, max_val=TURNS[1] - 1)
                with act.Fori(2, final + 1) as turn_no:
                    for b in range(NB):
                        step(turn_no, b)
                hidden_out(NB * final + (NB - 1))
                y_low(NB * final + (NB - 1), final, NB - 1)

        @block.vector
        def _(dve):
            V_ = nc.vector
            count = [0]

            def then(ins):
                count[0] += 1
                ins.then_inc(sem("dve_order"), 1)
                dve.wait_ge(sem("dve_order"), count[0])

            def tt(o, a, b, op):
                return V_.tensor_tensor(o, a, b, op)

            dve.wait_ge(sem("act_start"), 1)
            tt(csil[:, :, :].rearrange("p c s -> p s c"), ccol[:, :, :], csig[:, :, :], ALU.mult).then_inc(sem("dve_start"), 1)
            dve.wait_ge(sem("small_landed"), 16 * len(small))
            then(tt(lbt[:, 2, :], lbc[:, 0, :], lbc[:, 1, :], ALU.max))
            tt(lbt[:, 0, :], lbc[:, 0, :], lbt[:, 2, :], ALU.subtract)
            tt(lbt[:, 1, :], lbc[:, 1, :], lbt[:, 2, :], ALU.subtract).then_inc(sem("dve_start"), 1)
            V_.memset(lb[:, 0, :], 0.0)
            V_.memset(oml[:, 0, :], 1.0)
            V_.memset(noff[:, 0:NE], 0.0)
            then(V_.tensor_copy(masks[:, :], maskf))
            V_.tensor_copy(tri[:, :], trif[:, :]).then_inc(sem("dve_start"), 1)
            dve.wait_ge(sem("act_start"), 2)
            then(tt(lbt[:, 0, :], lbt[:, 0, :], lbt[:, 1, :], ALU.add))
            then(V_.reciprocal(lbt[:, 2, :], lbt[:, 0, :]))
            then(tt(lb[:, 1, :], lbt[:, 1, :], lbt[:, 2, :], ALU.mult))
            then(V_.tensor_scalar(oml[:, 1, :], lb[:, 1, :], -1.0, 1.0, ALU.mult, ALU.add))
            dve.wait_ge(sem("bmod_landed"), 16)
            for n in range(DEPTH * MODU):
                dve.wait_ge(sem("unit_done"), n + 1)
                tt(modrow[:, n * UC:(n + 1) * UC], bank[n % 4][0:2, 0:UC], bmod[:, n * UC:(n + 1) * UC], ALU.add).then_inc(sem("mod_added"), 1)

            def stats_of(t):
                V_.bn_stats(stats[:, t, 0, :], X[:, t, 0:512])
                then(V_.bn_stats(stats[:, t, 1, :], X[:, t, 512:1024]))
                then(V_.bn_aggr(mv[:, t, :], stats[:, t, :, :].rearrange("p a b -> p (a b)")))

            def inverse(l, name, k, src, dst, scale, eps=EPS):
                V_.tensor_scalar(dst, src, scale, eps, ALU.mult, ALU.add).then_inc(sem("var_ready"), 1)
                dve.wait_ge(sem("rstd_ready"), rstd_no(l, name, k))

            def norm_rows(l, name, t, o):
                stats_of(t)
                inverse(l, name, t, mv[:, t, 1:2], rin[:, 0:1], 1.0)
                then(V_.tensor_scalar(o, X[:, t, :], mv[:, t, 0:1], rout[:, 0:1], ALU.subtract, ALU.mult))

            dve.wait_ge(sem("pool_set"), 2)
            dve.wait_ge(sem("x_landed"), 16 * TILES)

            for l in range(DEPTH):
                tiles, segs = tiles_of(l), segs_of(l)
                nt, s0 = len(tiles), segs[0]
                x0 = tiles[0] * P
                r = slice(512 * s0, 1024)
                for t in range(TILES):
                    stats_of(t)
                dve.wait_ge(sem("modcol_landed"), 64 * l + 64)
                V_.tensor_scalar(modcol[:, :, 1, :], modcol[:, :, 1, :], 1.0, None, ALU.add).then_inc(sem("modcol_ready"), 1)
                inverse(l, "a", 0, mv[:, :, 1], rin[:, 0:TILES], 1.0)
                dve.wait_ge(sem("modcol_ready"), l + 1)

                def ht_high(t):
                    dve.wait_ge(sem("xh_turned"), TILES * l + t + 1)
                    for c in range(4, 8):
                        m = modcol[:, 1 - t // 2, :, c:c + 1]
                        last = V_.tensor_scalar(hT[:, c, t * P:(t + 1) * P], bank[2 * (t % 2) + 1][:, (c - 4) * P:(c - 3) * P],
                                                m[:, 1, :], m[:, 0, :], ALU.mult, ALU.add)
                    last.then_inc(sem("ht_high"), 1)

                if l == 0:
                    dve.wait_ge(sem("mod_stored"), 16)
                for t in range(TILES):
                    if t >= 2:
                        dve.wait_ge(sem("xh_turned"), TILES * l + t - 1)
                    V_.tensor_scalar(XH[:, t % 2, :], X[:, t, :], mv[:, t, 0:1], rout[:, t:t + 1], ALU.subtract, ALU.mult).then_inc(sem("xh_ready"), 1)
                    if t:
                        ht_high(t - 1)
                ht_high(TILES - 1)

                for p in range(2):
                    cp = 2 * l + p
                    for d in range(2):
                        for j in range(2):
                            dve.wait_ge(sem("f_sig"), 4 * cp + 2 * d + j + 1)
                            h = d * HEADS + 2 * p + j
                            last = V_.tensor_scalar(seg_head(kk[d], j), seg_head(kk[d], j), oml[:, l, h:h + 1], lb[:, l, h:h + 1], ALU.mult, ALU.add)
                        last.then_inc(sem("f_ready"), 1)
                    for j in range(2):
                        dve.wait_ge(sem("q_sig"), 2 * cp + j + 1)
                        o = seg_head(qq, j)[:, s0:2, :]
                        last = V_.scalar_tensor_tensor(o, bk(4 + j, 2, 256)[:, s0:2, :], HD ** -0.5, o, ALU.mult, ALU.mult)
                    last.then_inc(sem("q_ready"), 1)
                    for n, s in enumerate(segs):
                        dve.wait_ge(sem("g_sig"), 4 * l + p * len(segs) + n + 1)
                        g = G[:, 2 * s:2 * s + 2, :]
                        last = tt(g, g, bk(s, 2, 256), ALU.mult)
                    last.then_inc(sem("g_used"), 1)
                    dve.wait_ge(sem("g_used"), cp + 1)
                    g = G[:, 2 * s0:TILES, :].rearrange("p t (j v) -> p (t j) v", j=2)
                    tt(g, g, hgw[:, l, :].unsqueeze(1).broadcast_to([P, 4 * len(segs), HD]), ALU.mult)
                    if p == 0:
                        dve.wait_ge(sem("scan_landed"), 16 * l + 16)
                    for d in range(2):
                        dve.wait_ge(sem("lf_ready"), 2 * cp + d + 1)
                        V_.tensor_scalar(kk[d], kk[d], -1.0, 1.0, ALU.mult, ALU.add)
                        b = bb[d][:, ::-1] if d else bb[d]
                        V_.tensor_tensor_scan(b, scanm, b, 0.0, ALU.mult, ALU.add).then_inc(sem("b_ready"), 1)
                    if p:
                        dve.wait_ge(sem("lvl_done"), NLEV * cp)
                    for d in range(2):
                        dve.wait_ge(sem("b_ready"), 2 * cp + d + 1)
                        b = bb[d].rearrange("p (n t) -> p n t", t=P)
                        edge = b[:, :, P - 1:P] if d == 0 else b[:, :, 0:1]
                        tt((EA, EB)[d][0].rearrange("p (n t) -> p n t", t=P), edge.broadcast_to([P, 8, P]), b, ALU.subtract).then_inc(sem("kdx_ready"), 1)
                    for d in range(2):
                        dve.wait_ge(sem("eb_ready"), 2 * cp + d + 1)
                        q = QE[d].rearrange("p (n t) -> p n t", t=P)
                        last = V_.tensor_copy(el[:, d, :].unsqueeze(2), q[:, :, P - 1:P] if d == 0 else q[:, :, 0:1])
                    then(last)
                    dve.wait_ge(sem("q_ready"), cp + 1)
                    for d in range(2):
                        last = tt(QE[d][:, r], QE[d][:, r], qq[:, r], ALU.mult)
                    last.then_inc(sem("qe_ready"), 1)
                    for d in range(2):
                        dve.wait_ge(sem("kde_ready"), 2 * cp + d + 1)
                        e = (EA, EB)[d][0]
                        tt(e, e, kk[d], ALU.mult).then_inc(sem("kd_ready"), 1)

                    def halves(a, h):
                        return a[:, r].rearrange("p (n a h) -> p n a h", a=2, h=h)

                    def exponents(n):
                        h = 64 >> (n - 1)
                        nb = (1024 - 512 * s0) // (2 * h)
                        if n >= 3:
                            dve.wait_ge(sem("lvl_done"), NLEV * cp + n - 2)
                        b, c = halves(bb[0], h), halves(bb[1], h)
                        ea, eb = halves(EA[n % 3], h), halves(EB[n % 3], h)
                        bm = b[:, :, 0, h - 1:h].broadcast_to([P, nb, h])
                        cm = c[:, :, 1, 0:1].broadcast_to([P, nb, h])
                        tt(ea[:, :, 0, :], c[:, :, 0, :], cm, ALU.subtract)
                        tt(ea[:, :, 1, :], b[:, :, 1, :], bm, ALU.subtract)
                        tt(eb[:, :, 0, :], bm, b[:, :, 0, :], ALU.subtract)
                        tt(eb[:, :, 1, :], cm, c[:, :, 1, :], ALU.subtract).then_inc(sem("ex_ready"), 1)

                    def weigh(n):
                        h = 64 >> (n - 1)
                        dve.wait_ge(sem("exp_done"), (NLEV - 1) * cp + n)
                        tt(EA[n % 3][:, r], EA[n % 3][:, r], qq[:, r], ALU.mult)
                        eb = halves(EB[n % 3], h)
                        for d in range(2):
                            last = tt(eb[:, :, d, :], eb[:, :, d, :], halves(kk[d], h)[:, :, d, :], ALU.mult)
                        last.then_inc(sem("lvl_ready"), 1)

                    def collect(n):
                        dve.wait_ge(sem("lvl_done"), NLEV * cp + n + 1)
                        if n:
                            dve.wait_ge(sem("lvl_used"), NLEV * cp + n)
                        for s in segs:
                            o = ST[:, s, :].rearrange("p (a t) -> p a t", t=P)
                            x = bk(2 + 2 * (n % 2) + s, 4, P)
                            if n == 0:
                                last = tt(o, x, ident[:, :].unsqueeze(1).broadcast_to([P, 4, P]), ALU.mult)
                            else:
                                last = V_.copy_predicated(o, masks[:, n * P:(n + 1) * P].unsqueeze(1).broadcast_to([P, 4, P]), x)
                        last.then_inc(sem("lvl_used"), 1)

                    def state(k):
                        dve.wait_ge(sem("state_sum"), 3 * cp + k + 1)
                        if k:
                            dve.wait_ge(sem("state_ready"), 3 * cp + k)
                        for d, order in enumerate((CHUNKS_FW, CHUNKS_BW)):
                            for j in range(2):
                                blk = (order[k] // 2) * 4 + j * 2 + order[k] % 2
                                x = bank[6 + k % 2][:, (2 * d + j) * P:(2 * d + j + 1) * P]
                                at = (d * 2 + j) * 3 + k
                                if k:
                                    last = V_.scalar_tensor_tensor(SS[:, at, :], SS[:, at - 1, :], el[:, d, blk:blk + 1], x, ALU.mult, ALU.add)
                                else:
                                    last = V_.tensor_copy(SS[:, at, :], x)
                        last.then_inc(sem("state_ready"), 1)

                    exponents(1)
                    dve.wait_ge(sem("kd_turned"), 2 * cp + 2)
                    tt(EB[0][:, r], kk[0][:, r], kk[1][:, r], ALU.add).then_inc(sem("lvl_ready"), 1)
                    state(0)
                    state(1)
                    state(2)
                    exponents(2)
                    weigh(1)
                    collect(0)
                    for n in range(2, NLEV):
                        if n + 1 < NLEV:
                            exponents(n + 1)
                        weigh(n)
                        collect(n - 1)
                    collect(NLEV - 1)
                    dve.wait_ge(sem("ssq_ready"), 4 * l + p + 1)
                    inverse(l, "hg", p, ssq[:, 4 * s0:8], rin[:, 4 * s0:8], 1.0 / HD)
                    for s in segs:
                        for c in range(2):
                            for j in range(2):
                                n = s * 4 + c * 2 + j
                                last = V_.scalar_tensor_tensor(OT[:, 2 * s + c, j * P:(j + 1) * P], bank[s][:, (c * 2 + j) * P:(c * 2 + j + 1) * P],
                                                               rout[:, n:n + 1], G[:, 2 * s + c, j * P:(j + 1) * P], ALU.mult, ALU.mult)
                    last.then_inc(sem("ot_ready"), 1)

                dve.wait_ge(sem("ssq_ready"), 4 * l + 3)
                inverse(l, "cq", 0, ssq[:, tiles[0]:TILES], rin[:, tiles[0]:TILES], 1.0 / QL)
                for t in tiles:
                    last = V_.tensor_scalar(cqn[:, t, :], bank[t // 2][:, (t % 2) * QL:(t % 2 + 1) * QL], rout[:, t:t + 1], None, ALU.mult)
                last.then_inc(sem("cqn_ready"), 1)
                dve.wait_ge(sem("ssq_ready"), 4 * l + 4)
                inverse(l, "ckv", 0, ssq[:, 0:TILES], rin[:, 0:TILES], 1.0 / KVL)
                for t in range(TILES):
                    last = V_.tensor_scalar(ckvn[:, t, :], bank[4][:, t * P:(t + 1) * P], rout[:, t:t + 1], None, ALU.mult)
                last.then_inc(sem("ckvn_ready"), 1)
                dve.wait_ge(sem("qraw_ready"), MLA_HEADS * (l + 1))
                V_.tensor_copy(qrot[0:NOPE, :, :], qraw[0:NOPE, :, 256:512])
                dve.wait_ge(sem("kpr_ready"), l + 1)
                V_.tensor_copy(KR[:, 0:256], KPR[:, 0:256])
                cos, sin = cs[NOPE:QK, 0, :], cs[NOPE:QK, 1, :]
                for n in range(5):
                    if n < 4:
                        shape = [ROPE, 2, 256]
                        o, raw = qrot[NOPE:QK, 2 * n:2 * n + 2, :], qraw[NOPE:QK, 2 * n:2 * n + 2, 256:512]
                        sw = bank[2 + n % 2][NOPE:QK, :].rearrange("p (h t) -> p h t", h=2)
                    else:
                        shape = [ROPE, 1, 256]
                        o, raw, sw = KR[:, 256:512].unsqueeze(1), KPR[:, 256:512].unsqueeze(1), bank[2][NOPE:QK, 0:256].unsqueeze(1)
                    tmp = qsw[NOPE:QK, 512 * (n % 4):512 * (n % 4) + 256 * shape[1]].rearrange("p (h t) -> p h t", t=256)
                    tt(tmp, raw, cos.unsqueeze(1).broadcast_to(shape), ALU.mult)
                    dve.wait_ge(sem("swap_done"), 5 * l + n + 1)
                    then(tt(o, sw, sin.unsqueeze(1).broadcast_to(shape), ALU.mult))
                    tt(o, o, tmp, ALU.add).then_inc(sem("swap_used"), 1)
                dve.wait_ge(sem("swap_used"), 5 * (l + 1))
                V_.tensor_copy(kT[NOPE:QK, :, :], KR.unsqueeze(1).broadcast_to([ROPE, MLA_HEADS, 512])).then_inc(sem("keys_ready"), 1)
                its = items[l]

                def maximum(m):
                    g = item0[l] + m
                    dve.wait_ge(sem("scores_done"), g + 1)
                    nk = 512 if its[m][1] else 256
                    for qt in range(2):
                        last = V_.tensor_reduce(amax[:, m % 2, qt:qt + 1], bank[2 * (m % 2) + qt][:, 0:nk], AX.X, ALU.max)
                    then(last)
                    V_.tensor_scalar(nmax[:, m % 2, :], amax[:, m % 2, :], -(QK ** -0.5), None, ALU.mult).then_inc(sem("nmax_ready"), 1)

                def attended(m):
                    h, x = its[m]
                    g = item0[l] + m
                    dve.wait_ge(sem("pv_done"), g + 1)
                    rows = slice((h % 2) * MV, (h % 2 + 1) * MV)
                    V_.tensor_copy(mixT[rows, HEADS + h // 2, 256 * x:256 * x + 256], bank[6 + m % 2][rows, 0:256]).then_inc(sem("attn_out"), 1)

                maximum(0)
                for m in range(len(its)):
                    g = item0[l] + m
                    nk = 512 if its[m][1] else 256
                    if m + 1 < len(its):
                        maximum(m + 1)
                    dve.wait_ge(sem("pexp_ready"), g + 1)
                    then(V_.reciprocal(ainv[:, m % 2, :], asum[:, m % 2, :]))
                    for qt in range(2):
                        pr = PR[:, m % 2, qt, 0:nk]
                        last = V_.tensor_scalar(pr, pr, ainv[:, m % 2, qt:qt + 1], None, ALU.mult)
                    last.then_inc(sem("probs_ready"), 1)
                    if m:
                        attended(m - 1)
                attended(len(its) - 1)

                dve.wait_ge(sem("rows1_landed"), 128 * l + 16 * (2 + 3 * len(segs)))
                def add_mixed(x):
                    t = tiles[x]
                    for k in range(4):
                        wait_part(dve, l, "out", k, x)
                        cols = slice(k * UC, (k + 1) * UC)
                        then(tt(GT[:, k % 2, :], bank[4 + k][:, 0:UC], BV[:, 1 - t // 2, cols], ALU.mult))
                        last = V_.scalar_tensor_tensor(X[:, t, cols], X[:, t, cols], ALPHA, GT[:, k % 2, :], ALU.mult, ALU.add)
                        last.then_inc(sem("mix_added"), 1)
                    dve.wait_ge(sem("mix_added"), 4 * TILES * l + 4 * x + 4)

                def affine(t, wrow, brow):
                    then(tt(X[:, t, :], X[:, t, :], BV[:, wrow, :], ALU.mult))
                    then(tt(X[:, t, :], X[:, t, :], BV[:, brow, :], ALU.add))

                def ht2_high(x):
                    t = tiles[x]
                    dve.wait_ge(sem("h_turned"), TILES * l + x + 1)
                    V_.tensor_copy(hT[:, 4:8, t * P:(t + 1) * P], bk(2 * (x % 2) + 1, 4, P)).then_inc(sem("ht2_high"), 1)

                for x, t in enumerate(tiles):
                    s = 1 - t // 2
                    add_mixed(x)
                    norm_rows(l, "post1", t, X[:, t, :])
                    affine(t, 2, 3)
                    if x >= 2:
                        dve.wait_ge(sem("h_turned"), TILES * l + x - 1)
                        dve.wait_ge(sem(f"h_stored{x % 2}"), 32 * l + 16)
                    norm_rows(l, "post2", t, H[:, x % 2, :])
                    hh = H[:, x % 2, :]
                    if x == 0:
                        then(V_.tensor_scalar(BV[:, 6:6 + len(segs), :], BV[:, 6:6 + len(segs), :], 1.0, None, ALU.add))
                    then(tt(hh, hh, BV[:, 6 + s, :], ALU.mult))
                    tt(hh, hh, BV[:, 4 + s, :], ALU.add).then_inc(sem("h_ready"), 1)
                    if x:
                        ht2_high(x - 1)
                ht2_high(nt - 1)

                dve.wait_ge(sem("sco_ready"), l + 1)
                then(tt(bia[:, 0:nt, :], sco[:, 0:nt, :], rbias[:, l, :].unsqueeze(1).broadcast_to([P, nt, NE]), ALU.add))
                for x in range(nt):
                    last = V_.max(top8[:, x, :], bia[:, x, :])
                then(last)
                for x in range(nt):
                    last = V_.match_replace(rep[:, x, :], top8[:, x, :], bia[:, x, :], -1e30)
                then(last)
                tt(selb[:, 0:nt, :], rep[:, 0:nt, :], bia[:, 0:nt, :], ALU.not_equal).then_inc(sem("sel_ready"), 1)
                then(tt(sel[:, 0:nt, :], rep[:, 0:nt, :], bia[:, 0:nt, :], ALU.not_equal))

                def shared_hidden(x):
                    dve.wait_ge(sem("ssig_ready"), TILES * l + x + 1)
                    if x >= 2:
                        dve.wait_ge(sem("shid_turned"), TILES * l + x - 1)
                    b = bank[2 + x % 2]
                    then(tt(HID[:, x % 2, :], SG, b[:, 0:EH], ALU.mult))
                    tt(HID[:, x % 2, :], HID[:, x % 2, :], b[:, EH:2 * EH], ALU.mult).then_inc(sem("shid_ready"), 1)

                shared_hidden(0)
                shared_hidden(1)
                dve.wait_ge(sem("h_stored0"), 32 * l + 16 * (nt // 2))
                then(tt(CW[:, 0:nt, :], sel[:, 0:nt, :], sco[:, 0:nt, :], ALU.mult))
                then(V_.tensor_reduce(gsum[:, 0:nt, 0:1], CW[:, 0:nt, :], AX.X, ALU.add))
                then(V_.reciprocal(gsum[:, 0:nt, 1:2], gsum[:, 0:nt, 0:1]))
                for x in range(nt):
                    last = V_.tensor_scalar(CW[:, x, :], CW[:, x, :], gsum[:, x, 1:2], ROUTED_SCALE, ALU.mult, ALU.mult)
                then(last)
                for x in range(nt):
                    last = V_.tensor_tensor_scan(kth[:, x, :], onesf[:, :], sel[:, x, :], 0.0, ALU.mult, ALU.add)
                then(last)
                then(V_.tensor_copy(vals[:, 0:nt, :, 0:4], kv[:, 0:nt, 0:4].unsqueeze(2).broadcast_to([P, nt, NE, 4])))
                then(V_.tensor_copy(vals[:, 0:nt, :, 4:8], kv[:, 0:nt, 4:8].unsqueeze(2).broadcast_to([P, nt, NE, 4])))
                then(V_.tensor_copy(vals[:, 0:nt, :, 8:12], kv[:, 0:nt, 8:12].unsqueeze(2).broadcast_to([P, nt, NE, 4])))
                tt(vals[:, 0:nt, :, 7], kth[:, 0:nt, :], sel[:, 0:nt, :], ALU.subtract)
                for n in range(3):
                    then(V_.tensor_copy(vals[:, 0:nt, :, 8 + n], CW[:, 0:nt, :]))
                    if n < 2:
                        then(tt(CW[:, 0:nt, :], CW[:, 0:nt, :], vals[:, 0:nt, :, 8 + n], ALU.subtract))
                then(V_.tensor_scalar(posm[:, 0:nt, :], sel[:, 0:nt, :], -1000.0, 1000.0, ALU.mult, ALU.add))
                dve.wait_ge(sem("places_done"), l + 1)
                tt(posm[:, 0:nt, :], posm[:, 0:nt, :], bk(0, TILES, NE)[:, 0:nt, :], ALU.add)
                then(V_.tensor_copy(cnt[:, :], bank[1][:, 0:NE]))
                then(V_.tensor_scalar(over[:, :], cnt[:, :], float(P), None, ALU.is_gt))
                for n in range(2, TILES):
                    then(V_.scalar_tensor_tensor(over[:, :], cnt[:, :], float(n * P), over[:, :], ALU.is_gt, ALU.add))
                then(V_.tensor_tensor_scan(icum[:, :], onesf[:, :], over[:, :], 0.0, ALU.mult, ALU.add))
                ns = NSLOT - NE
                then(tt(cmpb, icum[:, :].unsqueeze(1).broadcast_to([P, ns, NE]), slotno[:, :].unsqueeze(2).broadcast_to([P, ns, NE]), ALU.is_le))
                then(V_.tensor_reduce(tabf[:, NE:NSLOT], cmpb, AX.X, ALU.add))
                then(tt(cmpb, cmpb, over[:, :].unsqueeze(1).broadcast_to([P, ns, NE]), ALU.mult))
                then(V_.tensor_reduce(exb[:, :], cmpb, AX.X, ALU.add))
                then(tt(exb[:, :], slotno[:, :], exb[:, :], ALU.subtract))
                then(V_.tensor_scalar(exb[:, :], exb[:, :], -float(P), -float(P), ALU.mult, ALU.add))
                then(V_.tensor_scalar(noff[:, NE:NSLOT], slotno[:, :], icum[:, NE - 1:NE], -8192.0, ALU.is_ge, ALU.mult))
                then(tt(noff[:, NE:NSLOT], noff[:, NE:NSLOT], exb[:, :], ALU.add))
                nx = TURNS[1] - TURNS[0]
                V_.tensor_scalar(exb[:, 0:nx], slotno[:, NB * TURNS[0] - NE:NB * TURNS[1] - NE:NB], icum[:, NE - 1:NE], None, ALU.is_lt)
                then(V_.tensor_scalar(tabi[:, 0:NSLOT], tabf[:, :], float(NE - 1), None, ALU.min))
                then(V_.tensor_reduce(nturn[:, 0:1], exb[:, 0:nx], AX.X, ALU.add))
                V_.tensor_scalar(tabi[:, NSLOT:NSLOT + 1], nturn[:, 0:1], float(TURNS[0] - 1), None, ALU.add).then_inc(sem("table_ready"), 1)
                dve.wait_ge(sem("table_ready"), l + 1)

                def shared_out(x):
                    wait_part(dve, l, "sw2", 0, x)
                    V_.tensor_copy(FF[:, x, 512:1024], bank[6][:, :]).then_inc(sem("sff_ready"), 1)

                for x in range(2, nt):
                    shared_hidden(x) if x == 2 else None
                    shared_out(x - 2)
                    if x + 1 < nt:
                        shared_hidden(x + 1)
                shared_out(nt - 2)
                shared_out(nt - 1)

                def hot(i, b):
                    e = dve.value_load(tabi[0:1, bass.ds(i, 1)] if not isinstance(i, int) else tabi[0:1, i:i + 1], min_val=0, max_val=NE - 1)
                    off = noff[:, bass.ds(i, 1)] if not isinstance(i, int) else noff[:, i:i + 1]
                    for x in range(nt):
                        last = V_.tensor_scalar(PH[:, b, x, :], iota[:, :], posm[:, x, bass.ds(e, 1)], off, ALU.subtract, ALU.is_equal)
                    last.then_inc(sem(f"hot_ready{l}"), 1)

                def indices(i, b, past=True):
                    dve.wait_ge(sem(f"slots_done{l}"), i + 1)
                    V_.tensor_reduce(idxf[:, b, :], bank[7][:, 0:12].rearrange("p (a k) -> p a k", k=4), AX.X, ALU.add).then_inc(sem(f"dve_turn{l}"), 1)
                    dve.wait_ge(sem(f"dve_turn{l}"), i + 1 + (i - NB + 1 if past else 0))
                    tt(idxi[:, b, :], idxf[:, b, 0:2], bigc[:, :], ALU.add).then_inc(sem(f"idx_ready{l}"), 1)

                def xt_high(i):
                    dve.wait_ge(sem(f"xg_turned{l}"), i + 1)
                    if not isinstance(i, int) or i:
                        dve.wait_ge(sem(f"up_done{l}"), i)
                    V_.tensor_copy(XT[:, 512:1024], bank[1][:, :]).then_inc(sem(f"xt_high{l}"), 1)

                def y_high(i, before, b):
                    dve.wait_ge(sem(f"down_done{l}"), i + 1)
                    if not isinstance(i, int) or i >= NB:
                        dve.wait_ge(sem(f"y_stored{b}_{l}"), 16 * before)
                    V_.tensor_copy(Y[b][:, 512:1024], bank[6][:, :]).then_inc(sem(f"y_ready{l}"), 1)

                def step(turn_no, b):
                    i = NB * turn_no + b
                    static = isinstance(i, int)
                    dve.wait_ge(sem(f"sig_ready{l}"), i + 1)
                    if not static or i:
                        dve.wait_ge(sem(f"hid_turned{l}"), i)
                    if not static or i >= NB:
                        dve.wait_ge(sem(f"y_stored{b}_{l}"), 16 * turn_no)
                    V_.scalar_tensor_tensor(HX, bank[2][:, 0:EH], idxf[:, b, 2:3], SG, ALU.mult, ALU.mult).then_inc(sem(f"dve_turn{l}"), 1)
                    V_.tensor_copy(sidx[:, b, :], idxi[:, b, 1:2])
                    dve.wait_ge(sem(f"dve_turn{l}"), NB + 2 * i + 1)
                    tt(HX, HX, bank[2][:, EH:2 * EH], ALU.mult).then_inc(sem(f"hid_ready{l}"), 1)
                    xt_high(i + 1)
                    indices(i + NB, b)
                    hot(i + NB + 1, (b + 1) % NB)
                    if not static or i:
                        y_high(i - 1, turn_no - (0 if b else 1), (b - 1) % NB)

                for i in range(NB):
                    hot(i, i)
                    if i:
                        indices(i - 1, i - 1, False)
                indices(NB - 1, NB - 1, False)
                hot(NB, 0)
                xt_high(0)
                for i in range(2 * NB):
                    step(i // NB, i % NB)
                final = dve.value_load(tabi[0:1, NSLOT:NSLOT + 1], min_val=TURNS[0] - 1, max_val=TURNS[1] - 1)
                with dve.Fori(2, final + 1) as turn_no:
                    for b in range(NB):
                        step(turn_no, b)
                y_high(NB * final + (NB - 1), final, NB - 1)

                dve.wait_ge(sem("rows2_landed"), 64 * l + 16 * (4 if l < DEPTH - 1 else 3))
                for x, t in enumerate(tiles):
                    s = 1 - t // 2
                    dve.wait_ge(sem("rb_landed1"), 64 * l + 16 * (x + 1))
                    then(tt(FF[:, x, :], FF[:, x, :], RB[1][:, 2, :], ALU.add))
                    tt(FF[:, x, :], FF[:, x, :], RB[1][:, 3, :], ALU.add).then_inc(sem("rb_read"), 1)
                    dve.wait_ge(sem("rb_read"), 2 * TILES * l + 2 * x + 1)
                    dve.wait_ge(sem("rb_summed"), 2 * TILES * l + 2 * x + 2)
                    for y in range(2):
                        last = tt(FF[:, x, y * 512:(y + 1) * 512], FF[:, x, y * 512:(y + 1) * 512], bank[4 + 2 * (x % 2) + y][:, :], ALU.add)
                    last.then_inc(sem("rb_read"), 1)
                    dve.wait_ge(sem("rb_read"), 2 * TILES * l + 2 * x + 2)
                    then(tt(FF[:, x, :], FF[:, x, :], BV[:, s, :], ALU.mult))
                    then(V_.scalar_tensor_tensor(X[:, t, :], X[:, t, :], ALPHA, FF[:, x, :], ALU.mult, ALU.add))
                    norm_rows(l, "fin", t, X[:, t, :])
                    then(tt(X[:, t, :], X[:, t, :], BV[:, 2, :], ALU.mult))
                    tt(X[:, t, :], X[:, t, :], BV[:, 3, :], ALU.add).then_inc(sem("x_final"), 1)
                dve.wait_ge(sem("x_final"), TILES * l + nt)


_INS = ["x", "c", "ctx", "c_ctx", "w_mod", "b_mod", "w_in", "hg_lb", "hg_norm_w", "q_norm_w", "w_uq", "kv_norm_w",
        "w_ukv", "w_out", "ln1_w", "ln1_b", "router_w", "router_bias", "moe_w1", "moe_w3", "moe_w2", "shared_w1",
        "shared_w3", "shared_w2", "ln2_w", "ln2_b"]


def kernel(**inputs):
    import concourse.bacc as _bacc
    from concourse.bass_utils import run_bass_kernel_spmd as _run

    nc = _bacc.Bacc("TRN2", target_bir_lowering=False, num_devices=1)
    arrays, args = {}, {}
    given = {name: np.ascontiguousarray(inputs[name]) for name in _INS}
    given.update(constants())
    for name, a in given.items():
        a = np.ascontiguousarray(a)
        arrays[f"in_{name}"] = a
        args[name] = nc.dram_tensor(f"in_{name}", a.shape, mybir.dt.from_np(a.dtype), kind="ExternalInput").ap()
    out = nc.dram_tensor("out_0", (1, 256, D), F32, kind="ExternalOutput").ap()
    build(nc, args, out)
    return _run(nc, [arrays], core_ids=[0]).results[0]["out_0"]
```

```python
from contextlib import ExitStack

import numpy as np

import concourse.bass as bass
from concourse import mybir

ALU = mybir.AluOpType
ACT = mybir.ActivationFunctionType
AX = mybir.AxisListType
F32 = mybir.dt.float32
BF16 = mybir.dt.bfloat16
I32 = mybir.dt.int32
U8 = mybir.dt.uint8

P = 128
D = 1024
KC = D // P
DEPTH = 2
TILES = 4
HEADS = 4
HD = 128
HGW = HEADS * HD
MLA_HEADS = 8
MV = 64
NOPE = 64
ROPE = 32
QK = NOPE + ROPE
QL = 256
KVL = 128
NE = 64
TOPK = 8
EH = 256
ROUTED_SCALE = 2.5
EPS = 1e-6
ALPHA = (2 * DEPTH) ** 0.25
GRID_W = 64
ROPE_BASE = 10000.0
UC = 256
RING = 4
NLEV = 8
CHUNKS_FW = [0, 1, 2, 3]
CHUNKS_BW = [1, 0, 3, 2]
NSLOT = 104
NB = 3
NQ = 4
BLOCK = (P, P // 2)
PER_TURN = (NB, NQ)
TURNS = [(-(-NE // n), 96 // n) for n in PER_TURN]
BIG = 4096.0
MODU = 6 * D // UC
MODA = 2 * D // UC

UNITS = ([(k, p) for p in range(2) for k in ("ffw", "fbw", "q", "i", "g")]
         + [("cq", 0), ("ckv", 0), ("uq", 0), ("ukv", 0)]
         + [("out", u) for u in range(4)] + [("sw1", 0), ("sw3", 0), ("sw2", 0)])


def sequence():
    mods = lambda l, a, b: [(l, "mod", v) for v in range(a, b)]
    units = [[(l, *u) for u in UNITS] for l in range(DEPTH)]
    first, half = units[0], (MODU - MODA) // 2
    return (mods(0, 0, MODA) + first[:5] + mods(0, MODA, MODA + half) + first[5:10] + mods(0, MODA + half, MODU)
            + first[10:14] + mods(1, 0, MODU) + first[14:] + [u for layer in units[1:] for u in layer])


SEQ = sequence()


def unit_no(l, name, k=0):
    return SEQ.index((l, name, k))


def rstd_calls(l):
    tiles = range(TILES) if l < DEPTH - 1 else range(2, 4)
    return ([("a", 0)] + [("hg", 0), ("hg", 1), ("cq", 0), ("ckv", 0)]
            + [(k, t) for t in tiles for k in ("post1", "post2")] + [("fin", t) for t in tiles])


RSTD = [(l, *c) for l in range(DEPTH) for c in rstd_calls(l)]


def rstd_no(l, name, k=0):
    return RSTD.index((l, name, k)) + 1


def constants():
    s = np.arange(P)
    x = s[:, None] ^ s[None, :]
    masks = np.stack([x == 0] + [(x >= 1 << n) & (x < 2 << n) for n in range(6, -1, -1)], 1)
    pos = np.arange(256)
    n_freq = ROPE // 4
    inv = ROPE_BASE ** (-np.arange(n_freq, dtype=np.float32) / n_freq)
    ang = np.concatenate([(pos // GRID_W)[:, None] * inv, (pos % GRID_W)[:, None] * inv], -1).T.astype(np.float32)
    cs = np.stack([np.concatenate([np.cos(ang)] * 2), np.concatenate([np.sin(ang)] * 2)], 1)
    swap = np.zeros((ROPE, ROPE), np.float32)
    for i in range(ROPE // 2):
        swap[i + ROPE // 2, i] = -1.0
        swap[i, i + ROPE // 2] = 1.0
    ident = np.eye(P, dtype=np.float32)
    iota = np.broadcast_to(s.astype(np.float32), (P, P)).copy()
    scan = np.ones((P, 1024), np.float32)
    scan[:, ::P] = 0.0
    vals = np.zeros((P, TILES, 1, 12), np.float32)
    for t in range(TILES):
        vals[:, t, 0, 0] = s
        vals[:, t, 0, 1] = P * t
        vals[:, t, 0, 2] = -BIG
        vals[:, t, 0, 4] = TOPK * s
        vals[:, t, 0, 5] = TOPK * P * t
        vals[:, t, 0, 6] = -BIG * TOPK
    tab = np.zeros((P, NSLOT), np.float32)
    tab[:, :NE] = np.arange(NE)
    slot = np.broadcast_to(np.arange(NSLOT - NE, dtype=np.float32), (P, NSLOT - NE)).copy()
    big = np.broadcast_to(np.array([BIG, BIG * TOPK], np.float32), (P, 2)).copy()
    return dict(k_masks=masks.astype(np.float32).reshape(P, NLEV * P), k_cs=cs.astype(np.float32),
                k_swap=swap, k_ident=ident, k_iota=iota, k_scan=scan, k_vals=vals[:, :, 0],
                k_tri=(s[:, None] < s[None, :]).astype(np.float32), k_tab=tab, k_slot=slot, k_big=big)


def build(nc, A, out):
    with ExitStack() as ctx:
        ctx.enter_context(nc.allow_non_contiguous_dma(reason="small parameter columns"))

        def sb(name, shape, dt=F32):
            return ctx.enter_context(nc.sbuf_tensor(name, shape, dt))

        sems = {}

        def sem(name):
            if name not in sems:
                sems[name] = ctx.enter_context(nc.semaphore(name))
            return sems[name]

        mod_dram = nc.dram_tensor("mod_dram", (2, DEPTH * 6 * D), F32, kind="Internal").ap()
        h_dram = [nc.dram_tensor(f"h_dram{l}", (TILES * P, D), F32, kind="Internal").ap() for l in range(DEPTH)]
        y_dram = [nc.dram_tensor(f"y_dram{l}", (TILES * P * TOPK, D), F32, kind="Internal").ap() for l in range(DEPTH)]

        X = sb("X", [P, TILES, D])
        hT = sb("hT", [P, KC, TILES * P])
        ring = sb("ring", [P, RING, KC * UC])
        EW0 = sb("EW0", [P, 3 * KC * EH])
        UF = 26112
        U = sb("U", [P, UF])
        masks = sb("masks", [P, NLEV * P], U8)
        cs = sb("cs", [P, 2, 256])
        swap = sb("swap", [P, ROPE])
        ident = sb("ident", [P, P])
        iota = sb("iota", [P, P])
        trif = sb("trif", [P, P])
        tri = sb("tri", [P, P], BF16)
        ones = sb("ones", [P, P], BF16)
        slotno = sb("slotno", [P, NSLOT - NE])
        bigc = sb("bigc", [P, 2])
        half = sb("half", [P, 8])
        rin = sb("rin", [P, 8])
        rout = sb("rout", [P, 8])
        ccol = sb("ccol", [P, 2, KC])
        csil = sb("csil", [P, KC, 32])
        modcol = sb("modcol", [P, 2, 2, KC])
        lbc = sb("lbc", [P, DEPTH, 8])
        lbt = sb("lbt", [P, 3, 8])
        lb = sb("lb", [P, DEPTH, 8])
        oml = sb("oml", [P, DEPTH, 8])
        hgw = sb("hgw", [P, DEPTH, HD])
        qnw = sb("qnw", [P, DEPTH, 2])
        kvw = sb("kvw", [P, DEPTH])
        rbias = sb("rbias", [P, DEPTH, NE])
        rw = sb("rw", [P, DEPTH, KC, NE])
        stats = sb("stats", [P, TILES, 2, 6])
        mv = sb("mv", [P, TILES, 2])
        el = sb("el", [P, 2, 8])
        amax = sb("amax", [P, 2, 2])
        nmax = sb("nmax", [P, 2, 2])
        asum = sb("asum", [P, 2, 2])
        ainv = sb("ainv", [P, 2, 2])
        selb = sb("selb", [P, TILES, NE], BF16)
        posm = sb("posm", [P, TILES, NE])
        top8 = sb("top8", [P, TILES, 8])
        gsum = sb("gsum", [P, TILES, 2])
        csig = sb("csig", [P, 2, KC])
        ssq = sb("ssq", [P, 8])
        kv = sb("kv", [P, TILES, 12])
        exb = sb("exb", [P, NSLOT - NE])
        cnt = sb("cnt", [P, NE])
        over = sb("over", [P, NE])
        icum = sb("icum", [P, NE])
        onesf = sb("onesf", [P, NE])
        tabf = sb("tabf", [P, NSLOT])
        tabi = sb("tabi", [P, NSLOT + 4], I32)
        noff = sb("noff", [P, NSLOT])
        nturn = sb("nturn", [P, 2])
        idxf = sb("idxf", [P, NB, 3])
        idxi = sb("idxi", [P, NB, 2], I32)
        sidx = sb("sidx", [P, NB, 1], I32)

        def u(a, *shape):
            n = int(np.prod(shape))
            v = U[:, a:a + n]
            if len(shape) == 2:
                v = v.rearrange("p (a b) -> p a b", b=shape[1])
            if len(shape) == 3:
                v = v.rearrange("p (a b c) -> p a b c", b=shape[1], c=shape[2])
            return v

        maskf = U[:, 0:NLEV * P]
        MR = EW0[:, 0:DEPTH * MODU * 64].rearrange("p (n c) -> p n c", c=64)
        mixT = u(0, KC, 512)
        a0 = 4096
        XH = u(a0 + 5120, 2, 1024)
        KR = u(a0 + 21504, 512)[NOPE:QK]
        KPR = u(a0 + 20992, 512)[NOPE:QK]
        kk = [u(a0, 1024), u(a0 + 1024, 1024)]
        bb = [u(a0 + 2048, 1024), u(a0 + 3072, 1024)]
        qq = u(a0 + 4096, 1024)
        EA = [u(a0 + 5120 + 2048 * n, 1024) for n in range(3)]
        EB = [u(a0 + 6144 + 2048 * n, 1024) for n in range(3)]
        QE = [u(a0 + 11264, 1024), u(a0 + 12288, 1024)]
        KDT = [u(a0 + 13312, 1024), u(a0 + 14336, 1024)]
        ST = u(a0 + 15360, 2, 512)
        SS = u(a0 + 16384, 12, 128)
        V = u(a0 + 17920, TILES, 256)
        G = u(a0 + 18944, TILES, 256)
        OT = u(a0 + 19968, TILES, 256)
        scanm = u(a0 + 20992, 1024)
        cqn = u(a0, TILES, QL)
        ckvn = u(a0 + 1024, TILES, KVL)
        cqT = u(a0 + 1536, 2, 512)
        ckvT = u(a0 + 2560, 512)
        qraw = u(a0 + 3072, MLA_HEADS, 512)
        qrot = u(a0 + 7168, MLA_HEADS, 256)
        qsw = u(a0 + 9216, MLA_HEADS * 256)
        kT = u(a0 + 11264, MLA_HEADS, 512)
        VM = u(a0 + 15360, TILES, 512)
        PR = u(a0 + 17408, 2, 2, 512)
        PTT = [u(a0 + 19456, 4, 256), u(a0 + 9216, 4, 256)]
        BV = u(a0, 8, 1024)
        H = u(a0 + 8192, 2, 1024)
        XG = u(a0 + 9216, NB, 1024)
        XT = u(a0 + 12288, 1024)
        GT = u(a0 + 12288, 2, UC)
        vals = U[:, a0 + 14336:a0 + 15872].bitcast(BF16).rearrange("p (t e k) -> p t e k", t=TILES, k=12)
        Y = [u(a0 + 4096, 1024), u(a0 + 5120, 1024), u(a0 + 13312, 1024)]
        HID = u(a0 + 6656, 2, 256)
        HIDT = u(a0 + 7168, 2, 256)
        HX = u(a0 + 6656, 256)
        HXT = u(a0 + 6912, 256)
        PH = U[:, a0 + 7168:a0 + 7936].bitcast(BF16).rearrange("p (b t j) -> p b t j", b=NB, j=P)
        SG = u(a0 + 7936, 256)
        FF = u(0, TILES, D)
        RB = [u(a0 + 8192, 4, 1024), u(UF - 6144, 4, 1024)]
        EW = [EW0[:, :], U[:, UF - 6144:UF], ring[:, 0:3, :].rearrange("p a b -> p (a b)")]
        UPB = [w[:, 0:4096] for w in EW] + [hT[:, :, :].rearrange("p a b -> p (a b)")]
        DOWNB = [w[:, 4096:6144] for w in EW] + [ring[:, 3, :]]
        W13 = [w.rearrange("p (m c n) -> p m c n", m=2, c=KC) for w in UPB]
        W2 = [w.rearrange("p (c n) -> p c n", c=2) for w in DOWNB]
        cmpb = u(a0 + 4096, NSLOT - NE, NE)
        CW = u(a0 + 13568, TILES, NE)
        HOT = [u(a0 + 10240 + 256 * n, 2, P) for n in range(2)]
        TOK = [u(a0 + 10752 + 256 * n, 2, P) for n in range(2)]
        sco, bia, rep, sel, kth = (u(a0 + 12288 + 256 * n, TILES, NE) for n in range(5))

        bank = [ctx.enter_context(nc.psum_tensor(f"bank{n}", [P, 512], F32)) for n in range(8)]

        def bk(n, *shape):
            v = bank[n][:, :]
            if len(shape) == 2:
                return v[:, 0:shape[0] * shape[1]].rearrange("p (a b) -> p a b", b=shape[1])
            return v

        def seg_head(a, j):
            return a.rearrange("p (s j t) -> p s j t", s=2, j=2)[:, :, j, :]

        def tiles_of(l):
            return list(range(TILES)) if l < DEPTH - 1 else [2, 3]

        def segs_of(l):
            return [0, 1] if l < DEPTH - 1 else [1]

        def unit(n):
            return ring[:, n % RING, :]

        def unit_landed(eng, n):
            eng.wait_ge(sem(f"ring_landed{n % RING}"), 16 * (n // RING + 1))

        def nparts(l, name):
            nt, ns = len(tiles_of(l)), len(segs_of(l))
            return dict(ffw=2, fbw=2, q=2, i=2, g=ns, cq=ns, ckv=2, uq=MLA_HEADS, ukv=MLA_HEADS + TILES,
                        out=nt, sw1=1, sw3=nt, sw2=nt)[name]

        def part_base(l, name, k):
            done = 0
            for ll in range(DEPTH):
                for nm, kk_ in UNITS:
                    if (ll, nm, kk_) == (l, name, k):
                        return done
                    done += nparts(ll, nm) - 1

        def part_done(ins, l, name, k, n):
            ins.then_inc(sem("unit_done" if n == nparts(l, name) - 1 else "part_done"), 1)

        def wait_part(eng, l, name, k, n):
            if n == nparts(l, name) - 1:
                eng.wait_ge(sem("unit_done"), unit_no(l, name, k) + 1)
            elif name == "out":
                eng.wait_ge(sem("part_done"), part_base(l, name, 0) + 4 * n + k + 1)
            else:
                eng.wait_ge(sem("part_done"), part_base(l, name, k) + n + 1)

        items = [[(h, x) for h in range(MLA_HEADS) for x in ((1, 0) if l < DEPTH - 1 else (1,))] for l in range(DEPTH)]
        item0 = [0, len(items[0])]

        small = [(maskf, A["k_masks"]), (cs[NOPE:QK, :, :], A["k_cs"]), (swap[NOPE:QK, :], A["k_swap"]),
                 (iota[:, :], A["k_iota"]), (trif[:, :], A["k_tri"]), (slotno[:, :], A["k_slot"]), (bigc[:, :], A["k_big"]),
                 (tabf[:, :], A["k_tab"]), (kv[:, :, :], A["k_vals"])]
        for l_ in range(DEPTH):
            small += [(lbc[:, l_, :], A["hg_lb"][l_].rearrange("(n p) -> p n", p=P)),
                      (hgw[:, l_, :], A["hg_norm_w"][l_].partition_broadcast(P)),
                      (qnw[:, l_, :], A["q_norm_w"][l_].rearrange("(n p) -> p n", p=P)),
                      (kvw[:, l_:l_ + 1], A["kv_norm_w"][l_].rearrange("(p n) -> p n", n=1)),
                      (rbias[:, l_, :], A["router_bias"][l_].partition_broadcast(P)),
                      (rw[:, l_, :, :], A["router_w"][l_].rearrange("(p c) n -> p c n", c=KC))]

        def expert_src(w, e):
            return w[e].rearrange("(p c) n -> p (c n)", p=P)

        def store_mod(eng, a, b, done="mod_stored"):
            eng.wait_ge(sem("mod_added"), b)
            for j in range(4):
                eng.dma_start(mod_dram.rearrange("s (n j c) -> s n j c", j=4, c=64)[:, a:b, j, :],
                              MR[32 * j:32 * j + 2, a:b, :]).then_inc(sem(done), 16)

        def mod_row(l, part, s):
            return mod_dram[s:s + 1, (l * 6 + part) * D:(l * 6 + part + 1) * D]

        def load_modcol(eng, l):
            for s in range(2):
                for part in range(2):
                    eng.dma_start(modcol[:, s, part, :], mod_row(l, part, s).rearrange("a (p c) -> (a p) c", c=KC)).then_inc(sem(f"modcol_landed{l}"), 16)

        block = ctx.enter_context(nc.Block())

        @block.sync
        def _(sp):
            sp.dma_start(ident[:, :], A["k_ident"]).then_inc(sem("ident_landed"), 16)
            sp.dma_start(ccol[:, 0, :], A["c"][0].rearrange("(p c) -> p c", p=P)).then_inc(sem("c_landed"), 16)
            sp.dma_start(ccol[:, 1, :], A["c_ctx"].rearrange("(p c) -> p c", p=P)).then_inc(sem("c_landed"), 16)

            def load_unit(n, dst, src):
                if n >= RING:
                    sp.wait_ge(sem("unit_done"), n - RING + 1)
                sp.dma_start(dst, src).then_inc(sem(f"ring_landed{n % RING}"), 16)

            def cols(n, w, a, m, pat="(p c) n -> p c n"):
                load_unit(n, unit(n)[:, 0:KC * m].rearrange("p (c n) -> p c n", n=m),
                          w[:, a:a + m].rearrange(pat, p=P, c=KC))

            def load_mods(l, a, b):
                for v in range(a, b):
                    cols(unit_no(l, "mod", v), A["w_mod"][l], v * UC, UC)

            load_mods(0, 0, RING)
            for t in range(TILES):
                src = A["ctx"][0] if t < 2 else A["x"][0]
                sp.dma_start(X[:, t, :], src[(t % 2) * P:(t % 2 + 1) * P, :]).then_inc(sem("x_landed"), 16)
            load_mods(0, RING, MODA)
            for l in range(DEPTH):
                w_in = A["w_in"][l]
                start = dict(ffw=0, fbw=HGW, i=2 * HGW, q=3 * HGW, g=4 * HGW)
                for name, k in UNITS:
                    n = unit_no(l, name, k)
                    if l == 0 and (name, k) in (("ffw", 1), ("cq", 0)):
                        half = (MODU - MODA) // 2
                        load_mods(0, MODA + half * (name == "cq"), MODA + half + half * (name == "cq"))
                    if l == 0 and (name, k) == ("out", 0):
                        load_mods(1, 0, MODU)
                    if name in start:
                        cols(n, w_in, start[name] + k * UC, UC)
                    elif name == "cq":
                        cols(n, w_in, 5 * HGW, QL)
                    elif name == "ckv":
                        cols(n, w_in, 5 * HGW + QL, KVL + ROPE)
                    elif name == "uq":
                        load_unit(n, unit(n)[:, 0:2 * MLA_HEADS * QK].rearrange("p (c n) -> p c n", c=2),
                                  A["w_uq"][l].rearrange("(c p) n -> p c n", p=P))
                    elif name == "ukv":
                        load_unit(n, unit(n)[:, 0:MLA_HEADS * P], A["w_ukv"][l])
                    elif name == "out":
                        cols(n, A["w_out"][l], k * UC, UC, "(c p) n -> p c n")
                    elif name in ("sw1", "sw3"):
                        cols(n, A["shared_w1" if name == "sw1" else "shared_w3"][l], 0, UC)
                    else:
                        load_unit(n, unit(n).rearrange("p (c n) -> p c n", c=2),
                                  A["shared_w2"][l].rearrange("(p c) n -> p c n", c=2))
                w1, w3, w2 = A["moe_w1"][l], A["moe_w3"][l], A["moe_w2"][l]

                def load_expert(b, e):
                    sp.dma_start(UPB[b][:, 0:2048], expert_src(w1, e)).then_inc(sem(f"w13_landed{b}_{l}"), 16)
                    sp.dma_start(UPB[b][:, 2048:4096], expert_src(w3, e)).then_inc(sem(f"w13_landed{b}_{l}"), 16)

                def load_down(b, e):
                    sp.dma_start(DOWNB[b], expert_src(w2, e)).then_inc(sem(f"w2_landed{b}_{l}"), 16)

                if l == 0:
                    sp.wait_ge(sem("mod_stored"), 2 * 64)
                load_expert(0, 0)
                load_down(0, 0)
                sp.wait_ge(sem("attn_out"), item0[l] + len(items[l]))
                load_expert(1, 1)
                load_down(1, 1)
                sp.wait_ge(sem("unit_done"), unit_no(l, *UNITS[-1]) + 1)
                load_expert(2, 2)
                load_down(2, 2)

                def load_up_of(b, e):
                    sp.dma_start(UPB[b][:, 0:2048], w1[bass.ds(e, 1)].rearrange("e (p c) n -> p (e c n)", p=P)).then_inc(sem(f"w13_landed{b}_{l}"), 16)
                    sp.dma_start(UPB[b][:, 2048:4096], w3[bass.ds(e, 1)].rearrange("e (p c) n -> p (e c n)", p=P)).then_inc(sem(f"w13_landed{b}_{l}"), 16)

                def load_down_of(b, e):
                    sp.dma_start(DOWNB[b], w2[bass.ds(e, 1)].rearrange("e (p c) n -> p (e c n)", p=P)).then_inc(sem(f"w2_landed{b}_{l}"), 16)

                def number(i):
                    return sp.value_load(tabi[0:1, bass.ds(i, 1)], min_val=0, max_val=NE - 1)

                if l < DEPTH - 1:
                    for e in range(NB, 2 * NB):
                        sp.wait_ge(sem(f"up_done{l}"), e - NB + 1)
                        load_expert(e % NB, e)
                        sp.wait_ge(sem(f"down_done{l}"), e - NB + 1)
                        load_down(e % NB, e)
                else:
                    load_expert(3, 3)
                    load_down(3, 3)
                sp.wait_ge(sem("table_ready"), l + 1)
                final = sp.value_load(tabi[0:1, NSLOT:NSLOT + 1], min_val=TURNS[l][0] - 1, max_val=TURNS[l][1] - 1)
                if l < DEPTH - 1:
                    with sp.Fori(2, final + 1) as turn_no:
                        for b in range(NB):
                            e = number(NB * turn_no + b)
                            sp.wait_ge(sem(f"up_done{l}"), NB * turn_no + (b - NB + 1))
                            load_up_of(b, e)
                            sp.wait_ge(sem(f"down_done{l}"), NB * turn_no + (b - NB + 1))
                            load_down_of(b, e)
                    sp.wait_ge(sem(f"down_done{l}"), NB * final + NB)
                else:
                    with sp.Fori(1, final + 1) as turn_no:
                        for b in range(2):
                            ea, eb = number(NQ * turn_no + 2 * b), number(NQ * turn_no + 2 * b + 1)
                            sp.wait_ge(sem(f"up_done{l}"), 2 * turn_no + b - 1)
                            load_up_of(2 * b, ea)
                            load_up_of(2 * b + 1, eb)
                            sp.wait_ge(sem(f"down_done{l}"), 2 * turn_no + b - 1)
                            load_down_of(2 * b, ea)
                            load_down_of(2 * b + 1, eb)

            for x in range(2):
                sp.wait_ge(sem("x_final"), TILES * (DEPTH - 1) + x + 1)
                sp.dma_start(out[0, x * P:(x + 1) * P, :], X[:, 2 + x, :]).then_inc(sem("out_stored"), 16)
            sp.wait_ge(sem("out_stored"), 32)

        @block.gpsimd
        def _(gp):
            gp.memset(half[:, :], -0.5).then_inc(sem("pool_set"), 1)
            gp.memset(rin[:, :], 1.0).then_inc(sem("pool_set"), 1)
            gp.memset(ones[:, :], 1.0).then_inc(sem("pool_set"), 1)
            gp.memset(onesf[:, :], 1.0).then_inc(sem("pool_set"), 1)
            gp.memset(MR, 0.0).then_inc(sem("mr_clear"), 1)
            gp.wait_ge(sem("mr_clear"), 1)
            for j in range(4):
                gp.dma_start(MR[32 * j:32 * j + 2, :, :], A["b_mod"].rearrange("l (v j c) -> j (l v) c", j=4, c=64)[j].partition_broadcast(2)
                             ).then_inc(sem("bmod_landed"), 16)

            def rstd(l, name, k=0):
                n = rstd_no(l, name, k)
                gp.wait_ge(sem("var_ready"), n)
                gp.tensor_tensor(rout[:, :], rin[:, :], half[:, :], ALU.pow).then_inc(sem("rstd_ready"), 1)

            for l in range(DEPTH):
                tiles = tiles_of(l)
                streams = [0, 1] if l < DEPTH - 1 else [0]
                if l:
                    gp.wait_ge(sem("h_ready"), TILES * l)
                gp.dma_start(scanm, A["k_scan"]).then_inc(sem("scan_landed"), 16) if l == 0 else None
                if l:
                    gp.wait_ge(sem("mod_stored"), 2 * 64)
                    load_modcol(gp, l)
                if l:
                    gp.wait_ge(sem("x_final"), TILES * l)
                    gp.dma_start(scanm, A["k_scan"]).then_inc(sem("scan_landed"), 16)
                rstd(l, "a")
                rstd(l, "hg", 0)
                rstd(l, "hg", 1)
                rstd(l, "cq")
                rstd(l, "ckv")
                if l == 0:
                    store_mod(gp, MODA, MODU)
                    gp.wait_ge(sem("mod_stored"), 64)
                gp.wait_ge(sem("attn_out"), item0[l] + len(items[l]))
                for row, src in [(2, A["ln1_w"][l:l + 1]), (3, A["ln1_b"][l:l + 1])]:
                    gp.dma_start(BV[:, row, :], src.rearrange("a n -> (a n)").partition_broadcast(P)).then_inc(sem("rows1_landed"), 16)
                for s in streams:
                    for row, part in [(0 + s, 2), (4 + s, 3), (6 + s, 4)]:
                        gp.dma_start(BV[:, row, :], mod_row(l, part, s).rearrange("a n -> (a n)").partition_broadcast(P)).then_inc(sem("rows1_landed"), 16)
                if l == 0:
                    store_mod(gp, MODU, DEPTH * MODU)
                for n, t in enumerate(tiles):
                    rstd(l, "post1", t)
                    rstd(l, "post2", t)
                    gp.wait_ge(sem("h_ready"), TILES * l + n + 1)
                    if l < DEPTH - 1:
                        gp.dma_start(h_dram[l][n * P:(n + 1) * P, :], H[:, n % 2, :]).then_inc(sem(f"h_stored{n % 2}"), 16)
                if l < DEPTH - 1:
                    gp.wait_ge(sem("h_stored0"), 32 * l + 16 * (len(tiles) // 2))
                    gp.wait_ge(sem("h_stored1"), 32 * l + 16 * (len(tiles) // 2))
                for row, src in [(2, A["ln2_w"][l:l + 1]), (3, A["ln2_b"][l:l + 1])]:
                    gp.dma_start(BV[:, row, :], src.rearrange("a n -> (a n)").partition_broadcast(P)).then_inc(sem("rows2_landed"), 16)
                for s in streams:
                    gp.dma_start(BV[:, s, :], mod_row(l, 5, s).rearrange("a n -> (a n)").partition_broadcast(P)).then_inc(sem("rows2_landed"), 16)
                if l == DEPTH - 1:
                    for t in tiles:
                        rstd(l, "fin", t)
                    break
                rows = P * len(tiles)

                def take_waits():
                    gp.sem_inc(sem("pool_turn"), 1)

                def gather(i, b):
                    gp.wait_ge(sem(f"idx_ready{l}"), i + 1)
                    if not isinstance(i, int) or i >= NB:
                        gp.wait_ge(sem(f"xg_turned{l}"), i - (NB - 1))
                    take_waits()
                    gp.indirect_dma_start(out=XG[:, b, :], out_offset=None, in_=h_dram[l][0:rows, :],
                                          in_offset=bass.IndirectOffsetOnAxis(ap=idxi[:, b, 0:1], axis=0),
                                          bounds_check=rows - 1, oob_is_err=False,
                                          compute_op=ALU.bypass).then_inc(sem(f"xg_landed{b}_{l}"), 16)

                def scatter(i, b):
                    gp.wait_ge(sem(f"y_ready{l}"), 2 * i + 2)
                    take_waits()
                    gp.indirect_dma_start(out=y_dram[l][0:rows * TOPK, :],
                                          out_offset=bass.IndirectOffsetOnAxis(ap=sidx[:, b, 0:1], axis=0),
                                          in_=Y[b], in_offset=None,
                                          bounds_check=rows * TOPK - 1, oob_is_err=False,
                                          compute_op=ALU.bypass).then_inc(sem(f"y_stored{b}_{l}"), 16)

                gp.wait_ge(sem("h_turned"), TILES * l + len(tiles))
                gp.memset(XG[:, :, :], 0.0).then_inc(sem("pool_set"), 1)
                gp.wait_ge(sem("pool_set"), l + 5)
                gp.wait_ge(sem("table_ready"), l + 1)
                final = gp.value_load(tabi[0:1, NSLOT:NSLOT + 1], min_val=TURNS[l][0] - 1, max_val=TURNS[l][1] - 1)
                for i in range(NB):
                    gather(i, i)
                for i in range(2 * NB):
                    gather(i + NB, i % NB)
                    if i:
                        scatter(i - 1, (i - 1) % NB)
                with gp.Fori(2, final + 1) as turn_no:
                    for b in range(NB):
                        i = NB * turn_no + b
                        gather(i + NB, b)
                        scatter(i - 1, (b - 1) % NB)
                scatter(NB * final + (NB - 1), NB - 1)
                for b in range(NB):
                    gp.wait_ge(sem(f"y_stored{b}_{l}"), 16 * (final + 1))
                for b in range(NB):
                    gp.wait_ge(sem(f"xg_landed{b}_{l}"), 16 * (final + 2))
                gp.wait_ge(sem(f"xg_turned{l}"), NB * final + (NB + 1))
                take_waits()
                for n, t in enumerate(tiles):
                    for k in range(2):
                        if n:
                            gp.wait_ge(sem("rb_summed"), 2 * TILES * l + 2 * (n - 1) + k + 1)
                            if k:
                                gp.wait_ge(sem("rb_read"), 2 * TILES * l + 2 * n - 1)
                        gp.dma_start(RB[k].rearrange("p k d -> p (k d)"),
                                     y_dram[l][n * P * TOPK:(n + 1) * P * TOPK, :].rearrange("(p k) d -> p k d", k=TOPK)[:, 4 * k:4 * k + 4, :].rearrange("p k d -> p (k d)")
                                     ).then_inc(sem(f"rb_landed{k}"), 16)
                    if n:
                        rstd(l, "fin", tiles[n - 1])
                rstd(l, "fin", tiles[-1])

        @block.tensor
        def _(pe):
            def mm(o, lhsT, rhs, start=True, stop=True):
                return nc.tensor.matmul(o, lhsT, rhs, start=start, stop=stop)

            pe.wait_ge(sem("dve_start"), 1)

            def modulation(l, v):
                n, done = unit_no(l, "mod", v), l * MODU + v
                unit_landed(pe, n)
                if done:
                    pe.wait_ge(sem("mod_added"), done)
                for c in range(KC):
                    for j in range(4):
                        last = mm(bank[7][32 * j:32 * j + 32, 0:64], csil[:, c, :], unit(n)[:, c * UC + 64 * j:c * UC + 64 * j + 64], c == 0, c == KC - 1)
                last.then_inc(sem("unit_done"), 1)

            for v in range(MODA):
                modulation(0, v)
            pe.wait_ge(sem("ident_landed"), 16)

            def turn(src, b0):
                for c in range(KC):
                    last = nc.tensor.transpose(bank[b0 + c // 4][:, (c % 4) * P:(c % 4 + 1) * P], src[:, c::KC], ident[:, :])
                return last

            for l in range(DEPTH):
                tiles, segs = tiles_of(l), segs_of(l)
                nt = len(tiles)
                x0 = tiles[0] * P

                for t in range(TILES):
                    pe.wait_ge(sem("xh_ready"), TILES * l + t + 1)
                    if t >= 2:
                        pe.wait_ge(sem("ht_low"), TILES * l + t - 1)
                        pe.wait_ge(sem("ht_high"), TILES * l + t - 1)
                    turn(XH[:, t % 2, :], 2 * (t % 2)).then_inc(sem("xh_turned"), 1)
                pe.wait_ge(sem("ht_low"), TILES * l + TILES)
                pe.wait_ge(sem("ht_high"), TILES * l + TILES)

                def feature_major(name, k, b0, t0):
                    n = unit_no(l, name, k)
                    unit_landed(pe, n)
                    for j in range(2):
                        for c in range(KC):
                            last = mm(bank[b0 + j][:, t0:512], unit(n)[:, c * UC + j * P:c * UC + (j + 1) * P],
                                      hT[:, c, t0:512], c == 0, c == KC - 1)
                        part_done(last, l, name, k, j)

                def token_major(name, k, b0, ts, part=0, w=UC, m=UC, each=2):
                    n = unit_no(l, name, k)
                    unit_landed(pe, n)
                    for x, t in enumerate(ts):
                        for c in range(KC):
                            last = mm(bank[b0 + t // each][:, (t % each) * m:(t % each + 1) * m],
                                      hT[:, c, t * P:(t + 1) * P], unit(n)[:, c * w:c * w + m], c == 0, c == KC - 1)
                        if t % each == each - 1:
                            part_done(last, l, name, k, part)
                            part += 1

                for p in range(2):
                    cp = 2 * l + p
                    if cp % 2:
                        pe.wait_ge(sem("ot_ready"), cp)
                        pe.wait_ge(sem("mix_ready"), cp)
                    if cp == 0:
                        pe.wait_ge(sem("small_landed"), 16 * len(small))
                    feature_major("ffw", p, 0, 0)
                    feature_major("fbw", p, 2, 0)
                    if cp:
                        pe.wait_ge(sem("lvl_used"), NLEV * cp)
                        pe.wait_ge(sem("attn_out"), item0[l])
                    feature_major("q", p, 4, x0)
                    if cp == 1:
                        pe.wait_ge(sem("mod_added"), MODA + (MODU - MODA) // 2)
                    token_major("i", p, 6, range(TILES))
                    pe.wait_ge(sem("f_sig"), 4 * cp + 2)
                    token_major("g", p, 0, tiles)
                    pe.wait_ge(sem("v_ready"), 2 * cp + 2)
                    for d in range(2):
                        b0 = 6 if d == 0 else 0
                        pe.wait_ge(sem("kd_ready"), 2 * cp + d + 1)
                        if d:
                            pe.wait_ge(sem("g_used"), cp + 1)
                        for blk in range(8):
                            last = nc.tensor.transpose(bank[b0 + blk // 4][:, (blk % 4) * P:(blk % 4 + 1) * P],
                                                       EA[0][:, blk * P:(blk + 1) * P] if d == 0 else EB[0][:, blk * P:(blk + 1) * P],
                                                       ident[:, :])
                        last.then_inc(sem("kd_turned"), 1)
                    pe.wait_ge(sem("kdt_ready"), 4 * cp + 4)
                    for k in range(3):
                        if k == 2:
                            pe.wait_ge(sem("state_ready"), 3 * cp + 1)
                        for d, order in enumerate((CHUNKS_FW, CHUNKS_BW)):
                            for j in range(2):
                                ch = order[k]
                                blk = (ch // 2) * 4 + j * 2 + ch % 2
                                last = mm(bank[6 + k % 2][:, (2 * d + j) * P:(2 * d + j + 1) * P],
                                          KDT[d][:, blk * P:(blk + 1) * P], V[:, ch, j * P:(j + 1) * P])
                        last.then_inc(sem("state_sum"), 1)
                    pe.wait_ge(sem("f_sig"), 4 * cp + 4)
                    pe.wait_ge(sem("q_ready"), cp + 1)
                    for n in range(NLEV):
                        pe.wait_ge(sem("lvl_ready"), NLEV * cp + n + 1)
                        if n >= 2:
                            pe.wait_ge(sem("lvl_used"), NLEV * cp + n - 1)
                        for s in segs:
                            for j in range(2):
                                for c in range(2):
                                    blk = s * 4 + j * 2 + c
                                    last = mm(bank[2 + 2 * (n % 2) + s][:, (j * 2 + c) * P:(j * 2 + c + 1) * P],
                                              EB[n % 3][:, blk * P:(blk + 1) * P],
                                              (EA[n % 3] if n else qq)[:, blk * P:(blk + 1) * P])
                        last.then_inc(sem("lvl_done"), 1)
                        if l == 0:
                            pe.wait_ge(sem("state_ready"), 3 * cp + 3)
                            modulation(0, MODA + p * NLEV + n)
                    pe.wait_ge(sem("lvl_used"), NLEV * (cp + 1))
                    pe.wait_ge(sem("state_ready"), 3 * cp + 3)
                    pe.wait_ge(sem("qe_ready"), cp + 1)
                    for s in segs:
                        for c in range(2):
                            for j in range(2):
                                ch = 2 * s + c
                                blk = s * 4 + j * 2 + c
                                o = bank[s][:, (c * 2 + j) * P:(c * 2 + j + 1) * P]
                                parts = [(ST[:, s, (j * 2 + c) * P:(j * 2 + c + 1) * P], V[:, ch, j * P:(j + 1) * P])]
                                for d, order in enumerate((CHUNKS_FW, CHUNKS_BW)):
                                    at = order.index(ch)
                                    if at:
                                        parts.append((QE[d][:, blk * P:(blk + 1) * P], SS[:, (d * 2 + j) * 3 + at - 1, :]))
                                for a, (x, y) in enumerate(parts):
                                    last = mm(o, x, y, a == 0, a == len(parts) - 1)
                    last.then_inc(sem("o_done"), 1)
                    pe.wait_ge(sem("ot_ready"), cp + 1)
                    for j in range(2):
                        for t in tiles:
                            last = nc.tensor.transpose(bank[2 + j][:, t * P:(t + 1) * P], OT[:, t, j * P:(j + 1) * P], ident[:, :])
                    last.then_inc(sem("ot_turned"), 1)

                pe.wait_ge(sem("ot_ready"), 2 * l + 2)
                token_major("cq", 0, 0, tiles)
                n = unit_no(l, "ckv")
                unit_landed(pe, n)
                w = KVL + ROPE
                for t in range(TILES):
                    for c in range(KC):
                        last = mm(bank[4][:, t * KVL:(t + 1) * KVL], hT[:, c, t * P:(t + 1) * P],
                                  unit(n)[:, c * w:c * w + KVL], c == 0, c == KC - 1)
                part_done(last, l, "ckv", 0, 0)
                for c in range(KC):
                    last = mm(bank[5][NOPE:QK, :], unit(n)[:, c * w + KVL:(c + 1) * w], hT[:, c, :], c == 0, c == KC - 1)
                part_done(last, l, "ckv", 0, 1)
                pe.wait_ge(sem("mix_ready"), 2 * l + 2)
                pe.wait_ge(sem("cqn_ready"), l + 1)
                for c in range(2):
                    for t in tiles:
                        last = nc.tensor.transpose(bank[2 + c][:, t * P:(t + 1) * P], cqn[:, t, c * P:(c + 1) * P], ident[:, :])
                last.then_inc(sem("cq_turned"), 1)
                pe.wait_ge(sem("ckvn_ready"), l + 1)
                for t in range(TILES):
                    last = nc.tensor.transpose(bank[6][:, t * P:(t + 1) * P], ckvn[:, t, :], ident[:, :])
                last.then_inc(sem("ckv_turned"), 1)
                pe.wait_ge(sem("cqt_ready"), 2 * l + 2)
                pe.wait_ge(sem("ckvt_ready"), l + 1)
                n = unit_no(l, "uq")
                unit_landed(pe, n)
                for h in range(MLA_HEADS):
                    if h >= 2:
                        pe.wait_ge(sem("qraw_ready"), MLA_HEADS * l + h - 1)
                    for c in range(2):
                        last = mm(bank[h % 2][0:QK, x0:512], unit(n)[:, c * MLA_HEADS * QK + h * QK:c * MLA_HEADS * QK + (h + 1) * QK],
                                  cqT[:, c, x0:512], c == 0, c == 1)
                    part_done(last, l, "uq", 0, h)
                n = unit_no(l, "ukv")
                unit_landed(pe, n)
                pe.wait_ge(sem("kpr_ready"), l + 1)
                for h in range(MLA_HEADS):
                    if h >= 2:
                        pe.wait_ge(sem("kt_ready"), MLA_HEADS * l + h - 1)
                    last = mm(bank[4 + h % 2][0:NOPE, :], unit(n)[:, h * P:h * P + NOPE], ckvT)
                    part_done(last, l, "ukv", 0, h)
                if l == 0:
                    pe.wait_ge(sem("mod_added"), MODU)
                wv = unit(n)[:, 0:MLA_HEADS * P].rearrange("p (h x) -> p h x", x=P)[:, :, NOPE:P]
                for t in range(TILES):
                    if t >= 2:
                        pe.wait_ge(sem("vm_ready"), TILES * l + t - 1)
                    last = mm(bank[6 + t % 2][:, :], ckvT[:, t * P:(t + 1) * P], wv)
                    part_done(last, l, "ukv", 0, MLA_HEADS + t)
                pe.wait_ge(sem("qraw_ready"), MLA_HEADS * (l + 1))
                for n in range(5):
                    if n >= 2:
                        pe.wait_ge(sem("swap_used"), 5 * l + n - 1)
                    if n < 4:
                        src, o = qraw[NOPE:QK, 2 * n:2 * n + 2, 256:512], bank[2 + n % 2][NOPE:QK, :].rearrange("p (h t) -> p h t", h=2)
                    else:
                        src, o = KPR[:, 256:512], bank[2][NOPE:QK, 0:256]
                    mm(o, swap[NOPE:QK, :], src).then_inc(sem("swap_done"), 1)
                its = items[l]

                def scores(m):
                    h, x = its[m]
                    g = item0[l] + m
                    if m >= 2:
                        pe.wait_ge(sem("probs_ready"), g - 1)
                    for qt in range(2):
                        o = bank[2 * (m % 2) + qt]
                        if x:
                            mm(o[:, 0:256], qrot[0:QK, h, qt * P:(qt + 1) * P], kT[0:QK, h, 256:512])
                            last = mm(o[:, 256:512], qraw[0:QK, h, 256 + qt * P:256 + (qt + 1) * P], kT[0:QK, h, 0:256])
                        else:
                            last = mm(o[:, 0:256], qraw[0:QK, h, qt * P:(qt + 1) * P], kT[0:QK, h, 0:256])
                    last.then_inc(sem("scores_done"), 1)

                pe.wait_ge(sem("swap_used"), 5 * (l + 1))
                pe.wait_ge(sem("keys_ready"), l + 1)
                pe.wait_ge(sem("kt_ready"), MLA_HEADS * (l + 1))
                pe.wait_ge(sem("vm_ready"), TILES * (l + 1))
                scores(0)
                for m, (h, x) in enumerate(its):
                    g = item0[l] + m
                    if m + 1 < len(its):
                        scores(m + 1)
                    nk = 4 if x else 2
                    pe.wait_ge(sem("probs_ready"), g + 1)
                    if m:
                        pe.wait_ge(sem("pt_ready"), g)
                    for kt in range(nk):
                        for qt in range(2):
                            last = nc.tensor.transpose(bank[4 + kt // 2][:, (kt % 2) * 256 + qt * P:(kt % 2) * 256 + (qt + 1) * P],
                                                       PR[:, m % 2, qt, kt * P:(kt + 1) * P], ident[:, :])
                    last.then_inc(sem("probs_turned"), 1)
                    if l == 0:
                        modulation(1, 3 * m // 2)
                    pe.wait_ge(sem("pt_ready"), g + 1)
                    if m >= (1 if l == 0 else 2):
                        pe.wait_ge(sem("attn_out"), g if l == 0 else g - 1)
                    o = bank[6 + (m % 2 if l else 0)][(h % 2) * MV:(h % 2 + 1) * MV, 0:256]
                    for kt in range(nk):
                        tile = (kt + 2) % 4 if x else kt
                        last = mm(o, VM[:, tile, h * MV:(h + 1) * MV], PTT[m % 2][:, kt, :], kt == 0, kt == nk - 1)
                    last.then_inc(sem("pv_done"), 1)
                    if l == 0 and m % 2:
                        modulation(1, 3 * m // 2 + 1)

                pe.wait_ge(sem("attn_out"), item0[l] + len(its))
                if l == 0:
                    pe.wait_ge(sem("mod_added"), DEPTH * MODU)
                def project(x):
                    t = tiles[x]
                    for k in range(4):
                        n = unit_no(l, "out", k)
                        unit_landed(pe, n)
                        q = x * 4 + k
                        if q >= 4:
                            pe.wait_ge(sem("mix_added"), 4 * TILES * l + q - 3)
                        for c in range(KC):
                            last = mm(bank[4 + k][:, 0:UC], mixT[:, c, t * P:(t + 1) * P], unit(n)[:, c * UC:(c + 1) * UC], c == 0, c == KC - 1)
                        part_done(last, l, "out", k, x)

                def turn_h(x):
                    pe.wait_ge(sem("h_ready"), TILES * l + x + 1)
                    if x >= 2:
                        pe.wait_ge(sem("ht2_low"), TILES * l + x - 1)
                        pe.wait_ge(sem("ht2_high"), TILES * l + x - 1)
                    turn(H[:, x % 2, :], 2 * (x % 2)).then_inc(sem("h_turned"), 1)

                for x in range(nt):
                    project(x)
                    if x >= 2:
                        turn_h(x - 2)
                pe.wait_ge(sem("mix_added"), 4 * TILES * l + 4 * nt)
                turn_h(nt - 2)
                turn_h(nt - 1)
                pe.wait_ge(sem("ht2_low"), TILES * l + nt)
                pe.wait_ge(sem("ht2_high"), TILES * l + nt)
                for x, t in enumerate(tiles):
                    for c in range(KC):
                        last = mm(bank[7][:, x * NE:(x + 1) * NE], hT[:, c, t * P:(t + 1) * P], rw[:, l, c, :], c == 0, c == KC - 1)
                last.then_inc(sem("logits_done"), 1)

                def shared_up(x):
                    t = tiles[x]
                    for m, name in enumerate(("sw1", "sw3")):
                        n = unit_no(l, name)
                        unit_landed(pe, n)
                        for c in range(KC):
                            last = mm(bank[2 + x % 2][:, m * EH:(m + 1) * EH], hT[:, c, t * P:(t + 1) * P], unit(n)[:, c * UC:(c + 1) * UC], c == 0, c == KC - 1)
                        if name == "sw3":
                            part_done(last, l, name, 0, x)
                        elif x == nt - 1:
                            part_done(last, l, name, 0, 0)

                def hidden_turn(x):
                    for c in range(2):
                        last = nc.tensor.transpose(bank[4][:, c * P:(c + 1) * P], HID[:, x % 2, c::2], ident[:, :])
                    return last

                def shared_down(x):
                    pe.wait_ge(sem("shid_ready"), TILES * l + x + 1)
                    if x:
                        pe.wait_ge(sem("shidt_ready"), TILES * l + x)
                        pe.wait_ge(sem("sff_ready"), 2 * TILES * l + 2 * x)
                    hidden_turn(x).then_inc(sem("shid_turned"), 1)
                    pe.wait_ge(sem("shidt_ready"), TILES * l + x + 1)
                    n = unit_no(l, "sw2")
                    unit_landed(pe, n)
                    for y in range(2):
                        for c in range(2):
                            last = mm(bank[5 + y][:, :], HIDT[:, x % 2, c * P:(c + 1) * P], unit(n)[:, c * D + y * 512:c * D + (y + 1) * 512], c == 0, c == 1)
                    part_done(last, l, "sw2", 0, x)

                shared_up(0)
                shared_up(1)
                pe.wait_ge(sem("sel_ready"), l + 1)
                pe.wait_ge(sem("dve_start"), 3)
                pe.wait_ge(sem("pool_set"), 4)
                for x in range(nt):
                    for y in range(x + 1):
                        mm(bank[0][:, x * NE:(x + 1) * NE], (tri if y == x else ones)[:, :], selb[:, y, :], y == 0, y == x)
                for y in range(nt):
                    last = mm(bank[1][:, 0:NE], ones[:, :], selb[:, y, :], y == 0, y == nt - 1)
                last.then_inc(sem("places_done"), 1)
                shared_down(0)
                for x in range(2, nt):
                    pe.wait_ge(sem("shid_ready"), TILES * l + x - 1)
                    shared_up(x)
                    shared_down(x - 1)
                shared_down(nt - 1)

                pe.wait_ge(sem("small_landed"), 16 * len(small))

                def slots(i, b):
                    pe.wait_ge(sem(f"hot_ready{l}"), i + 1)
                    e = pe.value_load(tabi[0:1, bass.ds(i, 1)] if not isinstance(i, int) else tabi[0:1, i:i + 1], min_val=0, max_val=NE - 1)
                    for x in range(nt):
                        last = mm(bank[7][:, 0:12], PH[:, b, x, :], vals[:, x, bass.ds(e, 1), :].rearrange("p e k -> p (e k)"), x == 0, x == nt - 1)
                    last.then_inc(sem(f"slots_done{l}"), 1)

                def up(b):
                    for c in range(KC):
                        last = mm(bank[2][:, :].rearrange("p (m n) -> p m n", m=2), XT[:, c * P:(c + 1) * P], W13[b][:, :, c, :], c == 0, c == KC - 1)
                    last.then_inc(sem(f"up_done{l}"), 1)

                def down(b):
                    for y in range(2):
                        for c in range(2):
                            last = mm(bank[5 + y][:, :], HXT[:, c * P:(c + 1) * P], W2[b][:, c, y * 512:(y + 1) * 512], c == 0, c == 1)
                    last.then_inc(sem(f"down_done{l}"), 1)

                def expert_turn():
                    for c in range(2):
                        last = nc.tensor.transpose(bank[4][:, c * P:(c + 1) * P], HX[:, c::2], ident[:, :])
                    last.then_inc(sem(f"hid_turned{l}"), 1)

                def step(turn_no, b):
                    i = NB * turn_no + b
                    static = isinstance(i, int)
                    pe.wait_ge(sem(f"xt_low{l}"), i + 1)
                    pe.wait_ge(sem(f"xt_high{l}"), i + 1)
                    if not static or i:
                        pe.wait_ge(sem(f"hid_ready{l}"), i)
                    pe.wait_ge(sem(f"w13_landed{b}_{l}"), 32 * (turn_no + 1))
                    up(b)
                    if not static or i:
                        expert_turn()
                    pe.wait_ge(sem(f"xg_landed{(b + 1) % NB}_{l}"), 16 * (turn_no + 1 + (b + 1) // NB))
                    turn(XG[:, (b + 1) % NB, :], 0).then_inc(sem(f"xg_turned{l}"), 1)
                    pe.wait_ge(sem(f"idx_ready{l}"), i + NB)
                    slots(i + NB, b)
                    if not static or i:
                        pe.wait_ge(sem(f"hidt_ready{l}"), i)
                        if not static or i > 1:
                            pe.wait_ge(sem(f"y_ready{l}"), 2 * i - 2)
                        pe.wait_ge(sem(f"w2_landed{(b - 1) % NB}_{l}"), 16 * (turn_no + (1 if b else 0)))
                        down((b - 1) % NB)

                def pair_slots(d, b):
                    pe.wait_ge(sem(f"hot_ready{l}"), 2 * d + 2)
                    for j in range(2):
                        i = 2 * d + j
                        e = pe.value_load(tabi[0:1, bass.ds(i, 1)] if not isinstance(i, int) else tabi[0:1, i:i + 1], min_val=0, max_val=NE - 1)
                        for x in range(nt):
                            last = mm(bank[7][:, 12 * j:12 * j + 12], PH[:, b, x, :], vals[:, x, bass.ds(e, 1), :].rearrange("p e k -> p (e k)"), x == 0, x == nt - 1)
                    last.then_inc(sem(f"slots_done{l}"), 1)

                def pair_gather(b, g):
                    for c in range(4 * g, 4 * g + 4):
                        for x in range(nt):
                            last = mm(bank[c // 4][:, (c % 4) * P:(c % 4 + 1) * P], H[:, x, c::KC], HOT[b][:, x, :], x == 0, x == nt - 1)
                    last.then_inc(sem(f"xg_turned{l}"), 1)

                def pair_up(b):
                    for c in range(KC):
                        for j in range(2):
                            last = mm(bank[2][64 * j:64 * j + 64, :].rearrange("p (m n) -> p m n", m=2), XT[:, c * P + 64 * j:c * P + 64 * j + 64],
                                      W13[2 * b + j][:, :, c, :], c == 0, c == KC - 1)
                    last.then_inc(sem(f"up_done{l}"), 1)

                def pair_down(b):
                    for y in range(2):
                        for c in range(2):
                            for j in range(2):
                                last = mm(bank[5 + y][64 * j:64 * j + 64, :], HXT[:, c * P + 64 * j:c * P + 64 * j + 64],
                                          W2[2 * b + j][:, c, y * 512:(y + 1) * 512], c == 0, c == 1)
                    last.then_inc(sem(f"down_done{l}"), 1)

                def combine(d, b):
                    pe.wait_ge(sem(f"y_ready{l}"), 2 * d + 2)
                    pe.wait_ge(sem(f"tok_ready{l}"), d + 1)
                    for q in range(4):
                        if q >= 2:
                            pe.wait_ge(sem(f"ff_added{l}"), 4 * d + (q - 1))
                        mm(bank[3 + q % 2][:, :], TOK[b][:, q // 2, :], Y[0][:, (q % 2) * 512:(q % 2 + 1) * 512]).then_inc(sem(f"comb_done{l}"), 1)

                def pair_step(turn_no, b):
                    d = 2 * turn_no + b
                    static = isinstance(d, int)
                    pe.wait_ge(sem(f"xt_low{l}"), d + 1)
                    pe.wait_ge(sem(f"xt_high{l}"), d + 1)
                    if not static or d:
                        pe.wait_ge(sem(f"hid_ready{l}"), d)
                    pe.wait_ge(sem(f"w13_landed{2 * b}_{l}"), 32 * (turn_no + 1))
                    pe.wait_ge(sem(f"w13_landed{2 * b + 1}_{l}"), 32 * (turn_no + 1))
                    pair_up(b)
                    if not static or d:
                        if not static or d > 1:
                            pe.wait_ge(sem(f"ff_added{l}"), 4 * d - 4)
                        expert_turn()
                    pe.wait_ge(sem(f"dve_turn{l}"), 2 * d + 1)
                    pair_slots(d + 1, 1 - b)
                    pair_gather(1 - b, 0)
                    if not static or d:
                        pe.wait_ge(sem(f"hidt_ready{l}"), d)
                        if not static or d > 1:
                            pe.wait_ge(sem(f"y_ready{l}"), 2 * d - 2)
                        for j in range(2):
                            pe.wait_ge(sem(f"w2_landed{2 * (1 - b) + j}_{l}"), 16 * (turn_no + b))
                        pair_down(1 - b)
                    pair_gather(1 - b, 1)
                    if not static or d:
                        combine(d - 1, 1 - b)

                if l == DEPTH - 1:
                    pe.wait_ge(sem("table_ready"), l + 1)
                    pe.wait_ge(sem("sff_ready"), 2 * TILES * l + 2 * nt)
                    final = pe.value_load(tabi[0:1, NSLOT:NSLOT + 1], min_val=TURNS[l][0] - 1, max_val=TURNS[l][1] - 1)
                    pair_slots(0, 0)
                    pair_gather(0, 0)
                    pair_gather(0, 1)
                    pair_step(0, 0)
                    pair_step(0, 1)
                    with pe.Fori(1, final + 1) as turn_no:
                        pair_step(turn_no, 0)
                        pair_step(turn_no, 1)
                    pe.wait_ge(sem(f"hid_ready{l}"), 2 * final + 2)
                    pe.wait_ge(sem(f"ff_added{l}"), 8 * final + 4)
                    expert_turn()
                    pe.wait_ge(sem(f"hidt_ready{l}"), 2 * final + 2)
                    pe.wait_ge(sem(f"y_ready{l}"), 4 * final + 2)
                    for j in range(2):
                        pe.wait_ge(sem(f"w2_landed{2 + j}_{l}"), 16 * (final + 1))
                    pair_down(1)
                    combine(2 * final + 1, 1)
                    pe.wait_ge(sem(f"xt_low{l}"), 2 * final + 3)
                    pe.wait_ge(sem(f"xt_high{l}"), 2 * final + 3)
                    break

                pe.wait_ge(sem("table_ready"), l + 1)
                pe.wait_ge(sem("sff_ready"), 2 * TILES * l + 2 * nt)
                final = pe.value_load(tabi[0:1, NSLOT:NSLOT + 1], min_val=TURNS[l][0] - 1, max_val=TURNS[l][1] - 1)
                for i in range(NB):
                    if i:
                        pe.wait_ge(sem(f"idx_ready{l}"), i)
                    slots(i, i)
                pe.wait_ge(sem(f"xg_landed0_{l}"), 16)
                turn(XG[:, 0, :], 0).then_inc(sem(f"xg_turned{l}"), 1)
                for i in range(2 * NB):
                    step(i // NB, i % NB)
                with pe.Fori(2, final + 1) as turn_no:
                    for b in range(NB):
                        step(turn_no, b)
                pe.wait_ge(sem(f"hid_ready{l}"), NB * final + NB)
                expert_turn()
                pe.wait_ge(sem(f"hidt_ready{l}"), NB * final + NB)
                pe.wait_ge(sem(f"y_ready{l}"), 2 * NB * final + 2 * (NB - 1))
                pe.wait_ge(sem(f"w2_landed{NB - 1}_{l}"), 16 * (final + 1))
                down(NB - 1)
                pe.wait_ge(sem(f"xt_low{l}"), NB * final + (NB + 1))
                pe.wait_ge(sem(f"xt_high{l}"), NB * final + (NB + 1))

                for x in range(nt):
                    if x >= 2:
                        pe.wait_ge(sem("rb_read"), 2 * TILES * l + 2 * x - 2)
                    if x == 0:
                        pe.wait_ge(sem(f"y_ready{l}"), 2 * NB * final + 2 * NB)
                    for k in range(2):
                        pe.wait_ge(sem(f"rb_landed{k}"), 64 * l + 16 * (x + 1))
                        for j in range(4 - 2 * k):
                            for y in range(2):
                                last = mm(bank[4 + 2 * (x % 2) + y][:, :], ident[:, :], RB[k][:, j, y * 512:(y + 1) * 512], k + j == 0, k == 1 and j == 1)
                        last.then_inc(sem("rb_summed"), 1)

        @block.scalar
        def _(act):
            def do(o, i, f, **kw):
                return nc.scalar.activation(o, i, f, **kw)

            act.wait_ge(sem("c_landed"), 32)
            do(csig[:, :, :], ccol[:, :, :], ACT.Sigmoid).then_inc(sem("act_start"), 1)
            for dst, src in small:
                act.dma_start(dst, src).then_inc(sem("small_landed"), 16)
            store_mod(act, 0, MODA, "mod_first_stored")
            act.wait_ge(sem("mod_first_stored"), 64)
            load_modcol(act, 0)
            act.wait_ge(sem("dve_start"), 2)
            do(lbt[:, 0:2, :], lbt[:, 0:2, :], ACT.Exp).then_inc(sem("act_start"), 1)
            act.wait_ge(sem("small_landed"), 16 * len(small))

            for l in range(DEPTH):
                tiles, segs = tiles_of(l), segs_of(l)
                nt, s0 = len(tiles), segs[0]
                x0 = tiles[0] * P
                act.wait_ge(sem("modcol_ready"), l + 1)
                for t in range(TILES):
                    act.wait_ge(sem("xh_turned"), TILES * l + t + 1)
                    for c in range(4):
                        m = modcol[:, 1 - t // 2, :, c:c + 1]
                        last = do(hT[:, c, t * P:(t + 1) * P], bank[2 * (t % 2)][:, c * P:(c + 1) * P], ACT.Identity, scale=m[:, 1, :], bias=m[:, 0, :])
                    last.then_inc(sem("ht_low"), 1)
                for p in range(2):
                    cp = 2 * l + p
                    if p:
                        act.wait_ge(sem("lvl_used"), NLEV * cp)
                    for d in range(2):
                        for j in range(2):
                            wait_part(act, l, ("ffw", "fbw")[d], p, j)
                            do(seg_head(kk[d], j), bk(2 * d + j, 2, 256), ACT.Sigmoid).then_inc(sem("f_sig"), 1)
                    for j in range(2):
                        wait_part(act, l, "q", p, j)
                        do(seg_head(qq, j)[:, s0:2, :], bk(4 + j, 2, 256)[:, s0:2, :], ACT.Sigmoid).then_inc(sem("q_sig"), 1)
                    for b in range(2):
                        wait_part(act, l, "i", p, b)
                        do(V[:, 2 * b:2 * b + 2, :], bk(6 + b, 2, 256), ACT.Copy).then_inc(sem("v_ready"), 1)
                    for n, s in enumerate(segs):
                        wait_part(act, l, "g", p, n)
                        do(G[:, 2 * s:2 * s + 2, :], bk(s, 2, 256), ACT.Sigmoid).then_inc(sem("g_sig"), 1)
                    for d in range(2):
                        act.wait_ge(sem("f_ready"), 2 * cp + d + 1)
                        do(bb[d], kk[d], ACT.Ln).then_inc(sem("lf_ready"), 1)
                    for d in range(2):
                        act.wait_ge(sem("b_ready"), 2 * cp + d + 1)
                        do(QE[d], bb[d], ACT.Exp).then_inc(sem("eb_ready"), 1)
                    for d in range(2):
                        act.wait_ge(sem("kdx_ready"), 2 * cp + d + 1)
                        e = (EA, EB)[d][0]
                        do(e, e, ACT.Exp).then_inc(sem("kde_ready"), 1)
                    for d in range(2):
                        act.wait_ge(sem("kd_turned"), 2 * cp + d + 1)
                        for y in range(2):
                            do(KDT[d][:, y * 512:(y + 1) * 512], bank[(6, 0)[d] + y][:, :], ACT.Copy).then_inc(sem("kdt_ready"), 1)
                    r = slice(512 * s0, 1024)
                    for n in range(1, NLEV):
                        act.wait_ge(sem("ex_ready"), (NLEV - 1) * cp + n)
                        do(EA[n % 3][:, r], EA[n % 3][:, r], ACT.Exp)
                        do(EB[n % 3][:, r], EB[n % 3][:, r], ACT.Exp).then_inc(sem("exp_done"), 1)
                    act.wait_ge(sem("o_done"), cp + 1)
                    for s in segs:
                        for n in range(4):
                            last = do(EA[1][:, (s * 4 + n) * P:(s * 4 + n + 1) * P], bank[s][:, n * P:(n + 1) * P], ACT.Square, accum_out=ssq[:, s * 4 + n:s * 4 + n + 1])
                    last.then_inc(sem("ssq_ready"), 1)
                    act.wait_ge(sem("ot_turned"), cp + 1)
                    for j in range(2):
                        last = do(mixT[:, 2 * p + j, x0:512], bank[2 + j][:, x0:512], ACT.Copy)
                    last.then_inc(sem("mix_ready"), 1)
                for n, s in enumerate(segs):
                    wait_part(act, l, "cq", 0, n)
                    for t in (2 * s, 2 * s + 1):
                        last = do(EA[1][:, t * QL:(t + 1) * QL], bank[s][:, (t % 2) * QL:(t % 2 + 1) * QL], ACT.Square, accum_out=ssq[:, t:t + 1])
                last.then_inc(sem("ssq_ready"), 1)
                wait_part(act, l, "ckv", 0, 0)
                act.wait_ge(sem("var_ready"), rstd_no(l, "cq"))
                for t in range(TILES):
                    last = do(EB[1][:, t * P:(t + 1) * P], bank[4][:, t * P:(t + 1) * P], ACT.Square, accum_out=ssq[:, t:t + 1])
                last.then_inc(sem("ssq_ready"), 1)
                wait_part(act, l, "ckv", 0, 1)
                do(KPR, bank[5][NOPE:QK, :], ACT.Copy).then_inc(sem("kpr_ready"), 1)
                act.wait_ge(sem("cq_turned"), l + 1)
                for c in range(2):
                    do(cqT[:, c, x0:512], bank[2 + c][:, x0:512], ACT.Copy, scale=qnw[:, l, c:c + 1]).then_inc(sem("cqt_ready"), 1)
                act.wait_ge(sem("ckv_turned"), l + 1)
                do(ckvT, bank[6][:, :], ACT.Copy, scale=kvw[:, l:l + 1]).then_inc(sem("ckvt_ready"), 1)
                for h in range(MLA_HEADS):
                    wait_part(act, l, "uq", 0, h)
                    do(qraw[0:QK, h, x0:512], bank[h % 2][0:QK, x0:512], ACT.Copy).then_inc(sem("qraw_ready"), 1)
                for h in range(MLA_HEADS):
                    wait_part(act, l, "ukv", 0, h)
                    do(kT[0:NOPE, h, :], bank[4 + h % 2][0:NOPE, :], ACT.Copy).then_inc(sem("kt_ready"), 1)
                for t in range(TILES):
                    wait_part(act, l, "ukv", 0, MLA_HEADS + t)
                    do(VM[:, t, :], bank[6 + t % 2][:, :], ACT.Copy).then_inc(sem("vm_ready"), 1)
                its = items[l]

                def probs(m):
                    g = item0[l] + m
                    act.wait_ge(sem("nmax_ready"), g + 1)
                    if m >= 2:
                        act.wait_ge(sem("probs_turned"), g - 1)
                    nk = 512 if its[m][1] else 256
                    for qt in range(2):
                        last = do(PR[:, m % 2, qt, 0:nk], bank[2 * (m % 2) + qt][:, 0:nk], ACT.Exp,
                                  bias=nmax[:, m % 2, qt:qt + 1], scale=QK ** -0.5, accum_out=asum[:, m % 2, qt:qt + 1])
                    last.then_inc(sem("pexp_ready"), 1)

                probs(0)
                for m in range(len(its)):
                    g = item0[l] + m
                    act.wait_ge(sem("probs_turned"), g + 1)
                    if m >= 2:
                        act.wait_ge(sem("pv_done"), g - 1)
                    for y in range(2 if its[m][1] else 1):
                        last = do(PTT[m % 2][:, 2 * y:2 * y + 2, :], bk(4 + y, 2, 256), ACT.Copy)
                    last.then_inc(sem("pt_ready"), 1)
                    if m + 1 < len(its):
                        probs(m + 1)

                for x, t in enumerate(tiles):
                    act.wait_ge(sem("h_turned"), TILES * l + x + 1)
                    do(hT[:, 0:4, t * P:(t + 1) * P], bk(2 * (x % 2), 4, P), ACT.Copy).then_inc(sem("ht2_low"), 1)
                act.wait_ge(sem("logits_done"), l + 1)
                do(sco[:, 0:nt, :], bk(7, TILES, NE)[:, 0:nt, :], ACT.Sigmoid).then_inc(sem("sco_ready"), 1)

                def shared_sig(x):
                    wait_part(act, l, "sw3", 0, x)
                    if x:
                        act.wait_ge(sem("shid_ready"), TILES * l + x)
                    do(SG, bank[2 + x % 2][:, 0:EH], ACT.Sigmoid).then_inc(sem("ssig_ready"), 1)

                act.wait_ge(sem("h_ready"), TILES * l + nt)
                shared_sig(0)
                shared_sig(1)
                for x in range(nt):
                    act.wait_ge(sem("shid_turned"), TILES * l + x + 1)
                    do(HIDT[:, x % 2, :], bank[4][:, 0:EH], ACT.Copy).then_inc(sem("shidt_ready"), 1)
                    wait_part(act, l, "sw2", 0, x)
                    do(FF[:, x, 0:512], bank[5][:, :], ACT.Copy).then_inc(sem("sff_ready"), 1)
                    if x + 2 < nt:
                        shared_sig(x + 2)

                def xt_low(i):
                    act.wait_ge(sem(f"xg_turned{l}"), i + 1)
                    if not isinstance(i, int) or i:
                        act.wait_ge(sem(f"up_done{l}"), i)
                    do(XT[:, 0:512], bank[0][:, :], ACT.Copy).then_inc(sem(f"xt_low{l}"), 1)

                def hidden_out(i):
                    act.wait_ge(sem(f"hid_turned{l}"), i + 1)
                    if not isinstance(i, int) or i:
                        act.wait_ge(sem(f"down_done{l}"), i)
                    do(HXT, bank[4][:, 0:EH], ACT.Copy).then_inc(sem(f"hidt_ready{l}"), 1)

                def step(turn_no, b):
                    i = NB * turn_no + b
                    static = isinstance(i, int)
                    act.wait_ge(sem(f"up_done{l}"), i + 1)
                    if not static or i:
                        act.wait_ge(sem(f"hid_ready{l}"), i)
                    do(SG, bank[2][:, 0:EH], ACT.Sigmoid).then_inc(sem(f"sig_ready{l}"), 1)
                    if not static or i:
                        hidden_out(i - 1)
                    xt_low(i + 1)
                    if not static or i:
                        y_low(i - 1, turn_no - (0 if b else 1), (b - 1) % NB)

                def y_low(i, before, b):
                    act.wait_ge(sem(f"down_done{l}"), i + 1)
                    if not isinstance(i, int) or i >= NB:
                        act.wait_ge(sem(f"y_stored{b}_{l}"), 16 * before)
                    do(Y[b][:, 0:512], bank[5][:, :], ACT.Copy).then_inc(sem(f"y_ready{l}"), 1)

                def pair_step(turn_no, b):
                    d = 2 * turn_no + b
                    static = isinstance(d, int)
                    act.wait_ge(sem(f"up_done{l}"), d + 1)
                    if not static or d:
                        act.wait_ge(sem(f"hid_ready{l}"), d)
                    do(SG, bank[2][:, 0:EH], ACT.Sigmoid).then_inc(sem(f"sig_ready{l}"), 1)
                    if not static or d:
                        hidden_out(d - 1)
                    pair_xt_low(d + 1)
                    if not static or d:
                        pair_y_low(d - 1)

                def pair_xt_low(d):
                    act.wait_ge(sem(f"xg_turned{l}"), 2 * d + 1)
                    do(XT[:, 0:512], bank[0][:, :], ACT.Copy).then_inc(sem(f"xt_low{l}"), 1)

                def pair_y_low(d):
                    act.wait_ge(sem(f"down_done{l}"), d + 1)
                    if not isinstance(d, int) or d:
                        act.wait_ge(sem(f"comb_done{l}"), 4 * d)
                    do(Y[0][:, 0:512], bank[5][:, :], ACT.Copy).then_inc(sem(f"y_ready{l}"), 1)

                if l == DEPTH - 1:
                    pair_xt_low(0)
                    pair_step(0, 0)
                    pair_step(0, 1)
                    act.wait_ge(sem("table_ready"), l + 1)
                    final = act.value_load(tabi[0:1, NSLOT:NSLOT + 1], min_val=TURNS[l][0] - 1, max_val=TURNS[l][1] - 1)
                    with act.Fori(1, final + 1) as turn_no:
                        pair_step(turn_no, 0)
                        pair_step(turn_no, 1)
                    hidden_out(2 * final + 1)
                    pair_y_low(2 * final + 1)
                    break

                xt_low(0)
                for i in range(2 * NB):
                    step(i // NB, i % NB)
                act.wait_ge(sem("table_ready"), l + 1)
                final = act.value_load(tabi[0:1, NSLOT:NSLOT + 1], min_val=TURNS[l][0] - 1, max_val=TURNS[l][1] - 1)
                with act.Fori(2, final + 1) as turn_no:
                    for b in range(NB):
                        step(turn_no, b)
                hidden_out(NB * final + (NB - 1))
                y_low(NB * final + (NB - 1), final, NB - 1)

        @block.vector
        def _(dve):
            V_ = nc.vector
            count = [0]

            def then(ins):
                count[0] += 1
                ins.then_inc(sem("dve_order"), 1)
                dve.wait_ge(sem("dve_order"), count[0])

            def tt(o, a, b, op):
                return V_.tensor_tensor(o, a, b, op)

            dve.wait_ge(sem("act_start"), 1)
            then(V_.memset(csil[:, :, :], 0.0))
            tt(csil[:, :, 0:2].rearrange("p c s -> p s c"), ccol[:, :, :], csig[:, :, :], ALU.mult).then_inc(sem("dve_start"), 1)

            def mod_add(l, v):
                n = l * MODU + v
                dve.wait_ge(sem("unit_done"), unit_no(l, "mod", v) + 1)
                tt(MR[:, n, :], bank[7][:, 0:64], MR[:, n, :], ALU.add).then_inc(sem("mod_added"), 1)

            dve.wait_ge(sem("bmod_landed"), 16 * 4)
            for v in range(MODA):
                mod_add(0, v)
            dve.wait_ge(sem("small_landed"), 16 * len(small))
            then(tt(lbt[:, 2, :], lbc[:, 0, :], lbc[:, 1, :], ALU.max))
            tt(lbt[:, 0, :], lbc[:, 0, :], lbt[:, 2, :], ALU.subtract)
            tt(lbt[:, 1, :], lbc[:, 1, :], lbt[:, 2, :], ALU.subtract).then_inc(sem("dve_start"), 1)
            V_.memset(lb[:, 0, :], 0.0)
            V_.memset(oml[:, 0, :], 1.0)
            V_.memset(noff[:, 0:NE], 0.0)
            then(V_.tensor_copy(masks[:, :], maskf))
            V_.tensor_copy(tri[:, :], trif[:, :]).then_inc(sem("dve_start"), 1)
            dve.wait_ge(sem("act_start"), 2)
            then(tt(lbt[:, 0, :], lbt[:, 0, :], lbt[:, 1, :], ALU.add))
            then(V_.reciprocal(lbt[:, 2, :], lbt[:, 0, :]))
            then(tt(lb[:, 1, :], lbt[:, 1, :], lbt[:, 2, :], ALU.mult))
            then(V_.tensor_scalar(oml[:, 1, :], lb[:, 1, :], -1.0, 1.0, ALU.mult, ALU.add))
            def stats_of(t):
                V_.bn_stats(stats[:, t, 0, :], X[:, t, 0:512])
                then(V_.bn_stats(stats[:, t, 1, :], X[:, t, 512:1024]))
                then(V_.bn_aggr(mv[:, t, :], stats[:, t, :, :].rearrange("p a b -> p (a b)")))

            def inverse(l, name, k, src, dst, scale, eps=EPS):
                V_.tensor_scalar(dst, src, scale, eps, ALU.mult, ALU.add).then_inc(sem("var_ready"), 1)
                dve.wait_ge(sem("rstd_ready"), rstd_no(l, name, k))

            def norm_rows(l, name, t, o):
                stats_of(t)
                inverse(l, name, t, mv[:, t, 1:2], rin[:, 0:1], 1.0)
                then(V_.tensor_scalar(o, X[:, t, :], mv[:, t, 0:1], rout[:, 0:1], ALU.subtract, ALU.mult))

            dve.wait_ge(sem("pool_set"), 2)
            dve.wait_ge(sem("x_landed"), 16 * TILES)

            for l in range(DEPTH):
                tiles, segs = tiles_of(l), segs_of(l)
                nt, s0 = len(tiles), segs[0]
                x0 = tiles[0] * P
                r = slice(512 * s0, 1024)
                for t in range(TILES):
                    stats_of(t)
                dve.wait_ge(sem(f"modcol_landed{l}"), 64)
                V_.tensor_scalar(modcol[:, :, 1, :], modcol[:, :, 1, :], 1.0, None, ALU.add).then_inc(sem("modcol_ready"), 1)
                inverse(l, "a", 0, mv[:, :, 1], rin[:, 0:TILES], 1.0)
                dve.wait_ge(sem("modcol_ready"), l + 1)

                def ht_high(t):
                    dve.wait_ge(sem("xh_turned"), TILES * l + t + 1)
                    for c in range(4, 8):
                        m = modcol[:, 1 - t // 2, :, c:c + 1]
                        last = V_.tensor_scalar(hT[:, c, t * P:(t + 1) * P], bank[2 * (t % 2) + 1][:, (c - 4) * P:(c - 3) * P],
                                                m[:, 1, :], m[:, 0, :], ALU.mult, ALU.add)
                    last.then_inc(sem("ht_high"), 1)

                for t in range(TILES):
                    if t >= 2:
                        dve.wait_ge(sem("xh_turned"), TILES * l + t - 1)
                    V_.tensor_scalar(XH[:, t % 2, :], X[:, t, :], mv[:, t, 0:1], rout[:, t:t + 1], ALU.subtract, ALU.mult).then_inc(sem("xh_ready"), 1)
                    if t:
                        ht_high(t - 1)
                ht_high(TILES - 1)

                for p in range(2):
                    cp = 2 * l + p
                    for d in range(2):
                        for j in range(2):
                            dve.wait_ge(sem("f_sig"), 4 * cp + 2 * d + j + 1)
                            h = d * HEADS + 2 * p + j
                            last = V_.tensor_scalar(seg_head(kk[d], j), seg_head(kk[d], j), oml[:, l, h:h + 1], lb[:, l, h:h + 1], ALU.mult, ALU.add)
                        last.then_inc(sem("f_ready"), 1)
                    for j in range(2):
                        dve.wait_ge(sem("q_sig"), 2 * cp + j + 1)
                        o = seg_head(qq, j)[:, s0:2, :]
                        last = V_.scalar_tensor_tensor(o, bk(4 + j, 2, 256)[:, s0:2, :], HD ** -0.5, o, ALU.mult, ALU.mult)
                    last.then_inc(sem("q_ready"), 1)
                    for n, s in enumerate(segs):
                        dve.wait_ge(sem("g_sig"), 4 * l + p * len(segs) + n + 1)
                        g = G[:, 2 * s:2 * s + 2, :]
                        last = tt(g, g, bk(s, 2, 256), ALU.mult)
                    last.then_inc(sem("g_used"), 1)
                    dve.wait_ge(sem("g_used"), cp + 1)
                    g = G[:, 2 * s0:TILES, :].rearrange("p t (j v) -> p (t j) v", j=2)
                    tt(g, g, hgw[:, l, :].unsqueeze(1).broadcast_to([P, 4 * len(segs), HD]), ALU.mult)
                    if p == 0:
                        dve.wait_ge(sem("scan_landed"), 16 * l + 16)
                    for d in range(2):
                        dve.wait_ge(sem("lf_ready"), 2 * cp + d + 1)
                        V_.tensor_scalar(kk[d], kk[d], -1.0, 1.0, ALU.mult, ALU.add)
                        b = bb[d][:, ::-1] if d else bb[d]
                        V_.tensor_tensor_scan(b, scanm, b, 0.0, ALU.mult, ALU.add).then_inc(sem("b_ready"), 1)
                    if p:
                        dve.wait_ge(sem("lvl_done"), NLEV * cp)
                    for d in range(2):
                        dve.wait_ge(sem("b_ready"), 2 * cp + d + 1)
                        b = bb[d].rearrange("p (n t) -> p n t", t=P)
                        edge = b[:, :, P - 1:P] if d == 0 else b[:, :, 0:1]
                        tt((EA, EB)[d][0].rearrange("p (n t) -> p n t", t=P), edge.broadcast_to([P, 8, P]), b, ALU.subtract).then_inc(sem("kdx_ready"), 1)
                    for d in range(2):
                        dve.wait_ge(sem("eb_ready"), 2 * cp + d + 1)
                        q = QE[d].rearrange("p (n t) -> p n t", t=P)
                        last = V_.tensor_copy(el[:, d, :].unsqueeze(2), q[:, :, P - 1:P] if d == 0 else q[:, :, 0:1])
                    then(last)
                    dve.wait_ge(sem("q_ready"), cp + 1)
                    for d in range(2):
                        last = tt(QE[d][:, r], QE[d][:, r], qq[:, r], ALU.mult)
                    last.then_inc(sem("qe_ready"), 1)
                    for d in range(2):
                        dve.wait_ge(sem("kde_ready"), 2 * cp + d + 1)
                        e = (EA, EB)[d][0]
                        tt(e, e, kk[d], ALU.mult).then_inc(sem("kd_ready"), 1)

                    def halves(a, h):
                        return a[:, r].rearrange("p (n a h) -> p n a h", a=2, h=h)

                    def exponents(n):
                        h = 64 >> (n - 1)
                        nb = (1024 - 512 * s0) // (2 * h)
                        if n >= 3:
                            dve.wait_ge(sem("lvl_done"), NLEV * cp + n - 2)
                        b, c = halves(bb[0], h), halves(bb[1], h)
                        ea, eb = halves(EA[n % 3], h), halves(EB[n % 3], h)
                        bm = b[:, :, 0, h - 1:h].broadcast_to([P, nb, h])
                        cm = c[:, :, 1, 0:1].broadcast_to([P, nb, h])
                        tt(ea[:, :, 0, :], c[:, :, 0, :], cm, ALU.subtract)
                        tt(ea[:, :, 1, :], b[:, :, 1, :], bm, ALU.subtract)
                        tt(eb[:, :, 0, :], bm, b[:, :, 0, :], ALU.subtract)
                        tt(eb[:, :, 1, :], cm, c[:, :, 1, :], ALU.subtract).then_inc(sem("ex_ready"), 1)

                    def weigh(n):
                        h = 64 >> (n - 1)
                        dve.wait_ge(sem("exp_done"), (NLEV - 1) * cp + n)
                        tt(EA[n % 3][:, r], EA[n % 3][:, r], qq[:, r], ALU.mult)
                        eb = halves(EB[n % 3], h)
                        for d in range(2):
                            last = tt(eb[:, :, d, :], eb[:, :, d, :], halves(kk[d], h)[:, :, d, :], ALU.mult)
                        last.then_inc(sem("lvl_ready"), 1)

                    def collect(n):
                        dve.wait_ge(sem("lvl_done"), NLEV * cp + n + 1)
                        if n:
                            dve.wait_ge(sem("lvl_used"), NLEV * cp + n)
                        for s in segs:
                            o = ST[:, s, :].rearrange("p (a t) -> p a t", t=P)
                            x = bk(2 + 2 * (n % 2) + s, 4, P)
                            if n == 0:
                                last = tt(o, x, ident[:, :].unsqueeze(1).broadcast_to([P, 4, P]), ALU.mult)
                            else:
                                last = V_.copy_predicated(o, masks[:, n * P:(n + 1) * P].unsqueeze(1).broadcast_to([P, 4, P]), x)
                        last.then_inc(sem("lvl_used"), 1)

                    def state(k):
                        dve.wait_ge(sem("state_sum"), 3 * cp + k + 1)
                        if k:
                            dve.wait_ge(sem("state_ready"), 3 * cp + k)
                        for d, order in enumerate((CHUNKS_FW, CHUNKS_BW)):
                            for j in range(2):
                                blk = (order[k] // 2) * 4 + j * 2 + order[k] % 2
                                x = bank[6 + k % 2][:, (2 * d + j) * P:(2 * d + j + 1) * P]
                                at = (d * 2 + j) * 3 + k
                                if k:
                                    last = V_.scalar_tensor_tensor(SS[:, at, :], SS[:, at - 1, :], el[:, d, blk:blk + 1], x, ALU.mult, ALU.add)
                                else:
                                    last = V_.tensor_copy(SS[:, at, :], x)
                        last.then_inc(sem("state_ready"), 1)

                    exponents(1)
                    dve.wait_ge(sem("kd_turned"), 2 * cp + 2)
                    tt(EB[0][:, r], kk[0][:, r], kk[1][:, r], ALU.add).then_inc(sem("lvl_ready"), 1)
                    state(0)
                    state(1)
                    state(2)
                    exponents(2)
                    weigh(1)
                    collect(0)
                    for n in range(2, NLEV):
                        if n + 1 < NLEV:
                            exponents(n + 1)
                        weigh(n)
                        collect(n - 1)
                        if l == 0:
                            mod_add(0, MODA + p * NLEV + n - 2)
                    collect(NLEV - 1)
                    if l == 0:
                        mod_add(0, MODA + p * NLEV + NLEV - 2)
                        mod_add(0, MODA + p * NLEV + NLEV - 1)
                    dve.wait_ge(sem("ssq_ready"), 4 * l + p + 1)
                    inverse(l, "hg", p, ssq[:, 4 * s0:8], rin[:, 4 * s0:8], 1.0 / HD)
                    for s in segs:
                        for c in range(2):
                            for j in range(2):
                                n = s * 4 + c * 2 + j
                                last = V_.scalar_tensor_tensor(OT[:, 2 * s + c, j * P:(j + 1) * P], bank[s][:, (c * 2 + j) * P:(c * 2 + j + 1) * P],
                                                               rout[:, n:n + 1], G[:, 2 * s + c, j * P:(j + 1) * P], ALU.mult, ALU.mult)
                    last.then_inc(sem("ot_ready"), 1)

                dve.wait_ge(sem("ssq_ready"), 4 * l + 3)
                inverse(l, "cq", 0, ssq[:, tiles[0]:TILES], rin[:, tiles[0]:TILES], 1.0 / QL)
                for t in tiles:
                    last = V_.tensor_scalar(cqn[:, t, :], bank[t // 2][:, (t % 2) * QL:(t % 2 + 1) * QL], rout[:, t:t + 1], None, ALU.mult)
                last.then_inc(sem("cqn_ready"), 1)
                dve.wait_ge(sem("ssq_ready"), 4 * l + 4)
                inverse(l, "ckv", 0, ssq[:, 0:TILES], rin[:, 0:TILES], 1.0 / KVL)
                for t in range(TILES):
                    last = V_.tensor_scalar(ckvn[:, t, :], bank[4][:, t * P:(t + 1) * P], rout[:, t:t + 1], None, ALU.mult)
                last.then_inc(sem("ckvn_ready"), 1)
                dve.wait_ge(sem("qraw_ready"), MLA_HEADS * (l + 1))
                V_.tensor_copy(qrot[0:NOPE, :, :], qraw[0:NOPE, :, 256:512])
                dve.wait_ge(sem("kpr_ready"), l + 1)
                V_.tensor_copy(KR[:, 0:256], KPR[:, 0:256])
                cos, sin = cs[NOPE:QK, 0, :], cs[NOPE:QK, 1, :]
                for n in range(5):
                    if n < 4:
                        shape = [ROPE, 2, 256]
                        o, raw = qrot[NOPE:QK, 2 * n:2 * n + 2, :], qraw[NOPE:QK, 2 * n:2 * n + 2, 256:512]
                        sw = bank[2 + n % 2][NOPE:QK, :].rearrange("p (h t) -> p h t", h=2)
                    else:
                        shape = [ROPE, 1, 256]
                        o, raw, sw = KR[:, 256:512].unsqueeze(1), KPR[:, 256:512].unsqueeze(1), bank[2][NOPE:QK, 0:256].unsqueeze(1)
                    tmp = qsw[NOPE:QK, 512 * (n % 4):512 * (n % 4) + 256 * shape[1]].rearrange("p (h t) -> p h t", t=256)
                    tt(tmp, raw, cos.unsqueeze(1).broadcast_to(shape), ALU.mult)
                    dve.wait_ge(sem("swap_done"), 5 * l + n + 1)
                    then(tt(o, sw, sin.unsqueeze(1).broadcast_to(shape), ALU.mult))
                    tt(o, o, tmp, ALU.add).then_inc(sem("swap_used"), 1)
                dve.wait_ge(sem("swap_used"), 5 * (l + 1))
                V_.tensor_copy(kT[NOPE:QK, :, :], KR.unsqueeze(1).broadcast_to([ROPE, MLA_HEADS, 512])).then_inc(sem("keys_ready"), 1)
                its = items[l]

                def maximum(m):
                    g = item0[l] + m
                    dve.wait_ge(sem("scores_done"), g + 1)
                    nk = 512 if its[m][1] else 256
                    for qt in range(2):
                        last = V_.tensor_reduce(amax[:, m % 2, qt:qt + 1], bank[2 * (m % 2) + qt][:, 0:nk], AX.X, ALU.max)
                    then(last)
                    V_.tensor_scalar(nmax[:, m % 2, :], amax[:, m % 2, :], -(QK ** -0.5), None, ALU.mult).then_inc(sem("nmax_ready"), 1)

                def attended(m):
                    h, x = its[m]
                    g = item0[l] + m
                    dve.wait_ge(sem("pv_done"), g + 1)
                    rows = slice((h % 2) * MV, (h % 2 + 1) * MV)
                    V_.tensor_copy(mixT[rows, HEADS + h // 2, 256 * x:256 * x + 256], bank[6 + (m % 2 if l else 0)][rows, 0:256]).then_inc(sem("attn_out"), 1)

                maximum(0)
                for m in range(len(its)):
                    g = item0[l] + m
                    nk = 512 if its[m][1] else 256
                    dve.wait_ge(sem("pexp_ready"), g + 1)
                    then(V_.reciprocal(ainv[:, m % 2, :], asum[:, m % 2, :]))
                    for qt in range(2):
                        pr = PR[:, m % 2, qt, 0:nk]
                        last = V_.tensor_scalar(pr, pr, ainv[:, m % 2, qt:qt + 1], None, ALU.mult)
                    last.then_inc(sem("probs_ready"), 1)
                    if m:
                        if l == 0:
                            mod_add(1, 3 * (m - 1) // 2)
                        attended(m - 1)
                        if l == 0 and (m - 1) % 2:
                            mod_add(1, 3 * (m - 1) // 2 + 1)
                    if m + 1 < len(its):
                        maximum(m + 1)
                if l == 0:
                    mod_add(1, MODU - 2)
                attended(len(its) - 1)
                if l == 0:
                    mod_add(1, MODU - 1)

                dve.wait_ge(sem("rows1_landed"), 128 * l + 16 * (2 + 3 * len(segs)))
                def add_mixed(x):
                    t = tiles[x]
                    for k in range(4):
                        wait_part(dve, l, "out", k, x)
                        cols = slice(k * UC, (k + 1) * UC)
                        then(tt(GT[:, k % 2, :], bank[4 + k][:, 0:UC], BV[:, 1 - t // 2, cols], ALU.mult))
                        last = V_.scalar_tensor_tensor(X[:, t, cols], X[:, t, cols], ALPHA, GT[:, k % 2, :], ALU.mult, ALU.add)
                        last.then_inc(sem("mix_added"), 1)
                    dve.wait_ge(sem("mix_added"), 4 * TILES * l + 4 * x + 4)

                def affine(t, wrow, brow):
                    then(tt(X[:, t, :], X[:, t, :], BV[:, wrow, :], ALU.mult))
                    then(tt(X[:, t, :], X[:, t, :], BV[:, brow, :], ALU.add))

                def ht2_high(x):
                    t = tiles[x]
                    dve.wait_ge(sem("h_turned"), TILES * l + x + 1)
                    V_.tensor_copy(hT[:, 4:8, t * P:(t + 1) * P], bk(2 * (x % 2) + 1, 4, P)).then_inc(sem("ht2_high"), 1)

                for x, t in enumerate(tiles):
                    s = 1 - t // 2
                    add_mixed(x)
                    norm_rows(l, "post1", t, X[:, t, :])
                    affine(t, 2, 3)
                    if x >= 2:
                        dve.wait_ge(sem("h_turned"), TILES * l + x - 1)
                        dve.wait_ge(sem(f"h_stored{x % 2}"), 32 * l + 16)
                    norm_rows(l, "post2", t, H[:, x % 2, :])
                    hh = H[:, x % 2, :]
                    if x == 0:
                        then(V_.tensor_scalar(BV[:, 6:6 + len(segs), :], BV[:, 6:6 + len(segs), :], 1.0, None, ALU.add))
                    then(tt(hh, hh, BV[:, 6 + s, :], ALU.mult))
                    tt(hh, hh, BV[:, 4 + s, :], ALU.add).then_inc(sem("h_ready"), 1)
                    if x:
                        ht2_high(x - 1)
                ht2_high(nt - 1)

                dve.wait_ge(sem("sco_ready"), l + 1)
                then(tt(bia[:, 0:nt, :], sco[:, 0:nt, :], rbias[:, l, :].unsqueeze(1).broadcast_to([P, nt, NE]), ALU.add))
                for x in range(nt):
                    last = V_.max(top8[:, x, :], bia[:, x, :])
                then(last)
                for x in range(nt):
                    last = V_.match_replace(rep[:, x, :], top8[:, x, :], bia[:, x, :], -1e30)
                then(last)
                tt(selb[:, 0:nt, :], rep[:, 0:nt, :], bia[:, 0:nt, :], ALU.not_equal).then_inc(sem("sel_ready"), 1)
                then(tt(sel[:, 0:nt, :], rep[:, 0:nt, :], bia[:, 0:nt, :], ALU.not_equal))

                def shared_hidden(x):
                    dve.wait_ge(sem("ssig_ready"), TILES * l + x + 1)
                    if x >= 2:
                        dve.wait_ge(sem("shid_turned"), TILES * l + x - 1)
                    b = bank[2 + x % 2]
                    then(tt(HID[:, x % 2, :], SG, b[:, 0:EH], ALU.mult))
                    tt(HID[:, x % 2, :], HID[:, x % 2, :], b[:, EH:2 * EH], ALU.mult).then_inc(sem("shid_ready"), 1)

                shared_hidden(0)
                shared_hidden(1)
                then(tt(CW[:, 0:nt, :], sel[:, 0:nt, :], sco[:, 0:nt, :], ALU.mult))
                then(V_.tensor_reduce(gsum[:, 0:nt, 0:1], CW[:, 0:nt, :], AX.X, ALU.add))
                then(V_.reciprocal(gsum[:, 0:nt, 1:2], gsum[:, 0:nt, 0:1]))
                for x in range(nt):
                    last = V_.tensor_scalar(CW[:, x, :], CW[:, x, :], gsum[:, x, 1:2], ROUTED_SCALE, ALU.mult, ALU.mult)
                then(last)
                for x in range(nt):
                    last = V_.tensor_tensor_scan(kth[:, x, :], onesf[:, :], sel[:, x, :], 0.0, ALU.mult, ALU.add)
                then(last)
                then(V_.tensor_copy(vals[:, 0:nt, :, 0:4], kv[:, 0:nt, 0:4].unsqueeze(2).broadcast_to([P, nt, NE, 4])))
                then(V_.tensor_copy(vals[:, 0:nt, :, 4:8], kv[:, 0:nt, 4:8].unsqueeze(2).broadcast_to([P, nt, NE, 4])))
                then(V_.tensor_copy(vals[:, 0:nt, :, 8:12], kv[:, 0:nt, 8:12].unsqueeze(2).broadcast_to([P, nt, NE, 4])))
                tt(vals[:, 0:nt, :, 7], kth[:, 0:nt, :], sel[:, 0:nt, :], ALU.subtract)
                for n in range(3):
                    then(V_.tensor_copy(vals[:, 0:nt, :, 8 + n], CW[:, 0:nt, :]))
                    if n < 2:
                        then(tt(CW[:, 0:nt, :], CW[:, 0:nt, :], vals[:, 0:nt, :, 8 + n], ALU.subtract))
                then(V_.tensor_scalar(posm[:, 0:nt, :], sel[:, 0:nt, :], -1000.0, 1000.0, ALU.mult, ALU.add))
                dve.wait_ge(sem("places_done"), l + 1)
                tt(posm[:, 0:nt, :], posm[:, 0:nt, :], bk(0, TILES, NE)[:, 0:nt, :], ALU.add)
                then(V_.tensor_copy(cnt[:, :], bank[1][:, 0:NE]))
                then(V_.tensor_scalar(over[:, :], cnt[:, :], float(BLOCK[l]), None, ALU.is_gt))
                for n in range(2, TILES):
                    then(V_.scalar_tensor_tensor(over[:, :], cnt[:, :], float(n * BLOCK[l]), over[:, :], ALU.is_gt, ALU.add))
                then(V_.tensor_tensor_scan(icum[:, :], onesf[:, :], over[:, :], 0.0, ALU.mult, ALU.add))
                ns = NSLOT - NE
                then(tt(cmpb, icum[:, :].unsqueeze(1).broadcast_to([P, ns, NE]), slotno[:, :].unsqueeze(2).broadcast_to([P, ns, NE]), ALU.is_le))
                then(V_.tensor_reduce(tabf[:, NE:NSLOT], cmpb, AX.X, ALU.add))
                then(tt(cmpb, cmpb, over[:, :].unsqueeze(1).broadcast_to([P, ns, NE]), ALU.mult))
                then(V_.tensor_reduce(exb[:, :], cmpb, AX.X, ALU.add))
                then(tt(exb[:, :], slotno[:, :], exb[:, :], ALU.subtract))
                then(V_.tensor_scalar(exb[:, :], exb[:, :], -float(BLOCK[l]), -float(BLOCK[l]), ALU.mult, ALU.add))
                then(V_.tensor_scalar(noff[:, NE:NSLOT], slotno[:, :], icum[:, NE - 1:NE], -8192.0, ALU.is_ge, ALU.mult))
                then(tt(noff[:, NE:NSLOT], noff[:, NE:NSLOT], exb[:, :], ALU.add))
                (t_min, t_max), pt = TURNS[l], PER_TURN[l]
                nx = t_max - t_min
                V_.tensor_scalar(exb[:, 0:nx], slotno[:, pt * t_min - NE:pt * t_max - NE:pt], icum[:, NE - 1:NE], None, ALU.is_lt)
                then(V_.tensor_scalar(tabi[:, 0:NSLOT], tabf[:, :], float(NE - 1), None, ALU.min))
                then(V_.tensor_reduce(nturn[:, 0:1], exb[:, 0:nx], AX.X, ALU.add))
                V_.tensor_scalar(tabi[:, NSLOT:NSLOT + 1], nturn[:, 0:1], float(t_min - 1), None, ALU.add).then_inc(sem("table_ready"), 1)
                dve.wait_ge(sem("table_ready"), l + 1)

                def shared_out(x):
                    wait_part(dve, l, "sw2", 0, x)
                    V_.tensor_copy(FF[:, x, 512:1024], bank[6][:, :]).then_inc(sem("sff_ready"), 1)

                for x in range(2, nt):
                    shared_hidden(x) if x == 2 else None
                    shared_out(x - 2)
                    if x + 1 < nt:
                        shared_hidden(x + 1)
                shared_out(nt - 2)
                shared_out(nt - 1)

                def pair_hot(d, b):
                    for j in range(2):
                        i = 2 * d + j
                        e = dve.value_load(tabi[0:1, bass.ds(i, 1)] if not isinstance(i, int) else tabi[0:1, i:i + 1], min_val=0, max_val=NE - 1)
                        off = noff[:, bass.ds(i, 1)] if not isinstance(i, int) else noff[:, i:i + 1]
                        for x in range(nt):
                            last = V_.tensor_scalar(HOT[b][:, x, 64 * j:64 * j + 64], iota[:, 0:64], posm[:, x, bass.ds(e, 1)], off, ALU.subtract, ALU.is_equal)
                    last.then_inc(sem(f"hot_ready{l}"), 1)
                    dve.wait_ge(sem(f"hot_ready{l}"), 2 * d + 1)
                    V_.tensor_copy(PH[:, b, 0:nt, :], HOT[b]).then_inc(sem(f"hot_ready{l}"), 1)

                def pair_indices(d, b):
                    dve.wait_ge(sem(f"slots_done{l}"), d + 1)
                    for j in range(2):
                        half_rows = slice(64 * j, 64 * j + 64)
                        last = V_.tensor_reduce(idxf[half_rows, b, :], bank[7][half_rows, 12 * j:12 * j + 12].rearrange("p (a k) -> p a k", k=4), AX.X, ALU.add)
                    last.then_inc(sem(f"dve_turn{l}"), 1)

                def pair_xt_high(d):
                    dve.wait_ge(sem(f"xg_turned{l}"), 2 * d + 2)
                    V_.tensor_copy(XT[:, 512:1024], bank[1][:, :]).then_inc(sem(f"xt_high{l}"), 1)

                def pair_y_high(d):
                    dve.wait_ge(sem(f"down_done{l}"), d + 1)
                    V_.tensor_copy(Y[0][:, 512:1024], bank[6][:, :]).then_inc(sem(f"y_ready{l}"), 1)

                def pair_sum(d):
                    if not isinstance(d, int) or d:
                        dve.wait_ge(sem(f"ff_added{l}"), 4 * d)
                    for q in range(4):
                        dve.wait_ge(sem(f"comb_done{l}"), 4 * d + (q + 1))
                        f = FF[:, q // 2, (q % 2) * 512:(q % 2 + 1) * 512]
                        tt(f, f, bank[3 + q % 2][:, :], ALU.add).then_inc(sem(f"ff_added{l}"), 1)

                def pair_step(turn_no, b):
                    d = 2 * turn_no + b
                    static = isinstance(d, int)
                    dve.wait_ge(sem(f"sig_ready{l}"), d + 1)
                    dve.wait_ge(sem(f"dve_turn{l}"), 2 * d + 1)
                    if not static or d:
                        dve.wait_ge(sem(f"hid_turned{l}"), d)
                    V_.scalar_tensor_tensor(HX, bank[2][:, 0:EH], idxf[:, b, 2:3], SG, ALU.mult, ALU.mult).then_inc(sem(f"dve_turn{l}"), 1)
                    for x in range(nt):
                        last = V_.tensor_scalar(TOK[b][:, x, :], iota[:, :], idxf[:, b, 0:1], BIG - P * x, ALU.subtract, ALU.is_equal)
                    last.then_inc(sem(f"tok_ready{l}"), 1)
                    dve.wait_ge(sem(f"dve_turn{l}"), 2 * d + 2)
                    tt(HX, HX, bank[2][:, EH:2 * EH], ALU.mult).then_inc(sem(f"hid_ready{l}"), 1)
                    if not static or d:
                        pair_y_high(d - 1)
                    pair_xt_high(d + 1)
                    if not static or d:
                        pair_sum(d - 1)
                        dve.wait_ge(sem(f"tok_ready{l}"), d)
                    pair_indices(d + 1, 1 - b)
                    pair_hot(d + 2, b)

                def hot(i, b):
                    e = dve.value_load(tabi[0:1, bass.ds(i, 1)] if not isinstance(i, int) else tabi[0:1, i:i + 1], min_val=0, max_val=NE - 1)
                    off = noff[:, bass.ds(i, 1)] if not isinstance(i, int) else noff[:, i:i + 1]
                    for x in range(nt):
                        last = V_.tensor_scalar(PH[:, b, x, :], iota[:, :], posm[:, x, bass.ds(e, 1)], off, ALU.subtract, ALU.is_equal)
                    last.then_inc(sem(f"hot_ready{l}"), 1)

                def indices(i, b, past=True):
                    dve.wait_ge(sem(f"slots_done{l}"), i + 1)
                    V_.tensor_reduce(idxf[:, b, :], bank[7][:, 0:12].rearrange("p (a k) -> p a k", k=4), AX.X, ALU.add).then_inc(sem(f"dve_turn{l}"), 1)
                    dve.wait_ge(sem(f"dve_turn{l}"), i + 1 + (i - NB + 1 if past else 0))
                    tt(idxi[:, b, :], idxf[:, b, 0:2], bigc[:, :], ALU.add).then_inc(sem(f"idx_ready{l}"), 1)

                def xt_high(i):
                    dve.wait_ge(sem(f"xg_turned{l}"), i + 1)
                    if not isinstance(i, int) or i:
                        dve.wait_ge(sem(f"up_done{l}"), i)
                    V_.tensor_copy(XT[:, 512:1024], bank[1][:, :]).then_inc(sem(f"xt_high{l}"), 1)

                def y_high(i, before, b):
                    dve.wait_ge(sem(f"down_done{l}"), i + 1)
                    if not isinstance(i, int) or i >= NB:
                        dve.wait_ge(sem(f"y_stored{b}_{l}"), 16 * before)
                    V_.tensor_copy(Y[b][:, 512:1024], bank[6][:, :]).then_inc(sem(f"y_ready{l}"), 1)

                def step(turn_no, b):
                    i = NB * turn_no + b
                    static = isinstance(i, int)
                    dve.wait_ge(sem(f"sig_ready{l}"), i + 1)
                    if not static or i:
                        dve.wait_ge(sem(f"hid_turned{l}"), i)
                    if not static or i >= NB:
                        dve.wait_ge(sem(f"y_stored{b}_{l}"), 16 * turn_no)
                    V_.scalar_tensor_tensor(HX, bank[2][:, 0:EH], idxf[:, b, 2:3], SG, ALU.mult, ALU.mult).then_inc(sem(f"dve_turn{l}"), 1)
                    V_.tensor_copy(sidx[:, b, :], idxi[:, b, 1:2])
                    dve.wait_ge(sem(f"dve_turn{l}"), NB + 2 * i + 1)
                    tt(HX, HX, bank[2][:, EH:2 * EH], ALU.mult).then_inc(sem(f"hid_ready{l}"), 1)
                    xt_high(i + 1)
                    indices(i + NB, b)
                    hot(i + NB + 1, (b + 1) % NB)
                    if not static or i:
                        y_high(i - 1, turn_no - (0 if b else 1), (b - 1) % NB)

                if l < DEPTH - 1:
                    for i in range(NB):
                        hot(i, i)
                        if i:
                            indices(i - 1, i - 1, False)
                    indices(NB - 1, NB - 1, False)
                    hot(NB, 0)
                    xt_high(0)
                    for i in range(2 * NB):
                        step(i // NB, i % NB)
                    final = dve.value_load(tabi[0:1, NSLOT:NSLOT + 1], min_val=TURNS[l][0] - 1, max_val=TURNS[l][1] - 1)
                    with dve.Fori(2, final + 1) as turn_no:
                        for b in range(NB):
                            step(turn_no, b)
                    y_high(NB * final + (NB - 1), final, NB - 1)
                else:
                    pair_hot(0, 0)
                    pair_hot(1, 1)
                    pair_indices(0, 0)
                    pair_xt_high(0)
                    pair_step(0, 0)
                    pair_step(0, 1)
                    final = dve.value_load(tabi[0:1, NSLOT:NSLOT + 1], min_val=TURNS[l][0] - 1, max_val=TURNS[l][1] - 1)
                    with dve.Fori(1, final + 1) as turn_no:
                        pair_step(turn_no, 0)
                        pair_step(turn_no, 1)
                    pair_y_high(2 * final + 1)
                    pair_sum(2 * final + 1)
                    dve.wait_ge(sem(f"ff_added{l}"), 8 * (final + 1))

                dve.wait_ge(sem("rows2_landed"), 64 * l + 16 * (4 if l < DEPTH - 1 else 3))
                for x, t in enumerate(tiles):
                    s = 1 - t // 2
                    if l < DEPTH - 1:
                        dve.wait_ge(sem("rb_landed1"), 64 * l + 16 * (x + 1))
                        then(tt(FF[:, x, :], FF[:, x, :], RB[1][:, 2, :], ALU.add))
                        tt(FF[:, x, :], FF[:, x, :], RB[1][:, 3, :], ALU.add).then_inc(sem("rb_read"), 1)
                        dve.wait_ge(sem("rb_read"), 2 * TILES * l + 2 * x + 1)
                        dve.wait_ge(sem("rb_summed"), 2 * TILES * l + 2 * x + 2)
                        for y in range(2):
                            last = tt(FF[:, x, y * 512:(y + 1) * 512], FF[:, x, y * 512:(y + 1) * 512], bank[4 + 2 * (x % 2) + y][:, :], ALU.add)
                        last.then_inc(sem("rb_read"), 1)
                        dve.wait_ge(sem("rb_read"), 2 * TILES * l + 2 * x + 2)
                    then(tt(FF[:, x, :], FF[:, x, :], BV[:, s, :], ALU.mult))
                    then(V_.scalar_tensor_tensor(X[:, t, :], X[:, t, :], ALPHA, FF[:, x, :], ALU.mult, ALU.add))
                    norm_rows(l, "fin", t, X[:, t, :])
                    then(tt(X[:, t, :], X[:, t, :], BV[:, 2, :], ALU.mult))
                    tt(X[:, t, :], X[:, t, :], BV[:, 3, :], ALU.add).then_inc(sem("x_final"), 1)
                dve.wait_ge(sem("x_final"), TILES * l + nt)


_INS = ["x", "c", "ctx", "c_ctx", "w_mod", "b_mod", "w_in", "hg_lb", "hg_norm_w", "q_norm_w", "w_uq", "kv_norm_w",
        "w_ukv", "w_out", "ln1_w", "ln1_b", "router_w", "router_bias", "moe_w1", "moe_w3", "moe_w2", "shared_w1",
        "shared_w3", "shared_w2", "ln2_w", "ln2_b"]


def kernel(**inputs):
    import concourse.bacc as _bacc
    from concourse.bass_utils import run_bass_kernel_spmd as _run

    nc = _bacc.Bacc("TRN2", target_bir_lowering=False, num_devices=1)
    arrays, args = {}, {}
    given = {name: np.ascontiguousarray(inputs[name]) for name in _INS}
    given.update(constants())
    for name, a in given.items():
        a = np.ascontiguousarray(a)
        arrays[f"in_{name}"] = a
        args[name] = nc.dram_tensor(f"in_{name}", a.shape, mybir.dt.from_np(a.dtype), kind="ExternalInput").ap()
    out = nc.dram_tensor("out_0", (1, 256, D), F32, kind="ExternalOutput").ap()
    build(nc, args, out)
    return _run(nc, [arrays], core_ids=[0]).results[0]["out_0"]
```
